# Optimizing a Trainium2 kernel written in Bass

```python
import math
import jax, jax.numpy as jnp
from jax import lax
import numpy as np

D_MODEL = 1024
BATCH = 1
SEQ = 512
DEPTH = 1

D_CONV = D_MODEL
CONV_WIDTH = 3
N_HEADS = 16
HEAD_DIM = 64
D_ATTN = N_HEADS * HEAD_DIM
ATTN_PATTERNS = ((128, 1), (512, 4), (2048, 16))
QB = 128
IN_COLS = 4 * D_CONV + 4 * D_ATTN + 2 * D_MODEL
EPS = 1e-6


def rms_norm(x, g):
    xf = x.astype(jnp.float32)
    y = xf * lax.rsqrt(jnp.mean(xf * xf, axis=-1, keepdims=True) + EPS)
    return (y * g.astype(jnp.float32)).astype(x.dtype)

def alibi_slopes(n_heads):
    return jnp.exp2(-8.0 * jnp.arange(1, n_heads + 1, dtype=jnp.float32) / n_heads)

def causal_depthwise_conv(u, w):
    return lax.conv_general_dilated(
        u, w.astype(u.dtype)[:, None, :], window_strides=(1,),
        padding=[(CONV_WIDTH - 1, 0)],
        dimension_numbers=("NWC", "WIO", "NWC"),
        feature_group_count=u.shape[-1])

def dilated_window_attention(q, k, v, window, dilation, slopes):
    B, S, H, Dh = q.shape
    d = dilation
    win = window // dilation
    assert win == QB
    L = S // d
    nb = -(-L // QB)
    Lp = nb * QB

    def to_sub(t):
        t = t.reshape(B, L, d, H, Dh)
        return jnp.pad(t, ((0, 0), (0, Lp - L), (0, 0), (0, 0), (0, 0)))

    qs = (to_sub(q) * (Dh ** -0.5)).reshape(B, nb, QB, d, H, Dh)

    def key_blocks(t):
        tp = jnp.pad(to_sub(t), ((0, 0), (QB, 0), (0, 0), (0, 0), (0, 0)))
        prev = tp[:, :Lp].reshape(B, nb, QB, d, H, Dh)
        cur = tp[:, QB:QB + Lp].reshape(B, nb, QB, d, H, Dh)
        return jnp.concatenate([prev, cur], axis=2)

    kb = key_blocks(k)
    vb = key_blocks(v)

    s = jnp.einsum("bnqrhe,bnkrhe->bnrhqk", qs, kb,
                   preferred_element_type=jnp.float32)
    q_loc = jnp.arange(QB)[:, None] + QB
    k_loc = jnp.arange(2 * QB)[None, :]
    delta = q_loc - k_loc
    key_sub = jnp.arange(nb)[:, None] * QB - QB + jnp.arange(2 * QB)[None, :]
    valid = ((delta >= 0) & (delta <= win))[None] & (key_sub >= 0)[:, None, :]
    bias = -slopes[:, None, None] * (d * delta).astype(jnp.float32)[None]
    s = jnp.where(valid[None, :, None, None], s + bias, -jnp.inf)

    m = jnp.max(s, axis=-1, keepdims=True)
    p = jnp.exp(s - m)
    den = jnp.sum(p, axis=-1)
    lse = m[..., 0] + jnp.log(den)
    o = jnp.einsum("bnrhqk,bnkrhe->bnqrhe", p, vb.astype(jnp.float32))
    o = o / jnp.transpose(den, (0, 1, 4, 2, 3))[..., None]
    o = o.reshape(B, Lp, d, H, Dh)[:, :L].reshape(B, S, H, Dh)
    lse = jnp.transpose(lse, (0, 1, 4, 2, 3)).reshape(B, Lp, d, H)[:, :L].reshape(B, S, H)
    return o, lse

def mixture_of_dilations(q, k, v, slopes):
    outs, lses = [], []
    for window, dilation in ATTN_PATTERNS:
        o, lse = dilated_window_attention(q, k, v, window, dilation, slopes)
        outs.append(o)
        lses.append(lse)
    alpha = jax.nn.softmax(jnp.stack(lses, axis=0), axis=0)
    o = jnp.sum(alpha[..., None] * jnp.stack(outs, axis=0), axis=0)
    return o.astype(q.dtype)

def hybrid_mixer(h, w_in, b_merge, conv_w, w_out_conv, w_out_attn, w_o):
    B, S, _ = h.shape
    proj = jnp.einsum("bsd,dc->bsc", h, w_in)
    splits = np.cumsum([D_CONV] * 4 + [D_ATTN] * 4 + [D_MODEL])
    xc, bg, cg, zc, q, k, v, za, g_conv, g_attn = jnp.split(proj, splits, axis=-1)

    c = causal_depthwise_conv(cg * xc, conv_w)
    y_conv = jnp.einsum("bsc,cd->bsd", jax.nn.silu(zc) * bg * c, w_out_conv)

    shp = (B, S, N_HEADS, HEAD_DIM)
    o = mixture_of_dilations(q.reshape(shp), k.reshape(shp), v.reshape(shp),
                             alibi_slopes(N_HEADS)).reshape(B, S, D_ATTN)
    y_attn = jnp.einsum("bsc,cd->bsd", jax.nn.silu(za) * o, w_out_attn)

    g_conv = jax.nn.sigmoid(g_conv + b_merge[:D_MODEL])
    g_attn = jax.nn.sigmoid(g_attn + b_merge[D_MODEL:])
    merged = g_conv * y_conv + g_attn * y_attn
    return jnp.einsum("bsd,de->bse", merged, w_o)

def first_inputs(seed: int = 0) -> dict:
    key = jax.random.key(seed)
    ks = jax.random.split(key, 10)
    f32 = jnp.float32
    x = jax.random.normal(ks[0], (BATCH, SEQ, D_MODEL), f32)
    norm_g = 1.0 + 0.02 * jax.random.normal(ks[1], (DEPTH, D_MODEL), f32)
    w_in = jax.random.normal(ks[2], (DEPTH, D_MODEL, IN_COLS), f32) * D_MODEL ** -0.5
    b_merge = 0.01 * jax.random.normal(ks[3], (DEPTH, 2 * D_MODEL), f32)
    conv_w = jax.random.normal(ks[4], (DEPTH, CONV_WIDTH, D_CONV), f32) * CONV_WIDTH ** -0.5
    w_out_conv = jax.random.normal(ks[5], (DEPTH, D_CONV, D_MODEL), f32) * D_CONV ** -0.5
    w_out_attn = jax.random.normal(ks[6], (DEPTH, D_ATTN, D_MODEL), f32) * D_ATTN ** -0.5
    w_o = jax.random.normal(ks[7], (DEPTH, D_MODEL, D_MODEL), f32) * D_MODEL ** -0.5
    final_g = 1.0 + 0.02 * jax.random.normal(ks[8], (D_MODEL,), f32)
    return {"x": x, "norm_g": norm_g, "w_in": w_in, "b_merge": b_merge,
            "conv_w": conv_w, "w_out_conv": w_out_conv, "w_out_attn": w_out_attn,
            "w_o": w_o, "final_g": final_g}

def first_block(x, norm_g, w_in, b_merge, conv_w, w_out_conv, w_out_attn, w_o, final_g):
    h = x
    for layer in range(DEPTH):
        u = rms_norm(h, norm_g[layer])
        h = h + hybrid_mixer(u, w_in[layer], b_merge[layer], conv_w[layer],
                             w_out_conv[layer], w_out_attn[layer], w_o[layer])
    return rms_norm(h, final_g)


NEG_INF = -1e30
FORCE_SCORE = 1e9
ROPE_THETA = 500000.0
Q_BLOCK = 128

A_HEADS = 8
A_KV_HEADS = 2
A_HEAD_DIM = 64
A_ROPE_DIM = A_HEAD_DIM // 4
CMP_LEN = 32
CMP_STRIDE = 16
CMP_HIDDEN = 256
SLC_LEN = 64
SLC_TOPK = 16
WINDOW = 512
A_WIDTH = A_HEADS * A_HEAD_DIM
A_KV_WIDTH = A_KV_HEADS * A_HEAD_DIM

B_HEADS = 8
Q_LORA = 256
KV_LORA = 128
B_NOPE = 64
B_ROPE = 32
B_V = 64
B_QK = B_NOPE + B_ROPE
B_WIDTH = B_HEADS * B_V

MIX_WIDTH = A_WIDTH + B_WIDTH
IN_SIZES = (A_WIDTH, A_KV_WIDTH, A_KV_WIDTH, A_KV_WIDTH, A_KV_WIDTH, A_KV_WIDTH, A_KV_WIDTH,
            3 * A_HEADS, Q_LORA, KV_LORA, B_ROPE)
IN_WIDTH = sum(IN_SIZES)

P_HEADS = 8
N_KEYS = 128
N_EXPERTS = N_KEYS * N_KEYS
P_KEY_DIM = 256
P_TOPK = 16
P_CHUNK = 128


def _rms(x):
    xf = x.astype(jnp.float32)
    return xf * lax.rsqrt(jnp.mean(xf * xf, axis=-1, keepdims=True) + EPS)

def rmsnorm(x, gain):
    return (_rms(x) * gain.astype(jnp.float32)).astype(x.dtype)

def rope_tables(pos, rot_dim):
    inv_freq = ROPE_THETA ** (-jnp.arange(0, rot_dim, 2, dtype=jnp.float32) / rot_dim)
    ang = pos.astype(jnp.float32)[..., None] * inv_freq
    return jnp.cos(ang), jnp.sin(ang)

def apply_rope(x, cos, sin):
    half = cos.shape[-1]
    xf = x.astype(jnp.float32)
    x1, x2, rest = xf[..., :half], xf[..., half:2 * half], xf[..., 2 * half:]
    out = jnp.concatenate([x1 * cos - x2 * sin, x2 * cos + x1 * sin, rest], axis=-1)
    return out.astype(x.dtype)

def masked_softmax(s, mask):
    s = jnp.where(mask, s.astype(jnp.float32), NEG_INF)
    p = jax.nn.softmax(s, axis=-1)
    return jnp.where(mask, p, 0.0)

def nsa_mixer(q, k_cmp, v_cmp, k_slc, v_slc, k_win, v_win, gates, positions,
              q_gain, kc_gain, ks_gain, kw_gain, cmp_pos, cmp_k_w1, cmp_k_w2, cmp_v_w1, cmp_v_w2):
    B, S = q.shape[:2]
    G, R, dk = A_KV_HEADS, A_HEADS // A_KV_HEADS, A_HEAD_DIM
    scale = dk ** -0.5
    cos, sin = rope_tables(positions, A_ROPE_DIM)
    cos_h, sin_h = cos[:, :, None, :], sin[:, :, None, :]
    q = apply_rope(rmsnorm(q, q_gain), cos_h, sin_h)
    k_slc = apply_rope(rmsnorm(k_slc, ks_gain), cos_h, sin_h)
    k_win = apply_rope(rmsnorm(k_win, kw_gain), cos_h, sin_h)

    n_cmp = (S - CMP_LEN) // CMP_STRIDE + 1
    cmp_idx = jnp.arange(n_cmp)[:, None] * CMP_STRIDE + jnp.arange(CMP_LEN)[None, :]
    cmp_start, cmp_end = cmp_idx[:, 0], cmp_idx[:, -1]

    def compress(t, w1, w2):
        blk = t[:, cmp_idx] + cmp_pos[:, None, :]
        blk = blk.transpose(0, 1, 3, 2, 4).reshape(B, n_cmp, G, CMP_LEN * dk)
        return jax.nn.gelu(blk @ w1) @ w2

    kc = compress(k_cmp, cmp_k_w1, cmp_k_w2)
    vc = compress(v_cmp, cmp_v_w1, cmp_v_w2)
    cos_c, sin_c = rope_tables(positions[:, cmp_end], A_ROPE_DIM)
    kc = apply_rope(rmsnorm(kc, kc_gain), cos_c[:, :, None, :], sin_c[:, :, None, :])

    n_slc = S // SLC_LEN
    topk = min(SLC_TOPK, n_slc)
    slc_start = jnp.arange(n_slc) * SLC_LEN
    overlap = ((cmp_start[:, None] < slc_start[None, :] + SLC_LEN)
               & (cmp_end[:, None] >= slc_start[None, :])).astype(jnp.float32)
    ks_blocks = k_slc.reshape(B, n_slc, SLC_LEN, G, dk).transpose(0, 3, 1, 2, 4)
    vs_blocks = v_slc.reshape(B, n_slc, SLC_LEN, G, dk).transpose(0, 3, 1, 2, 4)

    pad = ((0, 0), (WINDOW, 0), (0, 0), (0, 0))
    kw_pad, vw_pad = jnp.pad(k_win, pad), jnp.pad(v_win, pad)

    def block(qb):
        q0 = qb * Q_BLOCK
        t = q0 + jnp.arange(Q_BLOCK)
        qblk = lax.dynamic_slice_in_dim(q, q0, Q_BLOCK, axis=1).reshape(B, Q_BLOCK, G, R, dk)
        gblk = lax.dynamic_slice_in_dim(gates, q0, Q_BLOCK, axis=1).reshape(B, Q_BLOCK, G, R, 3)

        s_c = jnp.einsum('bqgrd,bngd->bgrqn', qblk, kc) * scale
        p_c = masked_softmax(s_c, cmp_end[None, :] <= t[:, None])
        o_c = jnp.einsum('bgrqn,bngd->bqgrd', p_c.astype(vc.dtype), vc)

        imp = jnp.einsum('bgrqn,nj->bgqj', p_c, overlap)
        j = jnp.arange(n_slc)
        forced = (j[None, :] == (t // SLC_LEN)[:, None]) | (j[None, :] == 0)
        causal_blk = slc_start[None, :] <= t[:, None]
        imp = jnp.where(forced, FORCE_SCORE, jnp.where(causal_blk, imp, NEG_INF))
        _, sel = lax.top_k(imp, topk)
        flat = sel.reshape(B, G, Q_BLOCK * topk)[..., None, None]
        ks = jnp.take_along_axis(ks_blocks, flat, axis=2).reshape(B, G, Q_BLOCK, topk * SLC_LEN, dk)
        vs = jnp.take_along_axis(vs_blocks, flat, axis=2).reshape(B, G, Q_BLOCK, topk * SLC_LEN, dk)
        tok = (sel[..., None] * SLC_LEN + jnp.arange(SLC_LEN)).reshape(B, G, Q_BLOCK, topk * SLC_LEN)
        mask_s = (tok <= t[:, None])[:, :, None]
        s_s = jnp.einsum('bqgrd,bgqsd->bgrqs', qblk, ks) * scale
        p_s = masked_softmax(s_s, mask_s)
        o_s = jnp.einsum('bgrqs,bgqsd->bqgrd', p_s.astype(vs.dtype), vs)

        kw = lax.dynamic_slice_in_dim(kw_pad, q0, Q_BLOCK + WINDOW, axis=1)
        vw = lax.dynamic_slice_in_dim(vw_pad, q0, Q_BLOCK + WINDOW, axis=1)
        s_pos = q0 - WINDOW + jnp.arange(Q_BLOCK + WINDOW)
        mask_w = ((s_pos[None, :] <= t[:, None]) & (s_pos[None, :] > t[:, None] - WINDOW)
                  & (s_pos[None, :] >= 0))
        s_w = jnp.einsum('bqgrd,bsgd->bgrqs', qblk, kw) * scale
        p_w = masked_softmax(s_w, mask_w)
        o_w = jnp.einsum('bgrqs,bsgd->bqgrd', p_w.astype(vw.dtype), vw)

        return gblk[..., 0:1] * o_c + gblk[..., 1:2] * o_s + gblk[..., 2:3] * o_w

    out = lax.map(block, jnp.arange(S // Q_BLOCK))
    return out.transpose(1, 0, 2, 3, 4, 5).reshape(B, S, A_WIDTH)

def mla_mixer(c_q, c_kv, k_rope, positions, q_lora_gain, w_uq, kv_lora_gain, w_ukv, q_gain, k_gain):
    B, S = c_q.shape[:2]
    H = B_HEADS
    cos, sin = rope_tables(positions, B_ROPE)
    cos_h, sin_h = cos[:, :, None, :], sin[:, :, None, :]
    q = (rmsnorm(c_q, q_lora_gain) @ w_uq).reshape(B, S, H, B_QK)
    kv = (rmsnorm(c_kv, kv_lora_gain) @ w_ukv).reshape(B, S, H, B_NOPE + B_V)
    k_nope, v = kv[..., :B_NOPE], kv[..., B_NOPE:]
    k = jnp.concatenate([k_nope, jnp.broadcast_to(k_rope[:, :, None, :], (B, S, H, B_ROPE))], axis=-1)
    q, k = rmsnorm(q, q_gain), rmsnorm(k, k_gain)
    q = jnp.concatenate([q[..., :B_NOPE], apply_rope(q[..., B_NOPE:], cos_h, sin_h)], axis=-1)
    k = jnp.concatenate([k[..., :B_NOPE], apply_rope(k[..., B_NOPE:], cos_h, sin_h)], axis=-1)
    scale = B_QK ** -0.5
    key_idx = jnp.arange(S)

    def block(qb):
        q0 = qb * Q_BLOCK
        t = q0 + jnp.arange(Q_BLOCK)
        qblk = lax.dynamic_slice_in_dim(q, q0, Q_BLOCK, axis=1)
        s = jnp.einsum('bqhd,bshd->bhqs', qblk, k) * scale
        p = masked_softmax(s, key_idx[None, :] <= t[:, None])
        return jnp.einsum('bhqs,bshd->bqhd', p.astype(v.dtype), v)

    out = lax.map(block, jnp.arange(S // Q_BLOCK))
    return out.transpose(1, 0, 2, 3, 4).reshape(B, S, B_WIDTH)

def peer_ffn(x, w_q, sub_keys, expert_u, expert_v):
    B, S, D = x.shape
    T = B * S
    xt = x.reshape(T, D)
    q = _rms((xt @ w_q).reshape(T, P_HEADS, P_KEY_DIM)).astype(x.dtype)
    half = P_KEY_DIM // 2
    s1 = jnp.einsum('thd,hnd->thn', q[..., :half], sub_keys[:, 0]).astype(jnp.float32)
    s2 = jnp.einsum('thd,hnd->thn', q[..., half:], sub_keys[:, 1]).astype(jnp.float32)
    v1, i1 = lax.top_k(s1, P_TOPK)
    v2, i2 = lax.top_k(s2, P_TOPK)
    cand = (v1[..., :, None] + v2[..., None, :]).reshape(T, P_HEADS, P_TOPK * P_TOPK)
    vals, ci = lax.top_k(cand, P_TOPK)
    e = (jnp.take_along_axis(i1, ci // P_TOPK, axis=-1) * N_KEYS
         + jnp.take_along_axis(i2, ci % P_TOPK, axis=-1))
    g = jax.nn.softmax(vals, axis=-1)
    n_chunks = T // P_CHUNK

    def chunk(args):
        xc, ec, gc = args
        a = jnp.einsum('cd,ckd->ck', xc, expert_u[ec])
        w = (gc * jax.nn.gelu(a.astype(jnp.float32))).astype(x.dtype)
        return jnp.einsum('ck,ckd->cd', w, expert_v[ec])

    y = lax.map(chunk, (xt.reshape(n_chunks, P_CHUNK, D),
                        e.reshape(n_chunks, P_CHUNK, P_HEADS * P_TOPK),
                        g.reshape(n_chunks, P_CHUNK, P_HEADS * P_TOPK)))
    return y.reshape(B, S, D)

def hybrid_layer(x, positions, norm1_gain, w_in,
                 nsa_q_gain, nsa_kc_gain, nsa_ks_gain, nsa_kw_gain,
                 cmp_pos, cmp_k_w1, cmp_k_w2, cmp_v_w1, cmp_v_w2,
                 mla_q_lora_gain, mla_w_uq, mla_kv_lora_gain, mla_w_ukv, mla_q_gain, mla_k_gain,
                 out_gain_a, out_gain_b, w_out,
                 norm2_gain, peer_w_q, peer_sub_keys, peer_u, peer_v):
    B, S, _ = x.shape
    proj = rmsnorm(x, norm1_gain) @ w_in
    pts = [int(p) for p in np.cumsum(IN_SIZES)[:-1]]
    (a_q, a_kc, a_vc, a_ks, a_vs, a_kw, a_vw, a_gate, b_cq, b_ckv, b_kr) = jnp.split(proj, pts, axis=-1)
    kvs = lambda t: t.reshape(B, S, A_KV_HEADS, A_HEAD_DIM)
    gates = jax.nn.sigmoid(a_gate).reshape(B, S, A_HEADS, 3)
    o_a = nsa_mixer(a_q.reshape(B, S, A_HEADS, A_HEAD_DIM), kvs(a_kc), kvs(a_vc), kvs(a_ks), kvs(a_vs),
                    kvs(a_kw), kvs(a_vw), gates, positions,
                    nsa_q_gain, nsa_kc_gain, nsa_ks_gain, nsa_kw_gain,
                    cmp_pos, cmp_k_w1, cmp_k_w2, cmp_v_w1, cmp_v_w2)
    o_b = mla_mixer(b_cq, b_ckv, b_kr, positions, mla_q_lora_gain, mla_w_uq,
                    mla_kv_lora_gain, mla_w_ukv, mla_q_gain, mla_k_gain)
    mixed = jnp.concatenate([rmsnorm(o_a, out_gain_a), rmsnorm(o_b, out_gain_b)], axis=-1) @ w_out
    h = x + mixed
    return h + peer_ffn(rmsnorm(h, norm2_gain), peer_w_q, peer_sub_keys, peer_u, peer_v)

def second_inputs(seed: int = 0) -> dict:
    key = jax.random.key(seed)
    ks = jax.random.split(key, 32)
    L = DEPTH
    nrm = lambda k, shape, s: jax.random.normal(k, shape, jnp.float32) * s
    gain = lambda k, n: 1.0 + 0.02 * jax.random.normal(k, (L, n), jnp.float32)
    start = jax.random.randint(ks[1], (BATCH, 1), 0, 4096, dtype=jnp.int32)
    return {
        'x': nrm(ks[0], (BATCH, SEQ, D_MODEL), 1.0),
        'positions': (start + jnp.arange(SEQ, dtype=jnp.int32)[None, :]).astype(jnp.int32),
        'norm1_gain': gain(ks[2], D_MODEL),
        'w_in': nrm(ks[3], (L, D_MODEL, IN_WIDTH), D_MODEL ** -0.5),
        'nsa_q_gain': gain(ks[4], A_HEAD_DIM),
        'nsa_kc_gain': gain(ks[5], A_HEAD_DIM),
        'nsa_ks_gain': gain(ks[6], A_HEAD_DIM),
        'nsa_kw_gain': gain(ks[7], A_HEAD_DIM),
        'cmp_pos': nrm(ks[8], (L, CMP_LEN, A_HEAD_DIM), 0.1),
        'cmp_k_w1': nrm(ks[9], (L, CMP_LEN * A_HEAD_DIM, CMP_HIDDEN), (CMP_LEN * A_HEAD_DIM) ** -0.5),
        'cmp_k_w2': nrm(ks[10], (L, CMP_HIDDEN, A_HEAD_DIM), CMP_HIDDEN ** -0.5),
        'cmp_v_w1': nrm(ks[11], (L, CMP_LEN * A_HEAD_DIM, CMP_HIDDEN), (CMP_LEN * A_HEAD_DIM) ** -0.5),
        'cmp_v_w2': nrm(ks[12], (L, CMP_HIDDEN, A_HEAD_DIM), CMP_HIDDEN ** -0.5),
        'mla_q_lora_gain': gain(ks[13], Q_LORA),
        'mla_w_uq': nrm(ks[14], (L, Q_LORA, B_HEADS * B_QK), Q_LORA ** -0.5),
        'mla_kv_lora_gain': gain(ks[15], KV_LORA),
        'mla_w_ukv': nrm(ks[16], (L, KV_LORA, B_HEADS * (B_NOPE + B_V)), KV_LORA ** -0.5),
        'mla_q_gain': gain(ks[17], B_QK),
        'mla_k_gain': gain(ks[18], B_QK),
        'out_gain_a': gain(ks[19], A_WIDTH),
        'out_gain_b': gain(ks[20], B_WIDTH),
        'w_out': nrm(ks[21], (L, MIX_WIDTH, D_MODEL), MIX_WIDTH ** -0.5),
        'norm2_gain': gain(ks[22], D_MODEL),
        'peer_w_q': nrm(ks[23], (L, D_MODEL, P_HEADS * P_KEY_DIM), D_MODEL ** -0.5),
        'peer_sub_keys': nrm(ks[24], (L, P_HEADS, 2, N_KEYS, P_KEY_DIM // 2), (P_KEY_DIM // 2) ** -0.5),
        'peer_u': nrm(ks[25], (L, N_EXPERTS, D_MODEL), D_MODEL ** -0.5),
        'peer_v': nrm(ks[26], (L, N_EXPERTS, D_MODEL), D_MODEL ** -0.5),
    }

def second_block(x, positions, norm1_gain, w_in,
              nsa_q_gain, nsa_kc_gain, nsa_ks_gain, nsa_kw_gain,
              cmp_pos, cmp_k_w1, cmp_k_w2, cmp_v_w1, cmp_v_w2,
              mla_q_lora_gain, mla_w_uq, mla_kv_lora_gain, mla_w_ukv, mla_q_gain, mla_k_gain,
              out_gain_a, out_gain_b, w_out,
              norm2_gain, peer_w_q, peer_sub_keys, peer_u, peer_v):
    h = x
    for l in range(DEPTH):
        h = hybrid_layer(h, positions, norm1_gain[l], w_in[l],
                         nsa_q_gain[l], nsa_kc_gain[l], nsa_ks_gain[l], nsa_kw_gain[l],
                         cmp_pos[l], cmp_k_w1[l], cmp_k_w2[l], cmp_v_w1[l], cmp_v_w2[l],
                         mla_q_lora_gain[l], mla_w_uq[l], mla_kv_lora_gain[l], mla_w_ukv[l],
                         mla_q_gain[l], mla_k_gain[l],
                         out_gain_a[l], out_gain_b[l], w_out[l],
                         norm2_gain[l], peer_w_q[l], peer_sub_keys[l], peer_u[l], peer_v[l])
    return h


def setup_inputs(seed=0):
    out = dict(first_inputs(seed))
    for name, value in second_inputs(seed + 1).items():
        if name != "x":
            out[name + "_2"] = value
    return out


def reference(
    x, norm_g, w_in, b_merge, conv_w, w_out_conv, w_out_attn, w_o, final_g, positions_2,
    norm1_gain_2, w_in_2, nsa_q_gain_2, nsa_kc_gain_2, nsa_ks_gain_2, nsa_kw_gain_2, cmp_pos_2,
    cmp_k_w1_2, cmp_k_w2_2, cmp_v_w1_2, cmp_v_w2_2, mla_q_lora_gain_2, mla_w_uq_2,
    mla_kv_lora_gain_2, mla_w_ukv_2, mla_q_gain_2, mla_k_gain_2, out_gain_a_2, out_gain_b_2,
    w_out_2, norm2_gain_2, peer_w_q_2, peer_sub_keys_2, peer_u_2, peer_v_2,
):
    x = first_block(
        x, norm_g, w_in, b_merge, conv_w, w_out_conv, w_out_attn, w_o, final_g,
    )
    return second_block(
        x, positions_2, norm1_gain_2, w_in_2, nsa_q_gain_2, nsa_kc_gain_2, nsa_ks_gain_2,
        nsa_kw_gain_2, cmp_pos_2, cmp_k_w1_2, cmp_k_w2_2, cmp_v_w1_2, cmp_v_w2_2,
        mla_q_lora_gain_2, mla_w_uq_2, mla_kv_lora_gain_2, mla_w_ukv_2, mla_q_gain_2,
        mla_k_gain_2, out_gain_a_2, out_gain_b_2, w_out_2, norm2_gain_2, peer_w_q_2,
        peer_sub_keys_2, peer_u_2, peer_v_2,
    )


_drawn_inputs = setup_inputs


def setup_inputs(seed=0):
    import zlib

    import numpy as np

    out = dict(_drawn_inputs(seed))
    spreads = {}
    factors = {'norm_g': 3.433,
     'b_merge': 8.0,
     'norm1_gain_2': 3.031,
     'nsa_q_gain_2': 8.0,
     'nsa_kc_gain_2': 8.0,
     'nsa_ks_gain_2': 8.0,
     'nsa_kw_gain_2': 8.0,
     'mla_q_lora_gain_2': 5.789,
     'mla_kv_lora_gain_2': 5.125,
     'mla_q_gain_2': 6.065,
     'mla_k_gain_2': 5.643,
     'out_gain_a_2': 5.417,
     'out_gain_b_2': 5.332,
     'norm2_gain_2': 8.0,
     'peer_w_q_2': 5.375,
     'peer_sub_keys_2': 5.353,
     'peer_u_2': 5.925,
     'peer_v_2': 5.339}
    for name, (base, spread) in spreads.items():
        noise = np.random.default_rng([zlib.crc32(name.encode()), seed]).standard_normal(out[name].shape)
        drawn = base * np.exp(spread * noise) if base else spread * noise
        out[name] = __import__('jax').numpy.asarray(drawn.astype(out[name].dtype))
    for name, factor in factors.items():
        out[name] = (out[name] * factor).astype(out[name].dtype)
    return out
```

```python
from contextlib import ExitStack

import concourse.bass as bass
import numpy as np
from concourse import mybir

F32 = mybir.dt.float32
F32R = mybir.dt.float32r
I32 = mybir.dt.int32
U32 = mybir.dt.uint32
ALU = mybir.AluOpType
ACT = mybir.ActivationFunctionType
AX = mybir.AxisListType.X

P = 128
T = 512
TT = T // P
D = 1024
KC = D // P
EPS = 1e-6
NEG = -1e30
LOWEST = -3e38

J_A = 0
J_B = J_A + 64
J_C = J_B + 32
J_D = J_C + 8
J_E = J_D + 14
J_F = J_E + 8
J_U = J_F + 16
J_V = J_U + P
GROUPS = 16
GJ = 8
JOBS = J_V + GROUPS * GJ
U_FIRST = 4
U_TILE = 11
U_GATES = U_FIRST + TT * U_TILE
U_REST = U_GATES + T // 16
RING = 4
AHEAD = 2

N_CMP = 31
CMP_LEN = 32
CMP_STRIDE = 16

QOFF = [0, 128, 384, 768]
QW = [128, 256, 384, 512]
QALL = 1280
QBANK = [(0, 0), (0, 128), (1, 0), (2, 0)]
SCALE_A = 64.0 ** -0.5
SCALE_B = 96.0 ** -0.5

CONST = {}


def _consts():
    parts, at = [], 0

    def put(name, a):
        nonlocal at
        a = np.asarray(a, np.float32)
        full = np.zeros((P, a.shape[1]), np.float32)
        full[: a.shape[0]] = a
        CONST[name] = (at, at + a.shape[1])
        at += a.shape[1]
        parts.append(full)

    p = np.arange(P)
    put("ident", np.eye(P))
    put("ones", np.ones((P, P)))
    put("halves", np.stack([p < 64, p >= 64], 1))
    r = np.zeros((P, P))
    for base in (0, 64):
        for i in range(8):
            r[base + i, base + i + 8] = -1
            r[base + i + 8, base + i] = 1
    put("rot64", r.T)
    r = np.zeros((P, 32))
    for i in range(16):
        r[64 + i + 16, i] = -1
        r[64 + i, i + 16] = 1
    put("rot32", r)
    put("iota", np.tile(np.arange(P), (P, 1)))
    f_a = np.zeros(P, np.float32)
    f_b = np.zeros(P, np.float32)
    inv_a = np.float32(500000.0) ** (-np.arange(0, 16, 2, dtype=np.float32) / np.float32(16))
    inv_b = np.float32(500000.0) ** (-np.arange(0, 32, 2, dtype=np.float32) / np.float32(32))
    for base in (0, 64):
        f_a[base:base + 8] = inv_a
        f_a[base + 8:base + 16] = inv_a
    f_b[64:80] = inv_b
    f_b[80:96] = inv_b
    put("freq", np.stack([f_a, f_b], 1))
    put("valid", (p[:, None] >= CMP_LEN - 1))
    put("half_pi", np.full((P, 1), np.pi / 2))
    delta = p[:, None] + (T - P) - np.arange(T)[None, :]
    put("causal", np.where(delta >= 0, 0.0, NEG))
    end = np.arange(N_CMP) * CMP_STRIDE + CMP_LEN - 1
    t = p[:, None, None] + P * np.arange(TT)[None, :, None]
    put("cmp_mask", np.where(end[None, None, :] <= t, 0.0, NEG).reshape(P, -1))
    return np.concatenate(parts, 1)


CONSTS = _consts()


def _alibi():
    delta = np.arange(P)[:, None] + (T - P) - np.arange(T)[None, :]
    n = ((delta >= 0) & (delta <= 128)) * 1.0
    n += (delta >= 0) & (delta % 4 == 0)
    n += (delta >= 0) & (delta % 16 == 0)
    slopes = np.exp2(-8.0 * np.arange(1, 17) / 16)
    b = -slopes[:, None, None] * delta[None] + np.log(np.maximum(n, 1))[None]
    return (np.where(n[None] > 0, b, NEG) / SCALE_A).astype(np.float32)


GAIN = dict(norm_g=0, final_g=8, b_merge=16, conv_w=32, norm1=56, q=64, kc=65, ks=66, kw=67,
            cq=68, ckv=70, mq=71, mk=72, out=73, norm2=81, pos=89)
N_GAIN = 121


class Job:

    def __init__(self, m, i=0, per=RING):
        assert per % RING == 0
        self.n = i * per + m
        self.turn = i * (per // RING) + m // RING
        self.slot = m % RING
        self.parts = (m, i, per)

    def ahead(self, by=AHEAD):
        m, i, per = self.parts
        return Job(m + by, i, per)


def two_layer_kernel(nc, tiles, x_t, consts, gains, alibi, positions, cmp_w1, cmp_w2, w_uq, w_ukv,
                     sub_keys, gates_dram, acts_dram, out):
    ctx = ExitStack()
    with ctx:
        def sem(name):
            return ctx.enter_context(nc.semaphore(name))

        KB = 1024
        base = nc.sbuf_base if isinstance(nc.sbuf_base, int) else 0
        base = (base + 63) // 64 * 64

        def at(name, place, shape, dt=F32):
            return nc.alloc_sbuf_tensor_at(name, shape, dt, offset=base + int(place))

        ROW = 2 * KB
        raw = at("raw", 0, [P, RING, D])
        whi = at("whi", 16 * KB, [P, RING, D], F32R)
        wlo = at("wlo", 32 * KB, [P, RING, D], F32R)
        res = at("res", 48 * KB, [P, KC, T])
        act_hi = at("act_hi", 64 * KB, [P, KC, T], F32R)
        act_lo = at("act_lo", 80 * KB, [P, KC, T], F32R)
        place = 96 * KB
        con = at("con", place, [P, CONSTS.shape[1]])
        place = (place + CONSTS.shape[1] * 4 + 31) // 32 * 32
        gain = at("gain", place, [P, N_GAIN])
        place += N_GAIN * 4
        place = (place + 31) // 32 * 32

        def cols(name, n, dt=F32):
            nonlocal place
            t = at(name, place, [P, n], dt)
            place += (n * 4 + 31) // 32 * 32
            return t

        half_b = cols("half_b", 16)
        neg_half = cols("neg_half", 64)
        ms = cols("ms", 64)
        rstd = cols("rstd", 64)
        mx = cols("mx", 24)
        negmax = cols("negmax", 24)
        waited = cols("waited", 2)
        den = cols("den", 24)
        inv = cols("inv", 24)
        factor = cols("factor", 24)
        rq_a = cols("rq_a", 32)
        rq_b = cols("rq_b", 32)
        gate = cols("gate", TT * 24)
        prod = at("prod", place, [P, T + 2])
        m1 = at("m1", place, [P, T])
        cprob = cols("cprob", 2 * P)
        kcr = cols("kcr", N_CMP)
        kc_sq = cols("kc_sq", N_CMP)
        kc_tmp = cols("kc_tmp", N_CMP)
        vcs = cols("vcs", P)
        w2s = at("w2s", place, [P, 2, 2, 64])
        place += 1024
        R = (place + 31) // 32 * 32

        yc_hi = at("yc_hi", R, [P, KC, T], F32R)
        yc_lo = at("yc_lo", R + 16 * KB, [P, KC, T], F32R)
        ya_hi = at("ya_hi", R + 32 * KB, [P, KC, T], F32R)
        ya_lo = at("ya_lo", R + 48 * KB, [P, KC, T], F32R)
        A0 = R + 64 * KB
        qT = at("qT", A0, [P, T])
        kT = at("kT", A0 + ROW, [P, T])
        vT = at("vT", A0 + 2 * ROW, [P, T])
        vtok = at("vtok", A0 + 3 * ROW, [P, TT, P])
        prob = at("prob", A0 + 4 * ROW, [P, 2, QALL])
        probT = at("probT", A0 + 18 * KB, [P, TT, T])
        bias = at("bias", A0 + 26 * KB, [P, 2, T])
        xc = at("xc", A0 + 30 * KB, [P, T])
        conv = at("conv", A0 + 32 * KB, [P, T])
        sgate = at("sgate", A0 + 34 * KB, [P, T])
        mg_hi = at("mg_hi", A0, [P, KC, T], F32R)
        mg_lo = at("mg_lo", A0 + 16 * KB, [P, KC, T], F32R)
        tg = at("tg", A0 + 32 * KB, [P, 2, T])
        sq = at("sq", R, [P, KC, T])
        sq2 = at("sq2", R + 16 * KB, [P, KC, T])
        hg = at("hg", R + 32 * KB, [P, KC, T])
        diag = at("diag", R + 86 * KB, [P, 8, P])
        w1s = at("w1s", R, [P, CMP_LEN, 256])
        cqr = at("cqr", R + 32 * KB, [P, 2, T])
        ckvr = at("ckvr", R + 36 * KB, [P, T])
        krg = at("krg", R + 38 * KB, [P, T])
        kvc = at("kvc", R + 40 * KB, [P, 2, T])
        ksw = at("ksw", R + 44 * KB, [P, 2, T])
        vsw = at("vsw", R + 48 * KB, [P, 2, T])
        qh = at("qh", R + 52 * KB, [P, 4, T])
        sqq = at("sqq", R + 60 * KB, [P, 4, T])
        sqk = at("sqk", R + 68 * KB, [P, 2, T])
        sqc = at("sqc", R + 72 * KB, [P, 3, T])
        rope = at("rope", R + 78 * KB, [P, 4, T])
        pos_i = at("pos_i", R + 60 * KB, [P, T], I32)
        pos_f = at("pos_f", R + 62 * KB, [P, T])
        turns = at("turns", R + 64 * KB, [P, 2, T])
        angle = at("angle", R + 68 * KB, [P, 2, T])
        angle_abs = at("angle_abs", R + 72 * KB, [P, 2, T])
        kp = at("kp", R + 90 * KB, [P, CMP_LEN, 2 * N_CMP])
        hid = at("hid", R + 72 * KB, [P, 4, 2 * N_CMP])
        vtb = at("vtb", R + 97.75 * KB, [P, 2, TT, P])
        rtmp = at("rtmp", R + 68 * KB, [P, 2, T])
        wuq = at("wuq", R, [P, 2, 8 * 96])
        wukv = at("wukv", R + 6 * KB, [P, 2, 8, 64])
        mv = at("mv", R + 10 * KB, [P, TT, T])
        sqb = at("sqb", R + 18 * KB, [P, 2, T])
        mq = at("mq", 64 * KB, [P, 8, T])
        mk = at("mk", 80 * KB, [P, 8, T])
        prob3 = at("prob3", R + 18 * KB, [P, 3, QALL])
        probT2 = at("probT2", R + 60 * KB, [P, 2, TT, T])
        cprobT = at("cprobT", R + 76 * KB, [P, T])
        o_a = at("o_a", R + 33 * KB, [P, 4, T])
        o_b = at("o_b", R + 90 * KB, [P, 4, T])
        sqo = at("sqo", R + 60 * KB, [P, 8, T])
        pq = at("pq", R + 32 * KB, [P, 16, T])
        sqf = at("sqf", R + 64 * KB, [P, 16, T])
        subk = at("subk", R + 16 * KB, [P, 16, P])
        ssb = at("ssb", R, [P, 16, P])
        srep = at("srep", R + 8 * KB, [P, 16, P])
        cand = at("cand", R + 24 * KB, [P, 8, 16, 16])
        crep = at("crep", R + 64 * KB, [P, 8, 16, 16])
        eq = at("eq", R + 72 * KB, [P, 8, 16, 16])
        v16 = at("v16", R + 80 * KB, [P, 16, 16])
        i16 = at("i16", R + 81 * KB, [P, 16, 16], U32)
        i16f = at("i16f", R + 82 * KB, [P, 16, 16])
        vals = at("vals", R + 83 * KB, [P, 8, 16])
        vci = at("vci", R + 83.5 * KB, [P, 8, 16], U32)
        ca = at("ca", R + 84 * KB, [P, 2, 8, 16], U32)
        caf = at("caf", R + 85 * KB, [P, 2, 8, 16])
        sel = at("sel", R + 86 * KB, [P, 3, 8, 16])
        selT = at("selT", R + 87.5 * KB, [P, 3, T])
        vsum = at("vsum", R + 93.5 * KB, [P, 2, 8])
        hot = at("hot", R + 64 * KB, [P, 16, 2, P])
        stage = at("stage", R, [P, 2, P, 64])
        wg = at("wg", R, [P, 2, TT * 2, GJ, 64])
        h_hi = at("h_hi", R + 32 * KB, [P, 2, GJ, T], F32R)
        h_lo = at("h_lo", R + 64 * KB, [P, 2, GJ, T], F32R)
        hf = at("hf", R + 64 * KB, [P, 2, GJ, T])
        gelu = at("gelu", R + 93.75 * KB, [P, 4, T])

        bank = [ctx.enter_context(nc.psum_tensor(f"bank{i}", [P, T], F32)) for i in range(8)]

        def k(name, rows=slice(0, P), cols=None):
            a, b = CONST[name]
            return con[rows, a:b] if cols is None else con[rows, a + cols.start:a + cols.stop]

        def g(name, j=0, rows=slice(0, P)):
            a = GAIN[name] + j
            return gain[rows, a:a + 1]

        ident, ones = k("ident"), k("ones")

        const_landed, x_landed = sem("const_landed"), sem("x_landed")
        raw_landed = [sem(f"raw_landed{i}") for i in range(RING)]
        hi_made = sem("hi_made")
        lo_made = sem("lo_made")
        job_done = sem("job_done")
        taken = [sem(f"taken{i}") for i in range(RING)]
        setup_done, halfb_made = sem("setup_done"), sem("halfb_made")

        sq_made, ssq_made, ms_made, rstd_made = (sem(s) for s in ("sq_made", "ssq_made", "ms_made", "rstd_made"))
        diag_made, row_made, normed, hi_act, lo_act = (sem(s) for s in ("diag_made", "row_made", "normed", "hi_act", "lo_act"))

        v_turned, vtok_copied = sem("v_turned"), sem("vtok_copied")
        bias_landed = [sem("bias_landed0"), sem("bias_landed1")]
        scores_made, scores_masked, negmax_made = sem("scores_made"), sem("scores_masked"), sem("negmax_made")
        probs_exp, inv_made, probs_scaled = sem("probs_exp"), sem("inv_made"), sem("probs_scaled")
        probs_turned, turned_copied, heads_mixed = sem("probs_turned"), sem("turned_copied"), sem("heads_mixed")
        conv_step, zc_tanh, za_tanh = sem("conv_step"), sem("zc_tanh"), sem("za_tanh")
        yc_made, ya_made, ychi_made, yahi_made, y_split = (sem(s) for s in ("yc_made", "ya_made", "ychi_made", "yahi_made", "y_split"))

        merged, mghi_made, mg_split = sem("merged"), sem("mghi_made"), sem("mg_split")
        hg_made = sem("hg_made")
        acts_stored = [sem(f"acts_stored{i}") for i in range(RING)]
        stored = sem("stored")
        NS = {}

        def S(name):
            if name not in NS:
                NS[name] = sem(name)
            return NS[name]

        def make_hi(act, j):
            act.wait_ge(raw_landed[j.slot], (j.turn + 1) * 16)
            act.wait_ge(job_done, j.n + 1)
            act.activation(whi[:, j.slot, :], raw[:, j.slot, :], ACT.Copy).then_inc(hi_made, 1)

        def make_lo(dve, j):
            dve.wait_ge(hi_made, j.n + 1)
            dve.tensor_tensor(wlo[:, j.slot, :], raw[:, j.slot, :], whi[:, j.slot, :].bitcast(F32),
                              ALU.subtract).then_inc(lo_made, 1)

        def multiply(pe, j, hi, lo, before=None):
            pe.wait_ge(lo_made, j.n + 1 + RING)
            pe.wait_ge(taken[j.slot], j.turn + 1)
            for kc in range(KC):
                w = slice(kc * P, (kc + 1) * P)
                wh, wl = whi[:, j.slot, w], wlo[:, j.slot, w]
                if before:
                    before(kc)
                pe.matmul(bank[j.slot][:, :], wh, hi[:, kc, :], start=(kc == 0), stop=False)
                pe.matmul(bank[j.slot][:, :], wh, lo[:, kc, :], start=False, stop=False)
                last = pe.matmul(bank[j.slot][:, :], wl, hi[:, kc, :], start=False, stop=(kc == KC - 1))
            last.then_inc(job_done, 1)

        def result_of(eng, j):
            eng.wait_ge(job_done, j.n + 1 + RING)

        def was_taken(eng, j):
            eng.wait_ge(taken[j.slot], j.turn + 2)

        PASSES = []
        for c in range(4):
            for grp in range(2):
                rows = slice(64 * grp, 64 * grp + 64)
                for b in range(2):
                    PASSES.append(dict(
                        q=qh[rows, c, :], k=ksw[rows, b, :], v=[vtb[:, b, kb, rows] for kb in range(TT)],
                        rows=rows, rq=(rq_a, 2 * c + grp), gate=(c + 4 * grp, 1 + b), first=(b == 0), last=False,
                        head=2 * c + grp if b else None, chunk=c, group=grp, opens=(b == 0 and grp == 0),
                        closes=(b == 1 and grp == 1)))
        for h in range(8):
            rows = slice(64 * (h % 2), 64 * (h % 2) + 64)
            PASSES.append(dict(
                q=mq[0:96, h, :], k=mk[0:96, h, :], v=[mv[:, kb, 64 * h:64 * h + 64] for kb in range(TT)],
                rows=rows, rq=(rq_b, h), gate=None, first=True, last=True, head=None, chunk=4 + h // 2,
                opens=(h % 2 == 0), closes=(h % 2 == 1)))
        DIAG_O = 12 + 24 + 2 + 32

        def rq_col(x, tt):
            t, h = x["rq"]
            return t[:, tt * 8 + h:tt * 8 + h + 1]

        def pass_scores(pe, p):
            x = PASSES[p]
            if p:
                pe.wait_ge(S("p_masked"), 4 * p)
                heads = sum(y["head"] is not None for y in PASSES[:p])
                if heads:
                    pe.wait_ge(S("c_masked"), 4 * heads)
            for qt in range(TT):
                b, col = QBANK[qt]
                pe.matmul(bank[b][:, col:col + QW[qt]], x["q"][:, qt * P:(qt + 1) * P], x["k"][:, 0:QW[qt]],
                          start=True, stop=True).then_inc(S("p_scores"), 1)
            if x["head"] is not None:
                for qt in range(TT):
                    last = pe.matmul(bank[0][:, 384 + 32 * qt:384 + 32 * qt + N_CMP],
                                     x["q"][:, qt * P:(qt + 1) * P], kcr[x["rows"], :], start=True, stop=True)
                last.then_inc(S("c_scores"), 1)

        def pass_turn(pe, p):
            x = PASSES[p]
            pe.wait_ge(S("p_scaled"), 4 * p + 4)
            if p:
                pe.wait_ge(S("p_copied"), 4 * p)
            for qt in range(TT):
                b, col = QBANK[qt]
                for kb in range(qt + 1):
                    last = pe.transpose(bank[3 + b][:, col + kb * P:col + (kb + 1) * P],
                                        prob3[:, p % 3, QOFF[qt] + kb * P:QOFF[qt] + (kb + 1) * P], ident)
                last.then_inc(S("p_turned"), 1)
            if x["head"] is not None:
                h = x["head"]
                pe.wait_ge(S("c_scaled"), 4 * h + 4)
                if h:
                    pe.wait_ge(S("c_copied"), h)
                for qt in range(TT):
                    last = pe.transpose(bank[7][0:N_CMP, qt * P:(qt + 1) * P],
                                        cprob[:, P * (h % 2) + 32 * qt:P * (h % 2) + 32 * qt + N_CMP], ident)
                last.then_inc(S("c_turned"), 1)

        def pass_mix(pe, p):
            x = PASSES[p]
            rows = x["rows"]
            pe.wait_ge(S("p_copied"), 4 * p + 4)
            if x["opens"] and x["chunk"]:
                pe.wait_ge(S("o_taken"), x["chunk"])
            for kb in range(TT):
                last = pe.matmul(bank[6][rows, kb * P:T], x["v"][kb], probT2[:, p % 2, kb, kb * P:T],
                                 start=(x["first"] and kb == 0), stop=(x["last"] and kb == TT - 1))
            if x["head"] is not None:
                pe.wait_ge(S("c_copied"), x["head"] + 1)
                grp = x["group"]
                last = pe.matmul(bank[6][rows, :], vcs[0:N_CMP, 64 * grp:64 * grp + 64], cprobT[0:N_CMP, :],
                                 start=False, stop=True)
            last.then_inc(S("p_mixed"), 1)

        def turn_selection(pe, tt):
            pe.wait_ge(S("selected"), tt + 1)
            if tt:
                pe.wait_ge(S("sel_copied"), tt)
            for n in range(3):
                last = pe.transpose(bank[4][:, n * P:(n + 1) * P], sel[:, n, :, :].rearrange("p h k -> p (h k)"), ident)
            last.then_inc(S("sel_turned"), 1)

        block = ctx.enter_context(nc.Block())

        @block.sync
        def _(sp):
            def load(j):
                sp.wait_ge(lo_made, j.n + 1)
                sp.dma_start(raw[:, j.slot, :], tiles[j.n, :, :]).then_inc(raw_landed[j.slot], 16)

            with sp.Fori(0, (J_U + 8) // RING) as i:
                for m in range(RING):
                    load(Job(m, i))
            for m in range((J_U + 8) // RING * RING, J_U + 8):
                load(Job(m))
            with sp.Fori(0, P // RING) as i:
                for m in range(RING):
                    load(Job(J_U + 8 + m, i))
                    j = Job(J_U + m, i)
                    was_taken(sp, j)
                    sp.dma_start(acts_dram[bass.ds(i * RING + m, 1), :, :], gelu[:, m, :])\
                        .then_inc(acts_stored[m], 16)
            with sp.Fori(0, (JOBS - J_V - 8) // RING) as i:
                for m in range(RING):
                    load(Job(J_V + 8 + m, i))

        @block.gpsimd
        def _(pool):
            pool.dma_start(con[:, :], consts).then_inc(const_landed, 16)
            pool.dma_start(gain[:, :], gains).then_inc(const_landed, 16)
            pool.memset(neg_half[:, :], -0.5).then_inc(setup_done, 1)
            pool.memset(prod[:, 0:2], 0.0).then_inc(setup_done, 1)
            pool.wait_ge(setup_done, 2)
            pool.wait_ge(ms_made, 1)
            pool.tensor_tensor(rstd[:, 0:4], ms[:, 0:4], neg_half[:, 0:4], ALU.pow).then_inc(rstd_made, 1)
            with pool.Fori(0, KC) as c:
                for e in range(2):
                    pool.wait_ge(scores_masked, c * 8 + 1)
                    pool.dma_start(bias[:, e, :], alibi[bass.ds(c * 2 + e, 1), :, :]).then_inc(bias_landed[e], 16)
            pool.wait_ge(ms_made, 2)
            pool.tensor_tensor(rstd[:, 0:4], ms[:, 0:4], neg_half[:, 0:4], ALU.pow).then_inc(rstd_made, 1)
            pool.wait_ge(ms_made, 3)
            pool.tensor_tensor(rstd[:, 4:8], ms[:, 4:8], neg_half[:, 0:4], ALU.pow).then_inc(rstd_made, 1)

            def power(n_ms, n, rows=P, view=None):
                pool.wait_ge(ms_made, n_ms)
                view = view or (lambda t: t[0:rows, 0:n])
                pool.tensor_tensor(view(rstd), view(ms), view(neg_half), ALU.pow).then_inc(rstd_made, 1)

            pool.wait_ge(job_done, J_C + RING)
            pool.dma_start(pos_i[:, :], positions.broadcast_to((P, T))).then_inc(S("pos_landed"), 16)
            pool.dma_start(w2s[:, :, :, :], cmp_w2).then_inc(S("w2_landed"), 16)
            pool.wait_ge(job_done, J_D + 1 + RING)
            pool.dma_start(w1s[:, :, :], cmp_w1).then_inc(S("w1_landed"), 16)
            power(6, 14, view=lambda t: t[:, 0:64].rearrange("p (t n) -> p t n", t=TT)[:, :, 0:14])
            power(7, 2, rows=N_CMP)
            pool.wait_ge(S("hidden_made"), 2)
            pool.dma_start(wuq[:, :, :], w_uq).then_inc(S("wuq_landed"), 16)
            pool.dma_start(wukv[:, :, :, :], w_ukv).then_inc(S("wukv_landed"), 16)
            power(8, 64)
            power(9, 8)
            power(10, 4)
            pool.wait_ge(job_done, J_F + 1 + RING)
            pool.dma_start(subk[:, :, :], sub_keys).then_inc(S("subk_landed"), 16)
            power(11, 32)
            def load_gates(grp, slot):
                pool.dma_start(wg[:, slot, :, :, :].rearrange("p b j t -> p b (j t)"),
                               gates_dram[:, :, bass.ds(grp * GJ, GJ), :].rearrange("b p j t -> p b (j t)"))\
                    .then_inc(S(f"wg_landed{slot}"), 16)

            def load_acts(grp, slot):
                pool.dma_start(hf[:, slot, :, :], acts_dram[bass.ds(grp * GJ, GJ), :, :].rearrange("j p t -> p j t"))\
                    .then_inc(S(f"hf_landed{slot}"), 16)

            pool.wait_ge(S("gates_stored0"), 16 * 5)
            pool.wait_ge(S("gates_stored1"), 16 * 5)
            load_gates(0, 0)
            load_gates(1, 1)
            for m in range(RING):
                pool.wait_ge(acts_stored[m], 16 * 3)
            load_acts(0, 0)
            for m in range(RING):
                pool.wait_ge(acts_stored[m], 16 * (P // RING + 1 if m < 2 else 5))
            load_acts(1, 1)
            for m in range(2, RING):
                pool.wait_ge(acts_stored[m], 16 * (P // RING + 1))
            with pool.Fori(0, GROUPS // 2 - 1) as g2:
                for slot in range(2):
                    pool.wait_ge(S("gated"), g2 * 16 + 8 * (slot + 1))
                    load_gates(g2 * 2 + (2 + slot), slot)
                    result_of(pool, Job(J_V + GJ * slot + GJ - 1, g2, 2 * GJ))
                    load_acts(g2 * 2 + (2 + slot), slot)

        @block.tensor
        def _(pe):
            def sums_of_squares(b, col, squares, n=KC):
                for tt in range(TT):
                    for kc in range(n):
                        last = pe.matmul(bank[b][:, col + tt:col + tt + 1], squares[:, kc, tt * P:(tt + 1) * P],
                                         ones[:, 0:1], start=(kc == 0), stop=(kc == n - 1))
                return last

            def row_of(b, slot):
                for tt in range(TT):
                    last = pe.matmul(bank[b][:, tt * P:(tt + 1) * P], ones, diag[:, slot + tt, :],
                                     start=True, stop=True)
                return last

            pe.sem_inc(job_done, RING)
            pe.wait_ge(const_landed, 32)
            pe.wait_ge(sq_made, KC)
            sums_of_squares(4, 0, sq).then_inc(ssq_made, 1)
            pe.wait_ge(diag_made, 4)
            row_of(5, 0).then_inc(row_made, 1)
            pe.wait_ge(lo_act, KC)

            def scores(c, e):
                rows = slice(64 * e, 64 * e + 64)
                for qt in range(TT):
                    b, col = QBANK[qt]
                    pe.matmul(bank[4 + b][:, col:col + QW[qt]], qT[rows, qt * P:(qt + 1) * P],
                              kT[rows, 0:QW[qt]], start=True, stop=True).then_inc(scores_made, 1)

            def turn_probs(e):
                for qt in range(TT):
                    b, col = QBANK[qt]
                    for kb in range(qt + 1):
                        last = pe.transpose(bank[4 + b][:, col + kb * P:col + (kb + 1) * P],
                                            prob[:, e, QOFF[qt] + kb * P:QOFF[qt] + (kb + 1) * P], ident)
                    last.then_inc(probs_turned, 1)

            def mix_values(e):
                rows = slice(64 * e, 64 * e + 64)
                for kb in range(TT):
                    last = pe.matmul(bank[7][rows, kb * P:T], vtok[:, kb, rows], probT[:, kb, kb * P:T],
                                     start=(kb == 0), stop=(kb == TT - 1))
                last.then_inc(heads_mixed, 1)

            with pe.Fori(0, KC) as c:
                def job(m):
                    multiply(pe, Job(m, c, 8), act_hi, act_lo)

                job(0)
                job(1)
                job(2)
                was_taken(pe, Job(0, c, 8))
                was_taken(pe, Job(1, c, 8))
                pe.wait_ge(turned_copied, c * 8 + 1)
                scores(c, 0)
                job(3)
                was_taken(pe, Job(2, c, 8))
                pe.wait_ge(ya_made, c + 1)
                for tt in range(TT):
                    last = pe.transpose(bank[7][:, tt * P:(tt + 1) * P], vT[:, tt * P:(tt + 1) * P], ident)
                last.then_inc(v_turned, 1)
                pe.wait_ge(scores_masked, c * 8 + 5)
                scores(c, 1)
                job(4)
                pe.wait_ge(probs_scaled, c * 8 + 4)
                pe.wait_ge(scores_masked, c * 8 + 9)
                turn_probs(0)
                job(5)
                pe.wait_ge(turned_copied, c * 8 + 5)
                pe.wait_ge(vtok_copied, c + 1)
                mix_values(0)
                pe.wait_ge(probs_scaled, c * 8 + 8)
                turn_probs(1)
                job(6)
                pe.wait_ge(turned_copied, c * 8 + 9)
                mix_values(1)
                job(7)

            pe.wait_ge(y_split, 2 * KC)
            with pe.Fori(0, 4) as i:
                for m in range(8):
                    hi, lo = ((act_hi, act_lo), (yc_hi, yc_lo), (act_hi, act_lo), (ya_hi, ya_lo))[m % 4]
                    multiply(pe, Job(J_B + m, i, 8), hi, lo)

            pe.wait_ge(mg_split, KC + 1)
            for m in range(8):
                multiply(pe, Job(J_C + m), mg_hi, mg_lo)
            pe.wait_ge(sq_made, KC + 2 * KC)
            sums_of_squares(4, 0, sq)
            sums_of_squares(4, 4, sq2).then_inc(ssq_made, 1)
            pe.wait_ge(diag_made, 8)
            row_of(5, 0).then_inc(row_made, 1)
            pe.wait_ge(diag_made, 12)
            row_of(6, 4).then_inc(row_made, 1)
            pe.wait_ge(lo_act, 2 * KC)
            for m in range(14):
                multiply(pe, Job(J_D + m), act_hi, act_lo)

            for b in range(2):
                was_taken(pe, Job(J_D + 8 + b))
                for tt in range(TT):
                    last = pe.transpose(bank[4 + b][:, tt * P:(tt + 1) * P], vsw[:, b, tt * P:(tt + 1) * P], ident)
                last.then_inc(S("vb_turned"), 1)
            for tt in range(TT):
                last = pe.transpose(bank[6][:, tt * 24:(tt + 1) * 24], krg[0:24, tt * P:(tt + 1) * P],
                                    k("ident", slice(0, 24), slice(0, 24)))
            last.then_inc(S("gates_turned"), 1)
            was_taken(pe, Job(J_D + 13))
            halves = k("halves")
            for tt in range(TT):
                t = slice(tt * P, (tt + 1) * P)
                for c in range(4):
                    pe.matmul(bank[7][:, tt * 16 + 2 * c:tt * 16 + 2 * c + 2], sqq[:, c, t], halves,
                              start=True, stop=True)
                for c in range(2):
                    pe.matmul(bank[7][:, tt * 16 + 8 + 2 * c:tt * 16 + 10 + 2 * c], sqk[:, c, t], halves,
                              start=True, stop=True)
                for c in range(2):
                    pe.matmul(bank[7][:, tt * 16 + 12:tt * 16 + 13], sqc[:, c, t], ones[:, 0:1],
                              start=(c == 0), stop=(c == 1))
                last = pe.matmul(bank[7][:, tt * 16 + 13:tt * 16 + 14], sqc[:, 2, t], ones[:, 0:1],
                                 start=True, stop=True)
            last.then_inc(ssq_made, 1)
            pe.wait_ge(S("kp_made"), 2)
            pe.wait_ge(S("w1_landed"), 16)
            for kv in range(2):
                rows = slice(64 * kv, 64 * kv + 64)
                for half in range(2):
                    for l in range(CMP_LEN):
                        last = pe.matmul(bank[kv][:, 62 * half:62 * half + 62], w1s[rows, l, half * P:(half + 1) * P],
                                         kp[rows, l, :], start=(l == 0), stop=(l == CMP_LEN - 1))
                last.then_inc(S("hidden_made"), 1)

            def row_unit(u, b, rows):
                pe.wait_ge(diag_made, 12 + 4 * (u + 1) + (2 if u >= 6 else 0))
                n = rows.stop - rows.start
                for tt in range(TT):
                    last = pe.matmul(bank[b][rows, tt * P:(tt + 1) * P], ones[:, 0:n],
                                     diag[:, 4 * (u % 2) + tt, :], start=True, stop=True)
                last.then_inc(row_made, 1)

            def rotate(r_, rows, w, x):
                if r_ >= 2:
                    pe.wait_ge(S("rot_used"), r_ - 1)
                pe.matmul(bank[4 + r_ % 2][rows, :], w, x, start=True, stop=True).then_inc(S("rot_made"), 1)

            all_, low, high = slice(0, P), slice(0, 64), slice(64, P)
            was_taken(pe, Job(J_D + 12))
            pe.wait_ge(S("gates_made"), 1)
            row_unit(0, 6, all_)
            row_unit(1, 2, all_)
            pe.wait_ge(S("vtb_copied"), 2)
            for c in range(4):
                rotate(c, all_, k("rot64"), qh[:, c, :])
            pe.wait_ge(S("latents"), 2)
            row_unit(2, 6, low)
            row_unit(3, 6, high)
            pe.wait_ge(S("latents"), 3)
            row_unit(4, 2, low)
            row_unit(5, 2, high)
            pe.wait_ge(S("hid_made"), 2)
            pe.wait_ge(S("w2_landed"), 16)
            for grp in range(2):
                for half in range(2):
                    pe.matmul(bank[3][64 * grp:64 * grp + 64, 0:N_CMP], w2s[:, 0, half, :],
                              hid[:, half, grp * N_CMP:(grp + 1) * N_CMP], start=(half == 0), stop=(half == 1))
            for grp in range(2):
                for half in range(2):
                    last = pe.matmul(bank[3][0:N_CMP, 64 + 64 * grp:128 + 64 * grp],
                                     hid[:, 2 + half, grp * N_CMP:(grp + 1) * N_CMP], w2s[:, 1, half, :],
                                     start=(half == 0), stop=(half == 1))
            last.then_inc(S("kc_made"), 1)
            pe.wait_ge(S("kc_copied"), 3)
            pe.matmul(bank[7][0:N_CMP, 96:98], kc_sq[:, :], halves, start=True, stop=True).then_inc(ssq_made, 1)
            pe.wait_ge(S("kw_normed"), 2)
            rotate(4, all_, k("rot64"), ksw[:, 0, :])
            rotate(5, all_, k("rot64"), ksw[:, 1, :])
            pe.wait_ge(diag_made, 38)
            for grp in range(2):
                last = pe.matmul(bank[3][64 * grp:64 * grp + 64, 256:256 + N_CMP], ones[0:N_CMP, 0:64],
                                 diag[0:N_CMP, grp, 0:N_CMP], start=True, stop=True)
            last.then_inc(row_made, 1)
            pe.wait_ge(S("kc_normed"), 1)
            pe.matmul(bank[3][:, 320:320 + N_CMP], k("rot64"), kcr[:, :], start=True, stop=True).then_inc(S("kc_rot"), 1)

            pe.wait_ge(S("wuq_landed"), 16)
            pe.wait_ge(S("wukv_landed"), 16)

            def product(p):
                b = bank[p % 2]
                if p >= 2:
                    pe.wait_ge(S("prod_taken"), p - 1)
                if p < 8:
                    for c in range(2):
                        last = pe.matmul(b[0:96, :], wuq[:, c, 96 * p:96 * p + 96], cqr[:, c, :],
                                         start=(c == 0), stop=(c == 1))
                elif p < 16:
                    last = pe.matmul(b[0:64, :], wukv[:, 0, p - 8, :], ckvr[:, :], start=True, stop=True)
                else:
                    tt = p - 16
                    last = pe.matmul(b[:, :], ckvr[:, tt * P:(tt + 1) * P],
                                     wukv[:, 1, :, :].rearrange("p h d -> p (h d)"), start=True, stop=True)
                last.then_inc(S("prod_made"), 1)

            def product_sums(p):
                pe.wait_ge(S("prod_taken"), p + 1)
                for tt in range(TT):
                    last = pe.matmul(bank[7][:, 128 + tt * 16 + p:129 + tt * 16 + p],
                                     sqb[0:96, p % 2, tt * P:(tt + 1) * P], ones[0:96, 0:1], start=True, stop=True)
                last.then_inc(S("sums_made"), 1)

            for p in range(20):
                product(p)
                if 1 <= p <= 16:
                    product_sums(p - 1)
            rot_rows = slice(64, 96)
            pe.wait_ge(S("kr_scaled"), 1)
            rotate(6, rot_rows, k("rot32", rot_rows), krg[rot_rows, :])
            for h in range(8):
                rotate(7 + h, rot_rows, k("rot32", rot_rows), mq[rot_rows, h, :])
            pe.wait_ge(S("roped"), 6)
            pe.wait_ge(S("kc_roped"), 1)
            for h in range(8):
                if h >= 2:
                    pe.wait_ge(S("mk_normed"), h - 1)
                row_unit(6 + h, 2 + h % 2, slice(0, 96))

            pe.wait_ge(S("roped"), 15)
            pe.wait_ge(S("mk_normed"), 8)
            for p in range(2):
                pass_scores(pe, p)
            for p in range(len(PASSES)):
                pass_turn(pe, p)
                if p + 2 < len(PASSES):
                    pass_scores(pe, p + 2)
                pass_mix(pe, p)

            pe.wait_ge(S("o_squared"), 8)
            sums_of_squares(0, 0, sqo[:, 0:4, :], 4)
            sums_of_squares(0, 4, sqo[:, 4:8, :], 4).then_inc(ssq_made, 1)
            pe.wait_ge(diag_made, DIAG_O + 4)
            row_of(4, 0).then_inc(row_made, 1)
            pe.wait_ge(diag_made, DIAG_O + 8)
            row_of(5, 4).then_inc(row_made, 1)
            pe.wait_ge(lo_act, 3 * KC)
            for m in range(8):
                multiply(pe, Job(J_E + m), act_hi, act_lo)
            pe.wait_ge(sq_made, 4 * KC)
            sums_of_squares(4, 0, sq).then_inc(ssq_made, 1)
            pe.wait_ge(diag_made, DIAG_O + 12)
            row_of(5, 0).then_inc(row_made, 1)
            pe.wait_ge(lo_act, 4 * KC)
            for m in range(16):
                multiply(pe, Job(J_F + m), act_hi, act_lo)
            def u_job(n):
                multiply(pe, Job(J_U + n), act_hi, act_lo)

            u_job(0)
            was_taken(pe, Job(J_F + 15))
            for h in range(8):
                for tt in range(TT):
                    for half in range(2):
                        last = pe.matmul(bank[7][:, tt * 8 + h:tt * 8 + h + 1],
                                         sqf[:, 2 * h + half, tt * P:(tt + 1) * P], ones[:, 0:1],
                                         start=(half == 0), stop=(half == 1))
            last.then_inc(ssq_made, 1)
            u_job(1)

            def routes(tt):
                for hc in range(16):
                    last = pe.matmul(bank[4 + hc // 4][:, (hc % 4) * P:(hc % 4 + 1) * P],
                                     pq[:, hc, tt * P:(tt + 1) * P], subk[:, hc, :], start=True, stop=True)
                last.then_inc(S("routes_made"), 1)

            pe.wait_ge(S("subk_landed"), 16)
            pe.wait_ge(ms_made, 11)
            routes(0)
            u_job(2)
            u_job(3)
            for tt in range(TT):
                for m in range(U_TILE):
                    u_job(U_FIRST + U_TILE * tt + m)
                    if m == 2:
                        pe.wait_ge(S("routes_scaled"), 8 * tt + 8)
                        if tt:
                            turn_selection(pe, tt - 1)
                    if m == 4 and tt + 1 < TT:
                        if tt:
                            pe.wait_ge(S("sel_copied"), tt)
                        routes(tt + 1)
            turn_selection(pe, TT - 1)
            pe.wait_ge(S("sel_copied"), TT)
            pe.sem_inc(S("gates_made4"), 4)
            with pe.Fori(0, TT) as tile:
                for q in range(8):
                    multiply(pe, Job(J_U + U_GATES + q, tile, 8), act_hi, act_lo)
                    for grp in range(4):
                        gi = tile * 32 + (q * 4 + grp)
                        pe.wait_ge(S("hot_made"), gi + 1)
                        pe.wait_ge(S("gates_copied"), gi + 1)
                        for x in range(4):
                            slot = grp * 4 + x
                            last = pe.matmul(bank[4 + grp][:, x * P:(x + 1) * P], hot[:, slot, 0, :],
                                             hot[:, slot, 1, :], start=True, stop=True)
                        last.then_inc(S("gates_made4"), 1)
            with pe.Fori(0, (P - U_REST) // RING) as i:
                for m in range(RING):
                    multiply(pe, Job(J_U + U_REST + m, i), act_hi, act_lo)
            with pe.Fori(0, GROUPS // 2) as g2:
                for slot in range(2):
                    for dc in range(KC):
                        def part_split(kc):
                            if dc == 0:
                                pe.wait_ge(S("h_split"), g2 * 16 + (8 * slot + kc + 1))
                        multiply(pe, Job(J_V + GJ * slot + dc, g2, 2 * GJ), h_hi[:, slot, :, :],
                                 h_lo[:, slot, :, :], part_split)

        @block.scalar
        def _(act):
            act.dma_start(res[:, :, :], x_t).then_inc(x_landed, 16)
            for b in range(RING):
                act.sem_inc(taken[b], 1)
            act.sem_inc(turned_copied, 1)
            act.wait_ge(x_landed, 16)
            for kc in range(KC):
                act.activation(sq[:, kc, :], res[:, kc, :], ACT.Square).then_inc(sq_made, 1)
            for m in range(AHEAD):
                make_hi(act, Job(m))
            for kc in range(KC):
                act.wait_ge(normed, kc + 1)
                act.activation(act_hi[:, kc, :], hg[:, kc, :], ACT.Copy).then_inc(hi_act, 1)

            def exps(c, e):
                act.wait_ge(negmax_made, c * 2 + e + 1)
                for qt in range(TT):
                    s = slice(QOFF[qt], QOFF[qt] + QW[qt])
                    act.activation(prob[:, e, s], prob[:, e, s], ACT.Exp, bias=negmax[:, 4 * e + qt:4 * e + qt + 1],
                                   accum_out=den[:, 4 * e + qt:4 * e + qt + 1]).then_inc(probs_exp, 1)

            def copy_turned(c, e):
                act.wait_ge(probs_turned, c * 8 + 4 * e + 2)
                act.activation(probT[:, 0, 0:256], bank[4][:, 0:256], ACT.Copy).then_inc(turned_copied, 1)
                act.activation(probT[:, 1, P:2 * P], bank[4][:, 256:384], ACT.Copy).then_inc(turned_copied, 1)
                for qt in (2, 3):
                    act.wait_ge(probs_turned, c * 8 + 4 * e + qt + 1)
                    act.activation(probT[:, 0:qt + 1, qt * P:(qt + 1) * P],
                                   bank[3 + qt][:, 0:QW[qt]].rearrange("p (k q) -> p k q", q=P),
                                   ACT.Copy).then_inc(turned_copied, 1)

            with act.Fori(0, KC) as c:
                def J(m):
                    return Job(m, c, 8)
                make_hi(act, J(0).ahead())
                make_hi(act, J(1).ahead())
                result_of(act, J(0))
                act.activation(qT[:, :], bank[0][:, :], ACT.Copy).then_inc(taken[0], 1)
                make_hi(act, J(2).ahead())
                result_of(act, J(1))
                act.activation(kT[:, :], bank[1][:, :], ACT.Copy).then_inc(taken[1], 1)
                make_hi(act, J(3).ahead())
                result_of(act, J(2))
                act.activation(vT[:, :], bank[2][:, :], ACT.Copy).then_inc(taken[2], 1)
                exps(c, 0)
                make_hi(act, J(4).ahead())
                result_of(act, J(3))
                act.activation(xc[:, :], bank[3][:, :], ACT.Copy).then_inc(taken[3], 1)
                act.wait_ge(v_turned, c + 1)
                act.activation(vtok[:, :, :], bank[7][:, :].rearrange("p (t v) -> p t v", t=TT),
                               ACT.Copy).then_inc(vtok_copied, 1)
                exps(c, 1)
                make_hi(act, J(5).ahead())
                copy_turned(c, 0)
                make_hi(act, J(6).ahead())
                act.wait_ge(heads_mixed, c * 2 + 1)
                copy_turned(c, 1)
                make_hi(act, J(7).ahead())
                result_of(act, J(6))
                act.activation(sgate[:, :], bank[2][:, :], ACT.Tanh, scale=0.5).then_inc(zc_tanh, 1)
                act.wait_ge(yc_made, c + 1)
                act.activation(yc_hi[:, bass.ds(c, 1), :], conv[:, :], ACT.Copy).then_inc(ychi_made, 1)
                result_of(act, J(7))
                act.activation(sgate[:, :], bank[3][:, :], ACT.Tanh, scale=0.5).then_inc(za_tanh, 1)
                act.wait_ge(ya_made, c + 2)
                act.activation(ya_hi[:, bass.ds(c, 1), :], sgate[:, :], ACT.Copy).then_inc(yahi_made, 1)

            with act.Fori(0, 4) as i:
                def J(m):
                    return Job(J_B + m, i, 8)
                for h in range(2):
                    make_hi(act, J(4 * h).ahead())
                    make_hi(act, J(4 * h + 1).ahead())
                    result_of(act, J(4 * h))
                    act.activation(tg[:, 0, :], bank[0][:, :], ACT.Tanh, scale=0.5,
                                   bias=half_b[:, bass.ds(i * 2 + h, 1)]).then_inc(taken[0], 1)
                    make_hi(act, J(4 * h + 2).ahead())
                    make_hi(act, J(4 * h + 3).ahead())
                    result_of(act, J(4 * h + 2))
                    act.activation(tg[:, 1, :], bank[2][:, :], ACT.Tanh, scale=0.5,
                                   bias=half_b[:, bass.ds(i * 2 + h + 8, 1)]).then_inc(taken[2], 1)
                    act.wait_ge(merged, i * 2 + h + 1)
                    act.activation(mg_hi[:, bass.ds(i * 2 + h, 1), :], m1[:, :], ACT.Copy,
                                   scale=0.5).then_inc(mghi_made, 1)

            for m in range(8):
                make_hi(act, Job(J_C + m).ahead())
                was_taken(act, Job(J_C + m))
                act.activation(sq[:, m, :], res[:, m, :], ACT.Square).then_inc(sq_made, 1)
                act.wait_ge(hg_made, m + 1)
                act.activation(sq2[:, m, :], hg[:, m, :], ACT.Square).then_inc(sq_made, 1)
            for kc in range(KC):
                act.wait_ge(normed, KC + kc + 1)
                act.activation(act_hi[:, kc, :], hg[:, kc, :], ACT.Copy).then_inc(hi_act, 1)

            def copy(dst, src, sm, scale=1.0):
                act.activation(dst, src, ACT.Copy, scale=scale).then_inc(sm, 1)

            def square(dst, src, sm):
                act.activation(dst, src, ACT.Square).then_inc(sm, 1)

            make_hi(act, Job(J_D).ahead())
            for j in range(2):
                act.wait_ge(S("angles"), j + 1)
                act.activation(rope[:, 2 * j + 1, :], angle[:, j, :], ACT.Sin).then_inc(S("rope_made"), 1)
                act.activation(angle_abs[:, j, :], angle[:, j, :], ACT.Abs).then_inc(S("rope_made"), 1)
                act.wait_ge(S("rope_made"), 3 * j + 2)
                act.activation(rope[:, 2 * j, :], angle_abs[:, j, :], ACT.Sin, scale=-1.0,
                               bias=k("half_pi")).then_inc(S("rope_made"), 1)
            act.wait_ge(S("rope_made"), 6)
            for m in range(14):
                j = Job(J_D + m)
                if m:
                    make_hi(act, j.ahead())
                result_of(act, j)
                b, tk = bank[j.slot], taken[j.slot]
                part = S("part_copied")
                if m < 2:
                    copy(cqr[:, m, :], b[:, :], part)
                    square(sqc[:, m, :], b[:, :], tk)
                elif m == 2:
                    copy(ckvr[:, :], b[:, :], part)
                    square(sqc[:, 2, :], b[:, :], tk)
                elif m == 3:
                    act.activation(krg[0:32, :], b[0:32, :], ACT.Tanh, scale=0.5).then_inc(part, 1)
                    copy(krg[64:96, :], b[64:96, :], tk)
                elif m < 6:
                    copy(kvc[:, m - 4, :], b[:, :], tk)
                elif m < 8:
                    copy(ksw[:, m - 6, :], b[:, :], part)
                    square(sqk[:, m - 6, :], b[:, :], tk)
                elif m < 10:
                    copy(vsw[:, m - 8, :], b[:, :], tk)
                else:
                    copy(qh[:, m - 10, :], b[:, :], part, g("q"))
                    square(sqq[:, m - 10, :], b[:, :], tk)
            for b in range(2):
                act.wait_ge(S("vb_turned"), b + 1)
                copy(vtb[:, b, :, :], bank[4 + b][:, :].rearrange("p (t v) -> p t v", t=TT), S("vtb_copied"))
            for kv in range(2):
                act.wait_ge(S("hidden_made"), kv + 1)
                act.activation(hid[:, 2 * kv:2 * kv + 2, :], bank[kv][:, 0:4 * N_CMP].rearrange("p (h n) -> p h n", h=2),
                               ACT.Gelu_apprx_tanh).then_inc(S("hid_made"), 1)
            act.wait_ge(S("kc_made"), 1)
            copy(kcr[:, :], bank[3][:, 0:N_CMP], S("kc_copied"))
            square(kc_sq[:, :], bank[3][:, 0:N_CMP], S("kc_copied"))
            copy(vcs[0:N_CMP, :], bank[3][0:N_CMP, 64:192], S("kc_copied"))
            for p in range(20):
                act.wait_ge(S("prod_made"), p + 1)
                b = bank[p % 2]
                if 2 <= p < 16:
                    act.wait_ge(S("sums_made"), p - 1)
                if p < 8:
                    copy(mq[0:96, p, :], b[0:96, :], S("prod_copied"), g("mq", 0, slice(0, 96)))
                    square(sqb[0:96, p % 2, :], b[0:96, :], S("prod_taken"))
                elif p < 16:
                    copy(mk[0:64, p - 8, :], b[0:64, :], S("prod_copied"), g("mk", 0, slice(0, 64)))
                    if p < 10:
                        square(sqb[64:96, p % 2, :], krg[64:96, :], S("kr_squared"))
                    square(sqb[0:64, p % 2, :], b[0:64, :], S("prod_taken"))
                else:
                    copy(mv[:, p - 16, :], b[:, :], S("prod_taken"))
            act.wait_ge(S("roped"), 7)
            copy(mk[64:96, :, :], krg[64:96, :].unsqueeze(1).broadcast_to((32, 8, T)), S("kr_spread"))

            def pass_exp(p):
                x, s3 = PASSES[p], 4 * (p % 3)
                act.wait_ge(S("p_negmax"), p + 1)
                for qt in range(TT):
                    s = slice(QOFF[qt], QOFF[qt] + QW[qt])
                    act.activation(prob3[:, p % 3, s], prob3[:, p % 3, s], ACT.Exp,
                                   bias=negmax[:, s3 + qt:s3 + qt + 1],
                                   accum_out=den[:, s3 + qt:s3 + qt + 1]).then_inc(S("p_exp"), 1)
                if x["head"] is not None:
                    h = x["head"]
                    act.wait_ge(S("c_negmax"), h + 1)
                    c0 = 16 + 4 * (h % 2)
                    for qt in range(TT):
                        s = slice(P * (h % 2) + 32 * qt, P * (h % 2) + 32 * qt + N_CMP)
                        act.activation(cprob[:, s], cprob[:, s], ACT.Exp, bias=negmax[:, c0 + qt:c0 + qt + 1],
                                       accum_out=den[:, c0 + qt:c0 + qt + 1]).then_inc(S("c_exp"), 1)

            def pass_copy(p):
                x = PASSES[p]
                act.wait_ge(S("p_turned"), 4 * p + 2)
                copy(probT2[:, p % 2, 0, 0:256], bank[3][:, 0:256], S("p_copied"))
                copy(probT2[:, p % 2, 1, P:2 * P], bank[3][:, 256:384], S("p_copied"))
                for qt in (2, 3):
                    act.wait_ge(S("p_turned"), 4 * p + qt + 1)
                    copy(probT2[:, p % 2, 0:qt + 1, qt * P:(qt + 1) * P],
                         bank[2 + qt][:, 0:QW[qt]].rearrange("p (k q) -> p k q", q=P), S("p_copied"))
                if x["head"] is not None:
                    act.wait_ge(S("c_turned"), x["head"] + 1)
                    if x["head"]:
                        act.wait_ge(S("p_mixed"), p - 1)
                    copy(cprobT[0:N_CMP, :], bank[7][0:N_CMP, :], S("c_copied"))

            def pass_out(p):
                x = PASSES[p]
                if x["closes"]:
                    act.wait_ge(S("p_mixed"), p + 1)
                    c = x["chunk"]
                    copy(o_a[:, c, :] if c < 4 else o_b[:, c - 4, :], bank[6][:, :], S("o_taken"))

            pass_exp(0)
            for p in range(len(PASSES)):
                if p + 1 < len(PASSES):
                    pass_exp(p + 1)
                pass_copy(p)
                if p:
                    pass_out(p - 1)
            pass_out(len(PASSES) - 1)
            act.wait_ge(S("o_taken"), 8)
            for c in range(8):
                square(sqo[:, c, :], o_a[:, c, :] if c < 4 else o_b[:, c - 4, :], S("o_squared"))
            for c in range(8):
                act.wait_ge(normed, 2 * KC + c + 1)
                copy(act_hi[:, c, :], o_a[:, c, :] if c < 4 else o_b[:, c - 4, :], hi_act)
            for m in range(8):
                make_hi(act, Job(J_E + m).ahead())
                was_taken(act, Job(J_E + m))
                square(sq[:, m, :], res[:, m, :], sq_made)
            for c in range(8):
                act.wait_ge(normed, 3 * KC + c + 1)
                copy(act_hi[:, c, :], hg[:, c, :], hi_act)
            for m in range(16):
                j = Job(J_F + m)
                make_hi(act, j.ahead())
                result_of(act, j)
                copy(pq[:, m, :], bank[j.slot][:, :], S("pq_copied"))
                square(sqf[:, m, :], bank[j.slot][:, :], taken[j.slot])

            def activation_of(j, turn):
                act.wait_ge(acts_stored[(j.slot - J_U) % RING], turn * 16 + 16)
                result_of(act, j)
                act.activation(gelu[:, (j.slot - J_U) % RING, :], bank[j.slot][:, :],
                               ACT.Gelu_apprx_tanh).then_inc(taken[j.slot], 1)

            def u_job(n):
                j = Job(J_U + n)
                make_hi(act, j.ahead())
                activation_of(j, n // RING)

            def scale_routes(tt):
                act.wait_ge(S("routes_made"), tt + 1)
                if tt:
                    act.wait_ge(S("ssb_used"), tt)
                for h in range(8):
                    act.activation(ssb[:, 2 * h:2 * h + 2, :],
                                   bank[4 + h // 2][:, (h % 2) * 256:(h % 2) * 256 + 256].rearrange("p (a n) -> p a n", a=2),
                                   ACT.Copy, scale=rstd[:, tt * 8 + h:tt * 8 + h + 1]).then_inc(S("routes_scaled"), 1)

            def copy_selection(tt):
                act.wait_ge(S("sel_turned"), tt + 1)
                copy(selT[:, :, tt * P:(tt + 1) * P], bank[4][:, 0:3 * P].rearrange("p (n t) -> p n t", n=3),
                     S("sel_copied"))

            for slot in range(RING):
                act.sem_inc(acts_stored[slot], 16)
            act.wait_ge(ssq_made, 7)
            u_job(0)
            u_job(1)
            act.wait_ge(rstd_made, 9)
            scale_routes(0)
            u_job(2)
            u_job(3)
            for tt in range(TT):
                for m in range(U_TILE):
                    u_job(U_FIRST + U_TILE * tt + m)
                    if m == 3 and tt:
                        copy_selection(tt - 1)
                    if m == 7 and tt + 1 < TT:
                        scale_routes(tt + 1)
                    if m == 8:
                        act.wait_ge(S("vals_shifted"), tt + 1)
                        act.activation(sel[:, 2, :, :], sel[:, 2, :, :], ACT.Exp).then_inc(S("vals_exp"), 1)
            copy_selection(TT - 1)
            act.sem_inc(S("gates_copied"), 4)
            act.sem_inc(S("gates_stored0"), 16)
            act.sem_inc(S("gates_stored1"), 16)
            with act.Fori(0, TT) as tile:
                for q in range(8):
                    j = Job(J_U + U_GATES + q, tile, 8)
                    make_hi(act, j.ahead())
                    activation_of(j, tile * 2 + (U_GATES + q) // RING)
                    buf = q // 4
                    if q % 4 == 0:
                        act.wait_ge(S(f"gates_stored{buf}"), tile * 16 + 16)
                    for grp in range(4):
                        gi = tile * 32 + (q * 4 + grp)
                        act.wait_ge(S("gates_made4"), gi + 5)
                        t = (q % 4) * 16 + grp * 4
                        act.activation(stage[:, buf, :, t:t + 4].rearrange("p j t -> p t j"),
                                       bank[4 + grp][:, :].rearrange("p (t j) -> p t j", t=4),
                                       ACT.Copy).then_inc(S("gates_copied"), 1)
                    if q % 4 == 3:
                        act.wait_ge(S("gates_copied"), tile * 32 + (4 * q + 8))
                        act.dma_start(gates_dram[bass.ds(tile * 2 + buf, 1), :, :, :],
                                      stage[:, buf, :, :]).then_inc(S(f"gates_stored{buf}"), 16)
            with act.Fori(0, (P - U_REST) // RING) as i:
                for m in range(RING):
                    j = Job(J_U + U_REST + m, i)
                    make_hi(act, j.ahead())
                    activation_of(j, i + (U_REST + m) // RING)

            def weigh_hi(grp, slot, m):
                act.wait_ge(S("gated"), grp * GJ + (m + 1))
                act.activation(h_hi[:, slot, m, :], hf[:, slot, m, :], ACT.Copy).then_inc(S("h_hi_made"), 1)

            for m in range(GJ):
                weigh_hi(0, 0, m)

            def group(g2, slot, last=False):
                for dc in range(KC):
                    j = Job(J_V + GJ * slot + dc, g2, 2 * GJ)
                    if not (last and dc + AHEAD >= KC):
                        make_hi(act, j.ahead())
                    if not last:
                        weigh_hi(g2 * 2 + (slot + 1), 1 - slot, dc)

            with act.Fori(0, GROUPS // 2 - 1) as g2:
                group(g2, 0)
                group(g2, 1)
            group(GROUPS // 2 - 1, 0)
            group(GROUPS // 2 - 1, 1, last=True)
            for slot in range(RING):
                was_taken(act, Job(JOBS - RING + slot))
            act.dma_start(out, res[:, :, :]).then_inc(stored, 16)
            act.wait_ge(stored, 16)

        @block.vector
        def _(dve):
            dve.sem_inc(lo_made, RING)
            dve.sem_inc(scores_masked, 1)
            dve.sem_inc(ya_made, 1)
            dve.sem_inc(mg_split, 1)
            dve.wait_ge(const_landed, 32)
            dve.tensor_scalar(half_b[:, :], gain[:, GAIN["b_merge"]:GAIN["b_merge"] + 16], 0.5, None,
                              ALU.mult).then_inc(halfb_made, 1)

            def make_ms(b, col, to, width, step):
                dve.tensor_scalar(ms[:, to:to + 4], bank[b][:, col:col + 4], 1.0 / width, EPS,
                                  ALU.mult, ALU.add).then_inc(ms_made, 1)

            def diagonals(slot, col):
                for tt in range(TT):
                    dve.tensor_scalar(diag[:, slot + tt, :], ident, rstd[:, col + tt:col + tt + 1], None,
                                      ALU.mult).then_inc(diag_made, 1)

            dve.wait_ge(ssq_made, 1)
            make_ms(4, 0, 0, D, 1)
            for m in range(AHEAD):
                make_lo(dve, Job(m))
            dve.wait_ge(rstd_made, 1)
            diagonals(0, 0)
            dve.wait_ge(row_made, 1)
            for kc in range(KC):
                dve.scalar_tensor_tensor(out=hg[:, kc, :], in0=res[:, kc, :], scalar=g("norm_g", kc),
                                         in1=bank[5][:, :], op0=ALU.mult, op1=ALU.mult).then_inc(normed, 1)
            for kc in range(KC):
                dve.wait_ge(hi_act, kc + 1)
                dve.tensor_tensor(act_lo[:, kc, :], hg[:, kc, :], act_hi[:, kc, :].bitcast(F32),
                                  ALU.subtract).then_inc(lo_act, 1)

            def mask_scores(c, e):
                dve.wait_ge(bias_landed[e], (c + 1) * 16)
                dve.wait_ge(scores_made, c * 8 + 4 * e + 4)
                dve.memset(waited[:, e:e + 1], 0.0)
                for qt in range(TT):
                    b, col = QBANK[qt]
                    dve.tensor_tensor_reduce(out=prob[:, e, QOFF[qt]:QOFF[qt] + QW[qt]],
                                             in0=bank[4 + b][:, col:col + QW[qt]],
                                             in1=bias[:, e, T - QW[qt]:T], scale=SCALE_A, scalar=LOWEST,
                                             op0=ALU.add, op1=ALU.max,
                                             accum_out=mx[:, 4 * e + qt:4 * e + qt + 1]).then_inc(scores_masked, 1)
                dve.wait_ge(scores_masked, c * 8 + 4 * e + 5)
                dve.tensor_scalar(negmax[:, 4 * e:4 * e + 4], mx[:, 4 * e:4 * e + 4], -1.0, None,
                                  ALU.mult).then_inc(negmax_made, 1)

            def scale_probs(c, e):
                dve.wait_ge(probs_exp, c * 8 + 4 * e + 4)
                dve.reciprocal(inv[:, 4 * e:4 * e + 4], den[:, 4 * e:4 * e + 4]).then_inc(inv_made, 1)
                dve.wait_ge(inv_made, c * 2 + e + 1)
                for qt in range(TT):
                    s = slice(QOFF[qt], QOFF[qt] + QW[qt])
                    dve.tensor_scalar(prob[:, e, s], prob[:, e, s], inv[:, 4 * e + qt:4 * e + qt + 1], None,
                                      ALU.mult).then_inc(probs_scaled, 1)

            conv0 = GAIN["conv_w"]
            with dve.Fori(0, KC) as c:
                def J(m):
                    return Job(m, c, 8)

                def tap(j):
                    return gain[:, bass.ds(c * 3 + (conv0 + j), 1)]

                for m in range(4):
                    make_lo(dve, J(m).ahead())
                mask_scores(c, 0)
                make_lo(dve, J(4).ahead())
                mask_scores(c, 1)
                scale_probs(c, 0)
                make_lo(dve, J(5).ahead())
                was_taken(dve, J(3))
                result_of(dve, J(4))
                dve.tensor_tensor(prod[:, 2:T + 2], bank[0][:, :], xc[:, :], ALU.mult).then_inc(taken[0], 1)
                scale_probs(c, 1)
                was_taken(dve, J(4))
                dve.tensor_scalar(conv[:, :], prod[:, 2:T + 2], tap(2), None, ALU.mult).then_inc(conv_step, 1)
                dve.wait_ge(conv_step, c * 3 + 1)
                dve.scalar_tensor_tensor(out=conv[:, :], in0=prod[:, 1:T + 1], scalar=tap(1), in1=conv[:, :],
                                         op0=ALU.mult, op1=ALU.add).then_inc(conv_step, 1)
                dve.wait_ge(conv_step, c * 3 + 2)
                dve.scalar_tensor_tensor(out=conv[:, :], in0=prod[:, 0:T], scalar=tap(0), in1=conv[:, :],
                                         op0=ALU.mult, op1=ALU.add).then_inc(conv_step, 1)
                make_lo(dve, J(6).ahead())
                dve.wait_ge(conv_step, c * 3 + 3)
                result_of(dve, J(5))
                dve.tensor_tensor(conv[:, :], conv[:, :], bank[1][:, :], ALU.mult).then_inc(taken[1], 1)
                make_lo(dve, J(7).ahead())
                dve.wait_ge(zc_tanh, c + 1)
                dve.scalar_tensor_tensor(out=sgate[:, :], in0=sgate[:, :], scalar=1.0, in1=bank[2][:, :],
                                         op0=ALU.add, op1=ALU.mult).then_inc(taken[2], 1)
                was_taken(dve, J(5))
                was_taken(dve, J(6))
                dve.scalar_tensor_tensor(out=conv[:, :], in0=sgate[:, :], scalar=0.5, in1=conv[:, :],
                                         op0=ALU.mult, op1=ALU.mult).then_inc(yc_made, 1)
                dve.wait_ge(ychi_made, c + 1)
                dve.tensor_tensor(yc_lo[:, bass.ds(c, 1), :], conv[:, :],
                                  yc_hi[:, bass.ds(c, 1), :].bitcast(F32), ALU.subtract).then_inc(y_split, 1)
                dve.wait_ge(za_tanh, c + 1)
                dve.scalar_tensor_tensor(out=sgate[:, :], in0=sgate[:, :], scalar=1.0, in1=bank[3][:, :],
                                         op0=ALU.add, op1=ALU.mult).then_inc(taken[3], 1)
                was_taken(dve, J(7))
                dve.wait_ge(heads_mixed, c * 2 + 2)
                dve.scalar_tensor_tensor(out=sgate[:, :], in0=sgate[:, :], scalar=0.5, in1=bank[7][:, :],
                                         op0=ALU.mult, op1=ALU.mult).then_inc(ya_made, 1)
                dve.wait_ge(yahi_made, c + 1)
                dve.tensor_tensor(ya_lo[:, bass.ds(c, 1), :], sgate[:, :],
                                  ya_hi[:, bass.ds(c, 1), :].bitcast(F32), ALU.subtract).then_inc(y_split, 1)

            with dve.Fori(0, 4) as i:
                def J(m):
                    return Job(J_B + m, i, 8)
                for h in range(2):
                    chunk = bass.ds(i * 2 + h, 1)
                    make_lo(dve, J(4 * h).ahead())
                    make_lo(dve, J(4 * h + 1).ahead())
                    was_taken(dve, J(4 * h))
                    result_of(dve, J(4 * h + 1))
                    dve.wait_ge(mg_split, i * 2 + h + 1)
                    dve.scalar_tensor_tensor(out=m1[:, :], in0=tg[:, 0, :], scalar=1.0, in1=bank[1][:, :],
                                             op0=ALU.add, op1=ALU.mult).then_inc(taken[1], 1)
                    make_lo(dve, J(4 * h + 2).ahead())
                    make_lo(dve, J(4 * h + 3).ahead())
                    was_taken(dve, J(4 * h + 2))
                    result_of(dve, J(4 * h + 3))
                    dve.scalar_tensor_tensor(out=tg[:, 1, :], in0=tg[:, 1, :], scalar=1.0, in1=bank[3][:, :],
                                             op0=ALU.add, op1=ALU.mult).then_inc(taken[3], 1)
                    was_taken(dve, J(4 * h + 3))
                    dve.tensor_tensor(m1[:, :], m1[:, :], tg[:, 1, :], ALU.add).then_inc(merged, 1)
                    dve.wait_ge(mghi_made, i * 2 + h + 1)
                    dve.scalar_tensor_tensor(out=mg_lo[:, chunk, :], in0=m1[:, :], scalar=0.5,
                                             in1=mg_hi[:, chunk, :].bitcast(F32), op0=ALU.mult,
                                             op1=ALU.subtract).then_inc(mg_split, 1)

            for m in range(8):
                make_lo(dve, Job(J_C + m).ahead())
                j = Job(J_C + m)
                result_of(dve, j)
                dve.tensor_tensor(res[:, m, :], res[:, m, :], bank[j.slot][:, :], ALU.add).then_inc(taken[j.slot], 1)
                was_taken(dve, j)
                dve.tensor_scalar(hg[:, m, :], res[:, m, :], g("final_g", m), None, ALU.mult).then_inc(hg_made, 1)
            dve.wait_ge(ssq_made, 2)
            make_ms(4, 0, 0, D, 1)
            dve.wait_ge(rstd_made, 2)
            diagonals(0, 0)
            step = sem("norm_step")
            dve.tensor_tensor(ms[:, 8:12], rstd[:, 0:4], rstd[:, 0:4], ALU.mult).then_inc(step, 1)
            dve.wait_ge(step, 1)
            dve.tensor_tensor(ms[:, 4:8], ms[:, 8:12], bank[4][:, 4:8], ALU.mult).then_inc(step, 1)
            dve.wait_ge(step, 2)
            dve.tensor_scalar(ms[:, 4:8], ms[:, 4:8], 1.0 / D, EPS, ALU.mult, ALU.add).then_inc(ms_made, 1)
            dve.wait_ge(rstd_made, 3)
            dve.tensor_tensor(rstd[:, 8:12], rstd[:, 0:4], rstd[:, 4:8], ALU.mult).then_inc(step, 1)
            dve.wait_ge(step, 3)
            diagonals(4, 8)
            dve.wait_ge(row_made, 2)
            for kc in range(KC):
                dve.tensor_tensor(res[:, kc, :], hg[:, kc, :], bank[5][:, :], ALU.mult).then_inc(step, 1)
            dve.wait_ge(row_made, 3)
            for kc in range(KC):
                dve.scalar_tensor_tensor(out=hg[:, kc, :], in0=hg[:, kc, :], scalar=g("norm1", kc),
                                         in1=bank[6][:, :], op0=ALU.mult, op1=ALU.mult).then_inc(normed, 1)
            for kc in range(KC):
                dve.wait_ge(hi_act, KC + kc + 1)
                dve.tensor_tensor(act_lo[:, kc, :], hg[:, kc, :], act_hi[:, kc, :].bitcast(F32),
                                  ALU.subtract).then_inc(lo_act, 1)

            MAGIC = 1.5 * 2.0 ** 23
            TWO_PI = (6.28125, 0.0019350051879882812, 3.0198386e-07)
            v = S("angle_step")

            def angles():
                dve.wait_ge(S("pos_landed"), 16)
                dve.tensor_copy(pos_f[:, :], pos_i[:, :]).then_inc(v, 1)
                dve.wait_ge(v, 1)
                fr = k("freq")
                n = 1
                for j in range(2):
                    dve.tensor_scalar(angle[:, j, :], pos_f[:, :], fr[:, j:j + 1], None, ALU.mult).then_inc(v, 1)
                    n += 1
                    dve.wait_ge(v, n)
                    dve.tensor_scalar(turns[:, j, :], angle[:, j, :], 1 / (2 * np.pi), MAGIC, ALU.mult, ALU.add).then_inc(v, 1)
                    n += 1
                    dve.wait_ge(v, n)
                    dve.tensor_scalar(turns[:, j, :], turns[:, j, :], -MAGIC, None, ALU.add).then_inc(v, 1)
                    n += 1
                    for part in TWO_PI:
                        dve.wait_ge(v, n)
                        dve.scalar_tensor_tensor(out=angle[:, j, :], in0=turns[:, j, :], scalar=-part,
                                                 in1=angle[:, j, :], op0=ALU.mult, op1=ALU.add).then_inc(v, 1)
                        n += 1
                    dve.wait_ge(v, n)
                    dve.tensor_scalar(angle[:, j, :], angle[:, j, :], 3.1415925, -3.1415925,
                                      ALU.min, ALU.max).then_inc(S("angles"), 1)

            angles()
            for m in range(14):
                make_lo(dve, Job(J_D + m).ahead())
                if m == 7:
                    for grp in range(2):
                        was_taken(dve, Job(J_D + 4 + grp))
                        src = kvc[:, grp, :]
                        src = bass.AP(tensor=src.tensor, offset=src.offset,
                                      ap=[list(src.ap[0]), [1, CMP_LEN], [CMP_STRIDE, N_CMP]])
                        pos = gain[:, GAIN["pos"]:GAIN["pos"] + CMP_LEN].unsqueeze(2).broadcast_to((P, CMP_LEN, N_CMP))
                        dve.tensor_tensor(kp[:, :, grp * N_CMP:(grp + 1) * N_CMP], src, pos, ALU.add)\
                            .then_inc(S("kp_made"), 1)
            dve.wait_ge(S("gates_turned"), 1)
            dve.tensor_scalar(gate[:, :], bank[6][:, 0:TT * 24], 0.5, 0.5, ALU.mult, ALU.add).then_inc(S("gates_made"), 1)
            dve.wait_ge(ssq_made, 3)

            def by_tile(t, a, b):
                return t.rearrange("p (t n) -> p t n", t=TT)[:, :, a:b]

            for a, b, width in ((0, 12, 64), (12, 13, 256), (13, 14, 128)):
                dve.tensor_scalar(by_tile(ms[:, 0:64], a, b), by_tile(bank[7][:, 0:64], a, b), 1.0 / width, EPS,
                                  ALU.mult, ALU.add).then_inc(ms_made, 1)
            dve.wait_ge(rstd_made, 4)
            dve.tensor_scalar(by_tile(rq_a[:, :], 0, 8), by_tile(rstd[:, 0:64], 0, 8), SCALE_A, None,
                              ALU.mult).then_inc(S("rq_made"), 1)
            DCOL = [12, 13, 8, 9, 10, 11]

            def diag_unit(u, col, per=16):
                if u >= 2:
                    dve.wait_ge(row_made, 3 + u - 1 + (u > 6))
                for tt in range(TT):
                    dve.tensor_scalar(diag[:, 4 * (u % 2) + tt, :], ident, rstd[:, tt * per + col:tt * per + col + 1],
                                      None, ALU.mult).then_inc(diag_made, 1)

            diag_unit(0, 12)
            diag_unit(1, 13)
            dve.wait_ge(row_made, 4)
            for c in range(2):
                dve.scalar_tensor_tensor(out=cqr[:, c, :], in0=cqr[:, c, :], scalar=g("cq", c), in1=bank[6][:, :],
                                         op0=ALU.mult, op1=ALU.mult).then_inc(S("latents"), 1)
            diag_unit(2, 8)
            dve.wait_ge(row_made, 5)
            dve.scalar_tensor_tensor(out=ckvr[:, :], in0=ckvr[:, :], scalar=g("ckv"), in1=bank[2][:, :],
                                     op0=ALU.mult, op1=ALU.mult).then_inc(S("latents"), 1)
            diag_unit(3, 9)

            def apply_rope(r_, x, rows=slice(0, P), table=0):
                dve.wait_ge(S("rot_made"), r_ + 1)
                if r_ >= 2:
                    dve.wait_ge(S("roped"), r_ - 1)
                tmp = rtmp[rows, r_ % 2, :]
                dve.tensor_tensor(tmp, bank[4 + r_ % 2][rows, :], rope[rows, 2 * table + 1, :], ALU.mult)\
                    .then_inc(S("rot_used"), 1)
                dve.tensor_tensor(x, x, rope[rows, 2 * table, :], ALU.mult).then_inc(S("rope_half"), 1)
                dve.wait_ge(S("rope_half"), r_ + 1)
                dve.tensor_tensor(x, x, tmp, ALU.add).then_inc(S("roped"), 1)

            for c in range(4):
                apply_rope(c, qh[:, c, :])
            diag_unit(4, 10)
            diag_unit(5, 11)
            dve.wait_ge(row_made, 7)
            dve.scalar_tensor_tensor(out=ksw[:, 0, :], in0=ksw[:, 0, :], scalar=g("ks"), in1=bank[6][:, :],
                                     op0=ALU.mult, op1=ALU.mult).then_inc(S("kw_normed"), 1)
            dve.wait_ge(row_made, 9)
            dve.scalar_tensor_tensor(out=ksw[:, 1, :], in0=ksw[:, 1, :], scalar=g("kw"), in1=bank[2][:, :],
                                     op0=ALU.mult, op1=ALU.mult).then_inc(S("kw_normed"), 1)
            dve.wait_ge(ssq_made, 4)
            dve.tensor_scalar(ms[0:N_CMP, 0:2], bank[7][0:N_CMP, 96:98], 1.0 / 64, EPS, ALU.mult, ALU.add)\
                .then_inc(ms_made, 1)
            dve.wait_ge(rstd_made, 5)
            for grp in range(2):
                dve.tensor_scalar(diag[0:N_CMP, grp, 0:N_CMP], k("ident", slice(0, N_CMP), slice(0, N_CMP)),
                                  rstd[0:N_CMP, grp:grp + 1], None, ALU.mult).then_inc(diag_made, 1)
            dve.wait_ge(row_made, 10)
            dve.scalar_tensor_tensor(out=kcr[:, :], in0=kcr[:, :], scalar=g("kc"), in1=bank[3][:, 256:256 + N_CMP],
                                     op0=ALU.mult, op1=ALU.mult).then_inc(S("kc_normed"), 1)
            apply_rope(4, ksw[:, 0, :])
            apply_rope(5, ksw[:, 1, :])

            def at_ends(j):
                t = rope[:, j, :]
                return bass.AP(tensor=t.tensor, offset=t.offset + CMP_LEN - 1,
                               ap=[list(t.ap[0]), [CMP_STRIDE, N_CMP]])
            dve.wait_ge(S("kc_rot"), 1)
            dve.tensor_tensor(kc_tmp[:, :], bank[3][:, 320:320 + N_CMP], at_ends(1), ALU.mult).then_inc(S("kc_step"), 1)
            dve.tensor_tensor(kcr[:, :], kcr[:, :], at_ends(0), ALU.mult).then_inc(S("kc_step"), 1)
            dve.wait_ge(S("kc_step"), 2)
            dve.tensor_tensor(kcr[:, :], kcr[:, :], kc_tmp[:, :], ALU.add).then_inc(S("kc_roped"), 1)

            r96 = slice(64, 96)
            dve.wait_ge(S("kr_squared"), 2)
            dve.tensor_scalar(krg[r96, :], krg[r96, :], g("mk", 0, r96), None, ALU.mult).then_inc(S("kr_scaled"), 1)
            dve.wait_ge(S("kr_scaled"), 1)
            apply_rope(6, krg[r96, :], r96, 1)
            dve.wait_ge(S("sums_made"), 16)
            dve.tensor_scalar(ms[:, 0:64], bank[7][:, 128:192], 1.0 / 96, EPS, ALU.mult, ALU.add).then_inc(ms_made, 1)
            for h in range(8):
                apply_rope(7 + h, mq[r96, h, :], r96, 1)
            dve.wait_ge(rstd_made, 6)
            dve.tensor_scalar(by_tile(rq_b[:, :], 0, 8), by_tile(rstd[:, 0:64], 0, 8), SCALE_B, None,
                              ALU.mult).then_inc(S("rq_made"), 1)
            dve.wait_ge(S("kr_spread"), 1)
            for h in range(9):
                if h < 8:
                    diag_unit(6 + h, 8 + h)
                if h:
                    dve.wait_ge(row_made, 10 + h)
                    dve.tensor_tensor(mk[0:96, h - 1, :], mk[0:96, h - 1, :], bank[2 + (h - 1) % 2][0:96, :], ALU.mult)\
                        .then_inc(S("mk_normed"), 1)
            dve.wait_ge(S("rq_made"), 2)
            causal, cmask = k("causal"), k("cmp_mask")

            def pass_mask(p):
                x, s3 = PASSES[p], 4 * (p % 3)
                for qt in range(TT):
                    b, col = QBANK[qt]
                    dve.wait_ge(S("p_scores"), 4 * p + max(qt + 1, 2))
                    if qt == 0 and x["head"] is not None:
                        dve.wait_ge(S("c_scores"), x["head"] + 1)
                    dve.tensor_tensor_reduce(out=prob3[:, p % 3, QOFF[qt]:QOFF[qt] + QW[qt]],
                                             in0=bank[b][:, col:col + QW[qt]], in1=causal[:, T - QW[qt]:T],
                                             scale=rq_col(x, qt), scalar=LOWEST, op0=ALU.add, op1=ALU.max,
                                             accum_out=mx[:, s3 + qt:s3 + qt + 1]).then_inc(S("p_masked"), 1)
                if x["head"] is not None:
                    h = x["head"]
                    c0 = 16 + 4 * (h % 2)
                    for qt in range(TT):
                        dve.tensor_tensor_reduce(out=cprob[:, P * (h % 2) + 32 * qt:P * (h % 2) + 32 * qt + N_CMP],
                                                 in0=bank[0][:, 384 + 32 * qt:384 + 32 * qt + N_CMP],
                                                 in1=cmask[:, N_CMP * qt:N_CMP * (qt + 1)], scale=rq_col(x, qt),
                                                 scalar=LOWEST, op0=ALU.add, op1=ALU.max,
                                                 accum_out=mx[:, c0 + qt:c0 + qt + 1]).then_inc(S("c_masked"), 1)
                dve.wait_ge(S("p_masked"), 4 * p + 4)
                dve.tensor_scalar(negmax[:, s3:s3 + 4], mx[:, s3:s3 + 4], -1.0, None, ALU.mult).then_inc(S("p_negmax"), 1)
                if x["head"] is not None:
                    dve.wait_ge(S("c_masked"), 4 * h + 4)
                    dve.tensor_scalar(negmax[:, c0:c0 + 4], mx[:, c0:c0 + 4], -1.0, None, ALU.mult)\
                        .then_inc(S("c_negmax"), 1)

            def gates_of(h, branch):
                return gate[:, :].rearrange("p (t n) -> p t n", t=TT)[:, :, 3 * h + branch:3 * h + branch + 1]\
                    .rearrange("p t n -> p (t n)")

            def pass_scale(p):
                x, s3 = PASSES[p], 4 * (p % 3)
                dve.wait_ge(S("p_exp"), 4 * p + 4)
                dve.reciprocal(inv[:, s3:s3 + 4], den[:, s3:s3 + 4]).then_inc(S("p_inv"), 1)
                by = inv
                if x["gate"]:
                    dve.wait_ge(S("p_inv"), p + 1)
                    dve.tensor_tensor(factor[:, s3:s3 + 4], inv[:, s3:s3 + 4], gates_of(*x["gate"]), ALU.mult)\
                        .then_inc(S("p_factor"), 1)
                    dve.wait_ge(S("p_factor"), p + 1)
                    by = factor
                else:
                    dve.wait_ge(S("p_inv"), p + 1)
                for qt in range(TT):
                    s = slice(QOFF[qt], QOFF[qt] + QW[qt])
                    dve.tensor_scalar(prob3[:, p % 3, s], prob3[:, p % 3, s], by[:, s3 + qt:s3 + qt + 1], None,
                                      ALU.mult).then_inc(S("p_scaled"), 1)
                if x["head"] is not None:
                    h = x["head"]
                    c0 = 16 + 4 * (h % 2)
                    dve.wait_ge(S("c_exp"), 4 * h + 4)
                    dve.reciprocal(inv[:, c0:c0 + 4], den[:, c0:c0 + 4]).then_inc(S("c_step"), 1)
                    dve.wait_ge(S("c_step"), 3 * h + 1)
                    dve.tensor_tensor(factor[:, c0:c0 + 4], inv[:, c0:c0 + 4], gates_of(x["gate"][0], 0), ALU.mult)\
                        .then_inc(S("c_step"), 1)
                    dve.wait_ge(S("c_step"), 3 * h + 2)
                    dve.tensor_tensor(factor[:, c0:c0 + 1], factor[:, c0:c0 + 1], k("valid"), ALU.mult)\
                        .then_inc(S("c_step"), 1)
                    dve.wait_ge(S("c_step"), 3 * h + 3)
                    for qt in range(TT):
                        s = slice(P * (h % 2) + 32 * qt, P * (h % 2) + 32 * qt + N_CMP)
                        dve.tensor_scalar(cprob[:, s], cprob[:, s], factor[:, c0 + qt:c0 + qt + 1], None, ALU.mult)\
                            .then_inc(S("c_scaled"), 1)

            pass_mask(0)
            pass_mask(1)
            for p in range(len(PASSES)):
                pass_scale(p)
                if p + 2 < len(PASSES):
                    pass_mask(p + 2)
            dve.wait_ge(ssq_made, 5)
            dve.tensor_scalar(ms[:, 0:8], bank[0][:, 0:8], 1.0 / 512, EPS, ALU.mult, ALU.add).then_inc(ms_made, 1)
            dve.wait_ge(rstd_made, 7)
            diagonals(0, 0)
            diagonals(4, 4)
            for c in range(8):
                dve.wait_ge(row_made, 19 + c // 4)
                x = o_a[:, c, :] if c < 4 else o_b[:, c - 4, :]
                dve.scalar_tensor_tensor(out=x, in0=x, scalar=g("out", c), in1=bank[4 + c // 4][:, :],
                                         op0=ALU.mult, op1=ALU.mult).then_inc(normed, 1)
            for c in range(8):
                dve.wait_ge(hi_act, 2 * KC + c + 1)
                dve.tensor_tensor(act_lo[:, c, :], o_a[:, c, :] if c < 4 else o_b[:, c - 4, :],
                                  act_hi[:, c, :].bitcast(F32), ALU.subtract).then_inc(lo_act, 1)
            for m in range(8):
                j = Job(J_E + m)
                make_lo(dve, j.ahead())
                result_of(dve, j)
                dve.tensor_tensor(res[:, m, :], res[:, m, :], bank[j.slot][:, :], ALU.add).then_inc(taken[j.slot], 1)
            dve.wait_ge(ssq_made, 6)
            make_ms(4, 0, 0, D, 1)
            dve.wait_ge(rstd_made, 8)
            diagonals(0, 0)
            dve.wait_ge(row_made, 21)
            for c in range(KC):
                dve.scalar_tensor_tensor(out=hg[:, c, :], in0=res[:, c, :], scalar=g("norm2", c), in1=bank[5][:, :],
                                         op0=ALU.mult, op1=ALU.mult).then_inc(normed, 1)
            for c in range(KC):
                dve.wait_ge(hi_act, 3 * KC + c + 1)
                dve.tensor_tensor(act_lo[:, c, :], hg[:, c, :], act_hi[:, c, :].bitcast(F32),
                                  ALU.subtract).then_inc(lo_act, 1)
            for m in range(16):
                make_lo(dve, Job(J_F + m).ahead())

            def u_job(n):
                make_lo(dve, Job(J_U + n).ahead())

            u_job(0)
            dve.wait_ge(ssq_made, 7)
            dve.tensor_scalar(ms[:, 0:32], bank[7][:, 0:32], 1.0 / 256, EPS, ALU.mult, ALU.add).then_inc(ms_made, 1)

            q = [0]
            step = S("route_step")

            def then(ins):
                q[0] += 1
                ins.then_inc(step, 1)
                dve.wait_ge(step, q[0])

            def mark(ins):
                q[0] += 1
                ins.then_inc(step, 1)

            iota = k("iota")
            for n in range(1, U_FIRST):
                u_job(n)
            for tt in range(TT):
                def beside(m):
                    u_job(U_FIRST + U_TILE * tt + m)

                for hc in range(16):
                    if hc % 2 == 0:
                        dve.wait_ge(S("routes_scaled"), 8 * tt + hc // 2 + 1)
                    mark(dve.max(v16[:, hc, 0:8], ssb[:, hc, :]))
                beside(0)
                dve.wait_ge(step, q[0])
                for hc in range(16):
                    mark(dve.match_replace(srep[:, hc, :], v16[:, hc, 0:8], ssb[:, hc, :], LOWEST))
                    mark(dve.max_index(i16[:, hc, 0:8], v16[:, hc, 0:8], ssb[:, hc, :]))
                    if hc == 7:
                        beside(1)
                beside(2)
                dve.wait_ge(step, q[0])
                for hc in range(16):
                    mark(dve.max(v16[:, hc, 8:16], srep[:, hc, :]))
                beside(3)
                dve.wait_ge(step, q[0])
                for hc in range(16):
                    ins = dve.max_index(i16[:, hc, 8:16], v16[:, hc, 8:16], srep[:, hc, :])
                    if hc < 15:
                        mark(ins)
                ins.then_inc(S("ssb_used"), 1)
                beside(4)
                dve.wait_ge(S("ssb_used"), tt + 1)
                mark(dve.tensor_copy(i16f[:, :, :], i16[:, :, :]))
                vv = v16[:, :, :].rearrange("p (h a) k -> p h a k", a=2)
                then(dve.tensor_tensor(cand[:, :, :, :], vv[:, :, 0, :].unsqueeze(3).broadcast_to((P, 8, 16, 16)),
                                       vv[:, :, 1, :].unsqueeze(2).broadcast_to((P, 8, 16, 16)), ALU.add))

                def flat(t, h):
                    return t[:, h, :, :].rearrange("p a b -> p (a b)")
                for h in range(8):
                    mark(dve.max(vals[:, h, 0:8], flat(cand, h)))
                dve.wait_ge(step, q[0])
                beside(5)
                for h in range(8):
                    mark(dve.match_replace(flat(crep, h), vals[:, h, 0:8], flat(cand, h), LOWEST))
                    mark(dve.max_index(vci[:, h, 0:8], vals[:, h, 0:8], flat(cand, h)))
                dve.wait_ge(step, q[0])
                for h in range(8):
                    mark(dve.max(vals[:, h, 8:16], flat(crep, h)))
                beside(6)
                dve.wait_ge(step, q[0])
                if tt:
                    dve.wait_ge(S("sel_turned"), tt)
                dve.tensor_tensor(sel[:, 2, :, :], vals[:, :, :], vals[:, :, 0:1].broadcast_to((P, 8, 16)), ALU.subtract)\
                    .then_inc(S("vals_shifted"), 1)
                for h in range(8):
                    mark(dve.max_index(vci[:, h, 8:16], vals[:, h, 8:16], flat(crep, h)))
                dve.wait_ge(step, q[0])
                mark(dve.tensor_scalar(ca[:, 0, :, :], vci[:, :, :], 4, None, ALU.logical_shift_right))
                then(dve.tensor_scalar(ca[:, 1, :, :], vci[:, :, :], 15, None, ALU.bitwise_and))
                then(dve.tensor_copy(caf[:, :, :, :], ca[:, :, :, :]))
                beside(7)
                for half in range(2):
                    then(dve.tensor_tensor(eq[:, :, :, :].rearrange("p h k a -> p (h k) a"),
                                           iota[:, 0:16].unsqueeze(1).broadcast_to((P, P, 16)),
                                           caf[:, half, :, :].rearrange("p h k -> p (h k)").unsqueeze(2).broadcast_to((P, P, 16)),
                                           ALU.is_equal))
                    ii = i16f[:, :, :].rearrange("p (h a) k -> p h a k", a=2)[:, :, half, :]
                    then(dve.tensor_tensor(eq[:, :, :, :], eq[:, :, :, :],
                                           ii.unsqueeze(2).broadcast_to((P, 8, 16, 16)), ALU.mult))
                    then(dve.tensor_reduce(sel[:, half, :, :].rearrange("p h k -> p (h k)"),
                                           eq[:, :, :, :].rearrange("p h k a -> p (h k) a"), AX, ALU.add))
                    beside(8 + half)
                dve.wait_ge(S("vals_exp"), tt + 1)
                then(dve.tensor_reduce(vsum[:, 0, :], sel[:, 2, :, :], AX, ALU.add))
                then(dve.reciprocal(vsum[:, 1, :], vsum[:, 0, :]))
                dve.tensor_tensor(sel[:, 2, :, :], sel[:, 2, :, :], vsum[:, 1, :].unsqueeze(2).broadcast_to((P, 8, 16)),
                                  ALU.mult).then_inc(S("selected"), 1)
                beside(10)

            dve.wait_ge(S("sel_copied"), TT)
            with dve.Fori(0, TT) as tile:
                for q in range(8):
                    for grp in range(4):
                        if grp == 2:
                            make_lo(dve, Job(J_U + U_GATES + q, tile, 8).ahead())
                        dve.wait_ge(S("gates_made4"), tile * 32 + (q * 4 + grp + 1))
                        for x in range(4):
                            t = tile * P + (q * 16 + grp * 4 + x)
                            slot = grp * 4 + x
                            dve.tensor_scalar(hot[:, slot, 0, :], iota, selT[:, 0, bass.ds(t, 1)], None, ALU.is_equal)
                            ins = dve.tensor_scalar(hot[:, slot, 1, :], iota, selT[:, 1, bass.ds(t, 1)],
                                                    selT[:, 2, bass.ds(t, 1)], ALU.is_equal, ALU.mult)
                        ins.then_inc(S("hot_made"), 1)
            with dve.Fori(0, (P - U_REST) // RING) as i:
                for m in range(RING):
                    make_lo(dve, Job(J_U + U_REST + m, i).ahead())

            def weigh(grp, slot, m):
                dve.tensor_tensor(hf[:, slot, m, :].rearrange("p (b t) -> p b t", t=64),
                                  hf[:, slot, m, :].rearrange("p (b t) -> p b t", t=64),
                                  wg[:, slot, :, m, :], ALU.mult).then_inc(S("gated"), 1)

            def weigh_lo(grp, slot, m):
                dve.wait_ge(S("h_hi_made"), grp * GJ + (m + 1))
                dve.tensor_tensor(h_lo[:, slot, m, :], hf[:, slot, m, :], h_hi[:, slot, m, :].bitcast(F32),
                                  ALU.subtract).then_inc(S("h_split"), 1)

            def group_landed(lap, slot):
                dve.wait_ge(S(f"wg_landed{slot}"), lap * 16 + 16)
                dve.wait_ge(S(f"hf_landed{slot}"), lap * 16 + 16)

            group_landed(0, 0)
            for m in range(GJ):
                weigh(0, 0, m)
            for m in range(GJ):
                weigh_lo(0, 0, m)

            def group(g2, slot, last=False):
                if not last:
                    group_landed(g2 + slot, 1 - slot)
                for dc in range(KC):
                    j = Job(J_V + GJ * slot + dc, g2, 2 * GJ)
                    if not (last and dc + AHEAD >= KC):
                        make_lo(dve, j.ahead())
                    if not last:
                        weigh(g2 * 2 + (slot + 1), 1 - slot, dc)
                        if dc:
                            weigh_lo(g2 * 2 + (slot + 1), 1 - slot, dc - 1)
                    result_of(dve, j)
                    dve.tensor_tensor(res[:, dc, :], res[:, dc, :], bank[j.slot][:, :], ALU.add)\
                        .then_inc(taken[j.slot], 1)
                if not last:
                    weigh_lo(g2 * 2 + (slot + 1), 1 - slot, KC - 1)

            with dve.Fori(0, GROUPS // 2 - 1) as g2:
                group(g2, 0)
                group(g2, 1)
            group(GROUPS // 2 - 1, 0)
            group(GROUPS // 2 - 1, 1, last=True)


def _weights(a):
    n = a.shape[1] // P
    return a.reshape(KC, P, n, P).transpose(2, 1, 0, 3).reshape(n, P, KC * P)


def lay_out(i):
    f = {k: np.asarray(v) for k, v in i.items()}
    w_in = _weights(f["w_in"][0])
    part = {n: w_in[8 * j:8 * j + 8] for j, n in enumerate("xc bg cg zc q k v za gc ga".split())}
    woc, woa, wo = (_weights(f[n][0]) for n in ("w_out_conv", "w_out_attn", "w_o"))
    a = np.stack([part[n] for n in "q k v xc cg bg zc za".split()], 1).reshape(64, P, D)
    b = np.stack([part["gc"], woc, part["ga"], woa], 1).reshape(32, P, D)

    w2 = f["w_in_2"][0]
    cut = np.cumsum([0, 512, 128, 128, 128, 128, 128, 128, 24, 256, 128, 32])
    q, kc, vc, ks, vs, kw, vw, gt, cq, ckv, kr = (w2[:, cut[j]:cut[j + 1]] for j in range(11))
    order = [h for c in range(4) for h in (c, c + 4)]
    qh = q.reshape(D, 8, 64)[:, order].reshape(D, 512)
    krg = np.zeros((D, P), w2.dtype)
    krg[:, 0:24] = gt
    krg[:, 64:96] = kr
    d = np.concatenate([cq, ckv, krg, kc[:, :64], vc[:, :64], kc[:, 64:], vc[:, 64:], ks, kw, vs, vw, qh], 1)
    wo2 = f["w_out_2"][0]
    wo2 = np.concatenate([wo2[:512].reshape(8, 64, D)[order].reshape(512, D), wo2[512:]], 0)
    u = f["peer_u_2"][0].reshape(P, GROUPS, GJ, KC, P).transpose(1, 2, 4, 3, 0).reshape(GROUPS, GJ, P, D)
    v = f["peer_v_2"][0].reshape(P, GROUPS, GJ, KC, P).transpose(1, 3, 0, 2, 4).reshape(GROUPS, KC, P, D)
    u, v = u.reshape(P, P, D), v.reshape(GROUPS * KC, P, D)
    tiles = np.concatenate([a, b, wo, _weights(d), _weights(wo2), _weights(f["peer_w_q_2"][0]), u, v], 0)

    def chunks(v):
        return v.reshape(-1, P).T

    gains = np.zeros((P, N_GAIN), np.float32)

    def put(name, v):
        gains[:v.shape[0], GAIN[name]:GAIN[name] + v.shape[1]] = v

    put("norm_g", chunks(f["norm_g"][0]))
    put("final_g", chunks(f["final_g"]))
    put("b_merge", chunks(f["b_merge"][0]))
    put("conv_w", f["conv_w"][0].reshape(3, 8, P).transpose(2, 1, 0).reshape(P, 24))
    put("norm1", chunks(f["norm1_gain_2"][0]))
    for n, s in (("q", "nsa_q_gain_2"), ("kc", "nsa_kc_gain_2"), ("ks", "nsa_ks_gain_2"), ("kw", "nsa_kw_gain_2")):
        put(n, np.concatenate([f[s][0], f[s][0]])[:, None])
    put("cq", chunks(f["mla_q_lora_gain_2"][0]))
    put("ckv", chunks(f["mla_kv_lora_gain_2"][0]))
    put("mq", f["mla_q_gain_2"][0][:, None])
    put("mk", f["mla_k_gain_2"][0][:, None])
    ga = f["out_gain_a_2"][0].reshape(8, 64)[order].reshape(512)
    put("out", chunks(np.concatenate([ga, f["out_gain_b_2"][0]])))
    put("norm2", chunks(f["norm2_gain_2"][0]))
    pos = f["cmp_pos_2"][0].T
    put("pos", np.concatenate([pos, pos], 0))

    def w1(a):
        return a.reshape(CMP_LEN, 64, 256).transpose(1, 0, 2)

    cmp_w1 = np.concatenate([w1(f["cmp_k_w1_2"][0]), w1(f["cmp_v_w1_2"][0])], 0)
    cmp_w2 = np.stack([f["cmp_k_w2_2"][0].reshape(2, P, 64), f["cmp_v_w2_2"][0].reshape(2, P, 64)], 0)
    ukv = f["mla_w_ukv_2"][0].reshape(P, 8, 2, 64).transpose(0, 2, 1, 3)
    return dict(
        tiles=tiles, x_t=f["x"][0].T.reshape(KC, P, T).transpose(1, 0, 2), consts=CONSTS, gains=gains,
        alibi=_alibi(), positions=f["positions_2"],
        cmp_w1=cmp_w1, cmp_w2=cmp_w2.transpose(2, 0, 1, 3),
        w_uq=f["mla_w_uq_2"][0].reshape(2, P, 768).transpose(1, 0, 2), w_ukv=ukv,
        sub_keys=f["peer_sub_keys_2"][0].transpose(3, 0, 1, 2).reshape(P, 16, P),
    )


def kernel(**inputs):
    import concourse.bacc as bacc
    from concourse.bass_utils import run_bass_kernel_spmd

    nc = bacc.Bacc("TRN2", target_bir_lowering=False, num_devices=1)
    arrays = {n: np.ascontiguousarray(a) for n, a in lay_out(inputs).items()}
    args = [nc.dram_tensor(n, a.shape, mybir.dt.from_np(a.dtype), kind="ExternalInput").ap()
            for n, a in arrays.items()]
    gates = nc.dram_tensor("gates_dram", (TT * 2, P, P, 64), F32, kind="Internal").ap()
    acts = nc.dram_tensor("acts_dram", (P, P, T), F32, kind="Internal").ap()
    out = nc.dram_tensor("out_t", (P, KC, T), F32, kind="ExternalOutput").ap()
    two_layer_kernel(nc, *args, gates, acts, out)
    r = run_bass_kernel_spmd(nc, [arrays], core_ids=[0])
    out = r.results[0]["out_t"]
    return np.ascontiguousarray(out.transpose(2, 1, 0).reshape(1, T, D))
```

```python
from contextlib import ExitStack

import concourse.bass as bass
import numpy as np
from concourse import mybir

F32 = mybir.dt.float32
F32R = mybir.dt.float32r
I32 = mybir.dt.int32
U32 = mybir.dt.uint32
ALU = mybir.AluOpType
ACT = mybir.ActivationFunctionType
AX = mybir.AxisListType.X

P = 128
T = 512
TT = T // P
D = 1024
KC = D // P
EPS = 1e-6
NEG = -1e30
LOWEST = -3e38

J_A = 0
J_B = J_A + 64
J_C = J_B + 32
J_D = J_C + 8
J_E = J_D + 14
J_F = J_E + 8
J_U = J_F + 16
J_V = J_U + P
GROUPS = 16
GJ = 8
JOBS = J_V + GROUPS * GJ
U_FIRST = 4
U_TILE = 11
U_GATES = U_FIRST + TT * U_TILE
U_REST = U_GATES + T // 16
RING = 4
AHEAD = 2

N_CMP = 31
CMP_LEN = 32
CMP_STRIDE = 16

QOFF = [0, 128, 384, 768]
QW = [128, 256, 384, 512]
QALL = 1280
QBANK = [(0, 0), (0, 128), (1, 0), (2, 0)]
SCALE_A = 64.0 ** -0.5
SCALE_B = 96.0 ** -0.5

CONST = {}


def _consts():
    parts, at = [], 0

    def put(name, a):
        nonlocal at
        a = np.asarray(a, np.float32)
        full = np.zeros((P, a.shape[1]), np.float32)
        full[: a.shape[0]] = a
        CONST[name] = (at, at + a.shape[1])
        at += a.shape[1]
        parts.append(full)

    p = np.arange(P)
    put("ident", np.eye(P))
    put("ones", np.ones((P, P)))
    put("halves", np.stack([p < 64, p >= 64], 1))
    r = np.zeros((P, P))
    for base in (0, 64):
        for i in range(8):
            r[base + i, base + i + 8] = -1
            r[base + i + 8, base + i] = 1
    put("rot64", r.T)
    r = np.zeros((P, 32))
    for i in range(16):
        r[64 + i + 16, i] = -1
        r[64 + i, i + 16] = 1
    put("rot32", r)
    put("iota", np.tile(np.arange(P), (P, 1)))
    f_a = np.zeros(P, np.float32)
    f_b = np.zeros(P, np.float32)
    inv_a = np.float32(500000.0) ** (-np.arange(0, 16, 2, dtype=np.float32) / np.float32(16))
    inv_b = np.float32(500000.0) ** (-np.arange(0, 32, 2, dtype=np.float32) / np.float32(32))
    for base in (0, 64):
        f_a[base:base + 8] = inv_a
        f_a[base + 8:base + 16] = inv_a
    f_b[64:80] = inv_b
    f_b[80:96] = inv_b
    put("freq", np.stack([f_a, f_b], 1))
    put("valid", (p[:, None] >= CMP_LEN - 1))
    put("half_pi", np.full((P, 1), np.pi / 2))
    put("eps", np.full((P, 1), EPS))
    put("half_eps", np.full((P, 1), -0.5 * EPS))
    delta = p[:, None] + (T - P) - np.arange(T)[None, :]
    put("causal", np.where(delta >= 0, 0.0, NEG))
    end = np.arange(N_CMP) * CMP_STRIDE + CMP_LEN - 1
    t = p[:, None, None] + P * np.arange(TT)[None, :, None]
    put("cmp_mask", np.where(end[None, None, :] <= t, 0.0, NEG).reshape(P, -1))
    return np.concatenate(parts, 1)


CONSTS = _consts()


def _alibi():
    delta = np.arange(P)[:, None] + (T - P) - np.arange(T)[None, :]
    n = ((delta >= 0) & (delta <= 128)) * 1.0
    n += (delta >= 0) & (delta % 4 == 0)
    n += (delta >= 0) & (delta % 16 == 0)
    slopes = np.exp2(-8.0 * np.arange(1, 17) / 16)
    b = -slopes[:, None, None] * delta[None] + np.log(np.maximum(n, 1))[None]
    return (np.where(n[None] > 0, b, NEG) / SCALE_A).astype(np.float32)


GAIN = dict(norm_g=0, final_g=8, b_merge=16, conv_w=32, norm1=56, q=64, kc=65, ks=66, kw=67,
            cq=68, ckv=70, mq=71, mk=72, out=73, norm2=81, pos=89)
N_GAIN = 121


class Job:

    def __init__(self, m, i=0, per=RING):
        assert per % RING == 0
        self.n = i * per + m
        self.turn = i * (per // RING) + m // RING
        self.slot = m % RING
        self.parts = (m, i, per)

    def ahead(self, by=AHEAD):
        m, i, per = self.parts
        return Job(m + by, i, per)


def two_layer_kernel(nc, tiles, x_t, consts, gains, alibi, positions, cmp_w1, cmp_w2, w_uq, w_ukv,
                     sub_keys, gates_dram, acts_dram, out):
    ctx = ExitStack()
    with ctx:
        def sem(name):
            return ctx.enter_context(nc.semaphore(name))

        KB = 1024
        base = nc.sbuf_base if isinstance(nc.sbuf_base, int) else 0
        base = (base + 63) // 64 * 64

        def at(name, place, shape, dt=F32):
            return nc.alloc_sbuf_tensor_at(name, shape, dt, offset=base + int(place))

        ROW = 2 * KB
        raw = at("raw", 0, [P, RING, D])
        whi = at("whi", 16 * KB, [P, RING, D], F32R)
        wlo = at("wlo", 32 * KB, [P, RING, D], F32R)
        res = at("res", 48 * KB, [P, KC, T])
        act_hi = at("act_hi", 64 * KB, [P, KC, T], F32R)
        act_lo = at("act_lo", 80 * KB, [P, KC, T], F32R)
        place = 96 * KB
        con = at("con", place, [P, CONSTS.shape[1]])
        place = (place + CONSTS.shape[1] * 4 + 31) // 32 * 32
        gain = at("gain", place, [P, N_GAIN])
        place += N_GAIN * 4
        place = (place + 31) // 32 * 32

        def cols(name, n, dt=F32):
            nonlocal place
            t = at(name, place, [P, n], dt)
            place += (n * 4 + 31) // 32 * 32
            return t

        half_b = cols("half_b", 16)
        neg_half = cols("neg_half", 64)
        ms = cols("ms", 64)
        rstd = cols("rstd", 64)
        mx = cols("mx", 24)
        negmax = cols("negmax", 24)
        waited = cols("waited", 2)
        den = cols("den", 24)
        inv = cols("inv", 24)
        factor = cols("factor", 24)
        rq_a = cols("rq_a", 32)
        rq_b = cols("rq_b", 32)
        gate = cols("gate", TT * 24)
        prod = at("prod", place, [P, T + 2])
        m1 = at("m1", place, [P, T])
        cprob = cols("cprob", 2 * P)
        kcr = cols("kcr", N_CMP)
        kc_sq = cols("kc_sq", N_CMP)
        kc_tmp = cols("kc_tmp", N_CMP)
        vcs = cols("vcs", P)
        w2s = at("w2s", place, [P, 2, 2, 64])
        place += 1024
        R = (place + 31) // 32 * 32

        yc_hi = at("yc_hi", R, [P, KC, T], F32R)
        yc_lo = at("yc_lo", R + 16 * KB, [P, KC, T], F32R)
        ya_hi = at("ya_hi", R + 32 * KB, [P, KC, T], F32R)
        ya_lo = at("ya_lo", R + 48 * KB, [P, KC, T], F32R)
        A0 = R + 64 * KB
        qT = at("qT", A0, [P, T])
        kT = at("kT", A0 + ROW, [P, T])
        vT = at("vT", A0 + 2 * ROW, [P, T])
        vtok = at("vtok", A0 + 3 * ROW, [P, TT, P])
        prob = at("prob", A0 + 4 * ROW, [P, 2, QALL])
        probT = at("probT", A0 + 18 * KB, [P, TT, T])
        bias = at("bias", A0 + 26 * KB, [P, 2, T])
        xc = at("xc", A0 + 30 * KB, [P, T])
        conv = at("conv", A0 + 32 * KB, [P, T])
        sgate = at("sgate", A0 + 34 * KB, [P, T])
        mg_hi = at("mg_hi", A0, [P, KC, T], F32R)
        mg_lo = at("mg_lo", A0 + 16 * KB, [P, KC, T], F32R)
        tg = at("tg", A0 + 32 * KB, [P, 2, T])
        sq = at("sq", R, [P, KC, T])
        sq2 = at("sq2", R + 16 * KB, [P, KC, T])
        hg = at("hg", R + 32 * KB, [P, KC, T])
        xn = at("xn", R + 52 * KB, [P, 2, T])
        diag = at("diag", R + 86 * KB, [P, 8, P])
        mean = at("mean", R + 48 * KB, [P, T])
        mend = at("mend", R + 50 * KB, [P, T])
        rrow = at("rrow", R + 86 * KB, [P, 2, T])
        w1s = at("w1s", R, [P, 2, CMP_LEN // 2, 256])
        cqr = at("cqr", R + 32 * KB, [P, 2, T])
        ckvr = at("ckvr", R + 36 * KB, [P, T])
        krg = at("krg", R + 38 * KB, [P, T])
        kvc = at("kvc", R + 52 * KB, [P, 2, 2, T])
        ksw = at("ksw", R + 44 * KB, [P, 2, T])
        vsw = at("vsw", R + 48 * KB, [P, 2, T])
        qh = at("qh", R + 52 * KB, [P, 4, T])
        sqq = at("sqq", R + 60 * KB, [P, 4, T])
        sqk = at("sqk", R + 68 * KB, [P, 2, T])
        sqc = at("sqc", R + 72 * KB, [P, 3, T])
        rope = at("rope", R + 78 * KB, [P, 4, T])
        pos_i = at("pos_i", R + 97.75 * KB, [P, T], I32)
        pos_f = at("pos_f", R + 99.75 * KB, [P, T])
        turns = at("turns", R + 94 * KB, [P, T])
        angle = at("angle", R + 90 * KB, [P, 2, T])
        angle_abs = at("angle_abs", R + 48 * KB, [P, 2, T])
        kp = at("kp", R + 90 * KB, [P, 2, CMP_LEN // 2, 2 * N_CMP])
        hid = at("hid", R + 72 * KB, [P, 4, 2 * N_CMP])
        hid_rows = at("hid_rows", R + 74 * KB, [P, 2, 256])
        vtb = at("vtb", R + 97.75 * KB, [P, 2, TT, P])
        rtmp = at("rtmp", R + 68 * KB, [P, 2, T])
        wuq = at("wuq", R, [P, 2, 8 * 96])
        wukv = at("wukv", R + 6 * KB, [P, 2, 8, 64])
        mv = at("mv", R + 10 * KB, [P, TT, T])
        sqb = at("sqb", R + 18 * KB, [P, 2, T])
        mq = at("mq", 64 * KB, [P, 8, T])
        mk = at("mk", 80 * KB, [P, 8, T])
        prob3 = at("prob3", R + 18 * KB, [P, 3, QALL])
        probT2 = at("probT2", R + 60 * KB, [P, 2, TT, T])
        cprobT = at("cprobT", R + 76 * KB, [P, T])
        o_a = at("o_a", R + 33 * KB, [P, 4, T])
        o_b = at("o_b", R + 90 * KB, [P, 4, T])
        sqo = at("sqo", R + 78 * KB, [P, 4, T])
        pq = at("pq", R + 32 * KB, [P, 16, T])
        sqf = at("sqf", R + 64 * KB, [P, 16, T])
        subk = at("subk", R + 16 * KB, [P, 16, P])
        ssb = at("ssb", R, [P, 16, P])
        srep = at("srep", R + 8 * KB, [P, 16, P])
        cand = at("cand", R + 24 * KB, [P, 8, 16, 16])
        crep = at("crep", R + 64 * KB, [P, 8, 16, 16])
        eq = at("eq", R + 72 * KB, [P, 8, 16, 16])
        v16 = at("v16", R + 80 * KB, [P, 16, 16])
        i16 = at("i16", R + 81 * KB, [P, 16, 16], U32)
        i16f = at("i16f", R + 82 * KB, [P, 16, 16])
        vals = at("vals", R + 83 * KB, [P, 8, 16])
        vci = at("vci", R + 83.5 * KB, [P, 8, 16], U32)
        ca = at("ca", R + 84 * KB, [P, 2, 8, 16], U32)
        caf = at("caf", R + 85 * KB, [P, 2, 8, 16])
        sel = at("sel", R + 86 * KB, [P, 3, 8, 16])
        selT = at("selT", R + 87.5 * KB, [P, 3, T])
        vsum = at("vsum", R + 93.5 * KB, [P, 2, 8])
        hot = at("hot", R + 64 * KB, [P, 16, 2, P])
        stage = at("stage", R, [P, 2, P, 64])
        wg = at("wg", R, [P, 2, TT * 2, GJ, 64])
        h_hi = at("h_hi", R + 32 * KB, [P, 2, GJ, T], F32R)
        h_lo = at("h_lo", R + 64 * KB, [P, 2, GJ, T], F32R)
        hf = at("hf", R + 64 * KB, [P, 2, GJ, T])
        gelu = at("gelu", R + 93.75 * KB, [P, 4, T])

        bank = [ctx.enter_context(nc.psum_tensor(f"bank{i}", [P, T], F32)) for i in range(8)]

        def k(name, rows=slice(0, P), cols=None):
            a, b = CONST[name]
            return con[rows, a:b] if cols is None else con[rows, a + cols.start:a + cols.stop]

        def g(name, j=0, rows=slice(0, P)):
            a = GAIN[name] + j
            return gain[rows, a:a + 1]

        ident, ones = k("ident"), k("ones")

        const_landed, x_landed = sem("const_landed"), [sem(f"x_landed{i}") for i in range(4)]
        raw_landed = [sem(f"raw_landed{i}") for i in range(RING)]
        hi_made = sem("hi_made")
        lo_made = sem("lo_made")
        job_done = sem("job_done")
        taken = [sem(f"taken{i}") for i in range(RING)]
        setup_done, halfb_made = sem("setup_done"), sem("halfb_made")

        sq_made, ssq_made, ms_made, rstd_made = (sem(s) for s in ("sq_made", "ssq_made", "ms_made", "rstd_made"))
        sums_made, roots_made, rrow_made = (sem(s) for s in ("sums_made", "roots_made", "rrow_made"))
        diag_made, row_made, normed, hi_act, lo_act = (sem(s) for s in ("diag_made", "row_made", "normed", "hi_act", "lo_act"))

        v_turned, vtok_copied = sem("v_turned"), sem("vtok_copied")
        bias_landed = [sem("bias_landed0"), sem("bias_landed1")]
        scores_made, scores_masked, negmax_made = sem("scores_made"), sem("scores_masked"), sem("negmax_made")
        probs_exp, inv_made, probs_scaled = sem("probs_exp"), sem("inv_made"), sem("probs_scaled")
        probs_turned, turned_copied, heads_mixed = sem("probs_turned"), sem("turned_copied"), sem("heads_mixed")
        conv_step, zc_tanh, za_tanh = sem("conv_step"), sem("zc_tanh"), sem("za_tanh")
        yc_made, ya_made, ychi_made, yahi_made, y_split = (sem(s) for s in ("yc_made", "ya_made", "ychi_made", "yahi_made", "y_split"))

        merged, mghi_made, mg_split = sem("merged"), sem("mghi_made"), sem("mg_split")
        hg_made = sem("hg_made")
        acts_stored = [sem(f"acts_stored{i}") for i in range(RING)]
        stored = sem("stored")
        named = {}

        def S(name):
            if name not in named:
                named[name] = sem(name)
            return named[name]

        def make_hi(act, j):
            act.wait_ge(raw_landed[j.slot], (j.turn + 1) * 16)
            act.wait_ge(job_done, j.n + 1)
            act.activation(whi[:, j.slot, :], raw[:, j.slot, :], ACT.Copy).then_inc(hi_made, 1)

        def make_lo(dve, j):
            dve.wait_ge(hi_made, j.n + 1)
            dve.tensor_tensor(wlo[:, j.slot, :], raw[:, j.slot, :], whi[:, j.slot, :].bitcast(F32),
                              ALU.subtract).then_inc(lo_made, 1)

        def multiply(pe, j, hi, lo, before=None, chunks=range(KC)):
            if chunks[0] == 0:
                pe.wait_ge(lo_made, j.n + 1 + RING)
                pe.wait_ge(taken[j.slot], j.turn + 1)
            for kc in chunks:
                w = slice(kc * P, (kc + 1) * P)
                wh, wl = whi[:, j.slot, w], wlo[:, j.slot, w]
                if before:
                    before(kc)
                pe.matmul(bank[j.slot][:, :], wh, hi[:, kc, :], start=(kc == 0), stop=False)
                pe.matmul(bank[j.slot][:, :], wh, lo[:, kc, :], start=False, stop=False)
                last = pe.matmul(bank[j.slot][:, :], wl, hi[:, kc, :], start=False, stop=(kc == KC - 1))
            if chunks[-1] == KC - 1:
                last.then_inc(job_done, 1)

        def result_of(eng, j):
            eng.wait_ge(job_done, j.n + 1 + RING)

        def was_taken(eng, j):
            eng.wait_ge(taken[j.slot], j.turn + 2)

        def turn(pe, out, x, unit):
            return pe.transpose(out, x, unit)

        PASSES = []
        for c in range(4):
            for grp in range(2):
                rows = slice(64 * grp, 64 * grp + 64)
                for b in range(2):
                    PASSES.append(dict(
                        q=qh[rows, c, :], k=ksw[rows, b, :], v=[vtb[:, b, kb, rows] for kb in range(TT)],
                        rows=rows, rq=(rq_a, 2 * c + grp), gate=(c + 4 * grp, 1 + b), first=(b == 0), last=False,
                        head=2 * c + grp if b else None, chunk=c, group=grp, opens=(b == 0 and grp == 0),
                        closes=(b == 1 and grp == 1)))
        for h in range(8):
            rows = slice(64 * (h % 2), 64 * (h % 2) + 64)
            PASSES.append(dict(
                q=mq[0:96, h, :], k=mk[0:96, h, :], v=[mv[:, kb, 64 * h:64 * h + 64] for kb in range(TT)],
                rows=rows, rq=(rq_b, h), gate=None, first=True, last=True, head=None, chunk=4 + h // 2,
                opens=(h % 2 == 0), closes=(h % 2 == 1)))

        def rq_col(x, tt):
            t, h = x["rq"]
            return t[:, tt * 8 + h:tt * 8 + h + 1]

        def pass_scores(pe, p):
            x = PASSES[p]
            if p:
                pe.wait_ge(S("p_masked"), 4 * p)
                heads = sum(y["head"] is not None for y in PASSES[:p])
                if heads:
                    pe.wait_ge(S("c_masked"), 4 * heads)
            for qt in range(TT):
                b, col = QBANK[qt]
                pe.matmul(bank[b][:, col:col + QW[qt]], x["q"][:, qt * P:(qt + 1) * P], x["k"][:, 0:QW[qt]],
                          start=True, stop=True).then_inc(S("p_scores"), 1)
            if x["head"] is not None:
                for qt in range(TT):
                    last = pe.matmul(bank[0][:, 384 + 32 * qt:384 + 32 * qt + N_CMP],
                                     x["q"][:, qt * P:(qt + 1) * P], kcr[x["rows"], :], start=True, stop=True)
                last.then_inc(S("c_scores"), 1)

        def pass_turn(pe, p):
            x = PASSES[p]
            pe.wait_ge(S("p_scaled"), 4 * p + 4)
            if p:
                pe.wait_ge(S("p_copied"), 4 * p)
            for qt in range(TT):
                b, col = QBANK[qt]
                for kb in range(qt + 1):
                    last = turn(pe, bank[3 + b][:, col + kb * P:col + (kb + 1) * P],
                                        prob3[:, p % 3, QOFF[qt] + kb * P:QOFF[qt] + (kb + 1) * P], ident)
                last.then_inc(S("p_turned"), 1)
            if x["head"] is not None:
                h = x["head"]
                pe.wait_ge(S("c_scaled"), 4 * h + 4)
                if h:
                    pe.wait_ge(S("c_copied"), h)
                for qt in range(TT):
                    last = turn(pe, bank[7][0:N_CMP, qt * P:(qt + 1) * P],
                                        cprob[:, P * (h % 2) + 32 * qt:P * (h % 2) + 32 * qt + N_CMP], ident)
                last.then_inc(S("c_turned"), 1)

        def pass_mix(pe, p):
            x = PASSES[p]
            rows = x["rows"]
            pe.wait_ge(S("p_copied"), 4 * p + 4)
            if x["opens"] and x["chunk"]:
                pe.wait_ge(S("o_taken"), x["chunk"])
            for kb in range(TT):
                last = pe.matmul(bank[6][rows, kb * P:T], x["v"][kb], probT2[:, p % 2, kb, kb * P:T],
                                 start=(x["first"] and kb == 0), stop=(x["last"] and kb == TT - 1))
            if x["head"] is not None:
                pe.wait_ge(S("c_copied"), x["head"] + 1)
                grp = x["group"]
                last = pe.matmul(bank[6][rows, :], vcs[0:N_CMP, 64 * grp:64 * grp + 64], cprobT[0:N_CMP, :],
                                 start=False, stop=True)
            last.then_inc(S("p_mixed"), 1)

        def turn_selection(pe, tt):
            pe.wait_ge(S("selected"), tt + 1)
            if tt:
                pe.wait_ge(S("sel_copied"), tt)
            for n in range(3):
                last = turn(pe, bank[4][:, n * P:(n + 1) * P], sel[:, n, :, :].rearrange("p h k -> p (h k)"), ident)
            last.then_inc(S("sel_turned"), 1)

        block = ctx.enter_context(nc.Block())

        @block.sync
        def _(sp):
            def load(j):
                sp.wait_ge(lo_made, j.n + 1)
                sp.dma_start(raw[:, j.slot, :], tiles[j.n, :, :]).then_inc(raw_landed[j.slot], 16)

            with sp.Fori(0, (J_U + 8) // RING) as i:
                for m in range(RING):
                    load(Job(m, i))
            for m in range((J_U + 8) // RING * RING, J_U + 8):
                load(Job(m))
            with sp.Fori(0, P // RING) as i:
                for m in range(RING):
                    load(Job(J_U + 8 + m, i))
                    j = Job(J_U + m, i)
                    was_taken(sp, j)
                    sp.dma_start(acts_dram[bass.ds(i * RING + m, 1), :, :], gelu[:, m, :])\
                        .then_inc(acts_stored[m], 16)
            with sp.Fori(0, (JOBS - J_V - 8) // RING) as i:
                for m in range(RING):
                    load(Job(J_V + 8 + m, i))

        @block.gpsimd
        def _(pool):
            pool.dma_start(con[:, :], consts).then_inc(const_landed, 16)
            pool.dma_start(gain[:, :], gains).then_inc(const_landed, 16)
            pool.memset(neg_half[:, :], -0.5).then_inc(setup_done, 1)
            pool.memset(prod[:, 0:2], 0.0).then_inc(setup_done, 1)
            pool.wait_ge(setup_done, 2)
            with pool.Fori(0, KC) as c:
                for e in range(2):
                    pool.wait_ge(scores_masked, c * 8 + 1)
                    pool.dma_start(bias[:, e, :], alibi[bass.ds(c * 2 + e, 1), :, :]).then_inc(bias_landed[e], 16)
            def power(n_ms, n, rows=P, view=None):
                pool.wait_ge(ms_made, n_ms)
                view = view or (lambda t: t[0:rows, 0:n])
                pool.tensor_tensor(view(rstd), view(ms), view(neg_half), ALU.pow).then_inc(rstd_made, 1)

            def add_up(squares, before, chunk):
                pool.wait_ge(sq_made, before)
                if chunk > 1:
                    pool.wait_ge(S("sq_added"), pool_added[0])
                pool.tensor_tensor(squares[:, 0, :], squares[:, 0, :], squares[:, chunk, :], ALU.add)\
                    .then_inc(S("sq_added"), 1)
                pool_added[0] += 1

            pool_added = [0]
            for c in range(1, 6):
                add_up(sq, KC + 2 * c + 2, c)
                add_up(sq2, KC + 2 * c + 2, c)
            pool.wait_ge(job_done, J_C + 1 + RING)
            pool.dma_start(pos_i[:, :], positions.broadcast_to((P, T))).then_inc(S("pos_landed"), 16)
            pool.dma_start(w2s[:, :, :, :], cmp_w2).then_inc(S("w2_landed"), 16)
            pool.wait_ge(job_done, J_D + 1 + RING)
            pool.dma_start(w1s[:, :, :, :], cmp_w1).then_inc(S("w1_landed"), 16)
            for grp in range(2):
                was_taken(pool, Job(J_D + 4 + grp))
            pool.dma_start(kvc[64:128, 0, :, 0:T - 1], kvc[0:64, 0, :, 1:T]).then_inc(S("shifted"), 16)
            pool.dma_start(kvc[0:64, 1, :, 0:T - 1], kvc[64:128, 1, :, 1:T]).then_inc(S("shifted"), 16)
            power(3, 14, view=lambda t: t[:, 0:64].rearrange("p (t n) -> p t n", t=TT)[:, :, 0:14])
            pool.wait_ge(S("hidden_made"), 2)
            pool.dma_start(wuq[:, :, :], w_uq).then_inc(S("wuq_landed"), 16)
            pool.dma_start(wukv[:, :, :, :], w_ukv).then_inc(S("wukv_landed"), 16)
            power(4, 2, rows=N_CMP)
            for n in range(2):
                power(5 + n, 8, view=lambda t: t[:, 0:64].rearrange("p (t n) -> p t n", t=TT)[:, :, 8 * n:8 * n + 8])
            for c in range(1, 6):
                add_up(sq, 3 * KC + c + 1, c)
            pool.wait_ge(job_done, J_F + 1 + RING)
            pool.dma_start(subk[:, :, :], sub_keys).then_inc(S("subk_landed"), 16)
            power(7, 32)
            def load_gates(grp, slot):
                pool.dma_start(wg[:, slot, :, :, :].rearrange("p b j t -> p b (j t)"),
                               gates_dram[:, :, bass.ds(grp * GJ, GJ), :].rearrange("b p j t -> p b (j t)"))\
                    .then_inc(S(f"wg_landed{slot}"), 16)

            def load_acts(grp, slot):
                pool.dma_start(hf[:, slot, :, :], acts_dram[bass.ds(grp * GJ, GJ), :, :].rearrange("j p t -> p j t"))\
                    .then_inc(S(f"hf_landed{slot}"), 16)

            pool.wait_ge(S("gates_stored0"), 16 * 5)
            pool.wait_ge(S("gates_stored1"), 16 * 5)
            load_gates(0, 0)
            load_gates(1, 1)
            for m in range(RING):
                pool.wait_ge(acts_stored[m], 16 * 3)
            load_acts(0, 0)
            for m in range(RING):
                pool.wait_ge(acts_stored[m], 16 * (P // RING + 1 if m < 2 else 5))
            load_acts(1, 1)
            for m in range(2, RING):
                pool.wait_ge(acts_stored[m], 16 * (P // RING + 1))
            with pool.Fori(0, GROUPS // 2 - 1) as g2:
                for slot in range(2):
                    pool.wait_ge(S("gated"), g2 * 16 + 8 * (slot + 1))
                    load_gates(g2 * 2 + (2 + slot), slot)
                    result_of(pool, Job(J_V + GJ * slot + GJ - 1, g2, 2 * GJ))
                    load_acts(g2 * 2 + (2 + slot), slot)

        @block.tensor
        def _(pe):
            def add_squares(b, squares, first=False, last=False):
                return pe.matmul(bank[b][:, :], ones, squares, start=first, stop=last)

            def chunk_normed(before):
                return lambda kc: pe.wait_ge(lo_act, before + kc + 1)

            pe.sem_inc(job_done, RING)
            pe.wait_ge(const_landed, 32)
            for kc in range(KC):
                pe.wait_ge(sq_made, kc + 1)
                last = add_squares(4, sq[:, kc, :], kc == 0, kc == KC - 1)
            last.then_inc(sums_made, 1)

            def scores(c, e):
                rows = slice(64 * e, 64 * e + 64)
                for qt in range(TT):
                    b, col = QBANK[qt]
                    pe.matmul(bank[4 + b][:, col:col + QW[qt]], qT[rows, qt * P:(qt + 1) * P],
                              kT[rows, 0:QW[qt]], start=True, stop=True).then_inc(scores_made, 1)

            def turn_probs(e):
                for qt in range(TT):
                    b, col = QBANK[qt]
                    for kb in range(qt + 1):
                        last = turn(pe, bank[4 + b][:, col + kb * P:col + (kb + 1) * P],
                                            prob[:, e, QOFF[qt] + kb * P:QOFF[qt] + (kb + 1) * P], ident)
                    last.then_inc(probs_turned, 1)

            def mix_values(e):
                rows = slice(64 * e, 64 * e + 64)
                for kb in range(TT):
                    last = pe.matmul(bank[7][rows, kb * P:T], vtok[:, kb, rows], probT[:, kb, kb * P:T],
                                     start=(kb == 0), stop=(kb == TT - 1))
                last.then_inc(heads_mixed, 1)

            with pe.Fori(0, KC) as c:
                def job(m):
                    multiply(pe, Job(m, c, 8), act_hi, act_lo, chunk_normed(0) if m == 0 else None)

                job(0)
                job(1)
                job(2)
                was_taken(pe, Job(0, c, 8))
                was_taken(pe, Job(1, c, 8))
                pe.wait_ge(turned_copied, c * 8 + 1)
                scores(c, 0)
                job(3)
                was_taken(pe, Job(2, c, 8))
                pe.wait_ge(ya_made, c + 1)
                for tt in range(TT):
                    last = turn(pe, bank[7][:, tt * P:(tt + 1) * P], vT[:, tt * P:(tt + 1) * P], ident)
                last.then_inc(v_turned, 1)
                pe.wait_ge(scores_masked, c * 8 + 5)
                scores(c, 1)
                job(4)
                pe.wait_ge(probs_scaled, c * 8 + 4)
                pe.wait_ge(scores_masked, c * 8 + 9)
                turn_probs(0)
                job(5)
                pe.wait_ge(turned_copied, c * 8 + 5)
                pe.wait_ge(vtok_copied, c + 1)
                mix_values(0)
                pe.wait_ge(probs_scaled, c * 8 + 8)
                turn_probs(1)
                job(6)
                pe.wait_ge(turned_copied, c * 8 + 9)
                mix_values(1)
                job(7)

            with pe.Fori(0, 4) as i:
                for m in range(8):
                    if m == 1:
                        pe.wait_ge(y_split, 2 * KC)
                    hi, lo = ((act_hi, act_lo), (yc_hi, yc_lo), (act_hi, act_lo), (ya_hi, ya_lo))[m % 4]
                    multiply(pe, Job(J_B + m, i, 8), hi, lo)

            for m in range(8):
                multiply(pe, Job(J_C + m), mg_hi, mg_lo,
                         (lambda kc: pe.wait_ge(mg_split, kc + 2)) if m == 0 else None)
            def first_of_d(kc):
                if kc == 6:
                    pe.wait_ge(S("sq_added"), 10)
                    for chunk in (0, 6, 7):
                        pe.wait_ge(sq_made, KC + 2 * chunk + 2)
                        s1 = add_squares(4, sq[:, chunk, :], chunk == 0, chunk == 7)
                        s2 = add_squares(5, sq2[:, chunk, :], chunk == 0, chunk == 7)
                    s1.then_inc(sums_made, 1)
                    s2.then_inc(sums_made, 1)
                pe.wait_ge(lo_act, KC + kc + 1)

            for m in range(14):
                multiply(pe, Job(J_D + m), act_hi, act_lo, first_of_d if m == 0 else None)

            for b in range(2):
                was_taken(pe, Job(J_D + 8 + b))
                for tt in range(TT):
                    last = turn(pe, bank[4 + b][:, tt * P:(tt + 1) * P], vsw[:, b, tt * P:(tt + 1) * P], ident)
                last.then_inc(S("vb_turned"), 1)
            pe.wait_ge(S("d_finished"), 4)
            for tt in range(TT):
                last = turn(pe, bank[6][:, tt * 24:(tt + 1) * 24], krg[0:24, tt * P:(tt + 1) * P],
                                    k("ident", slice(0, 24), slice(0, 24)))
            last.then_inc(S("gates_turned"), 1)
            pe.wait_ge(S("d_finished"), 14)
            halves = k("halves")
            for tt in range(TT):
                t = slice(tt * P, (tt + 1) * P)
                for c in range(4):
                    pe.matmul(bank[7][:, tt * 16 + 2 * c:tt * 16 + 2 * c + 2], sqq[:, c, t], halves,
                              start=True, stop=True)
                for c in range(2):
                    pe.matmul(bank[7][:, tt * 16 + 8 + 2 * c:tt * 16 + 10 + 2 * c], sqk[:, c, t], halves,
                              start=True, stop=True)
                for c in range(2):
                    pe.matmul(bank[7][:, tt * 16 + 12:tt * 16 + 13], sqc[:, c, t], ones[:, 0:1],
                              start=(c == 0), stop=(c == 1))
                last = pe.matmul(bank[7][:, tt * 16 + 13:tt * 16 + 14], sqc[:, 2, t], ones[:, 0:1],
                                 start=True, stop=True)
            last.then_inc(ssq_made, 1)
            pe.wait_ge(S("kp_made"), 4)
            pe.wait_ge(S("w1_landed"), 16)
            for kv in range(2):
                for l in range(CMP_LEN // 2):
                    last = pe.matmul(bank[kv][0:2 * N_CMP, 0:256], kp[:, kv, l, :], w1s[:, kv, l, :],
                                     start=(l == 0), stop=(l == CMP_LEN // 2 - 1))
                last.then_inc(S("hidden_made"), 1)

            def row_unit(u, b, rows):
                pe.wait_ge(diag_made, 4 * (u + 1) + (2 if u >= 6 else 0))
                n = rows.stop - rows.start
                for tt in range(TT):
                    last = pe.matmul(bank[b][rows, tt * P:(tt + 1) * P], ones[:, 0:n],
                                     diag[:, 4 * (u % 2) + tt, :], start=True, stop=True)
                last.then_inc(row_made, 1)

            def rotate(r_, rows, w, x):
                if r_ >= 2:
                    pe.wait_ge(S("rot_used"), r_ - 1)
                pe.matmul(bank[4 + r_ % 2][rows, :], w, x, start=True, stop=True).then_inc(S("rot_made"), 1)

            all_, low, high = slice(0, P), slice(0, 64), slice(64, P)
            was_taken(pe, Job(J_D + 12))
            pe.wait_ge(S("gates_made"), 1)
            row_unit(0, 6, all_)
            row_unit(1, 2, all_)
            pe.wait_ge(S("vtb_copied"), 2)
            for c in range(2):
                rotate(c, all_, k("rot64"), qh[:, c, :])
            for kv in range(2):
                pe.wait_ge(S("hid_made"), kv + 1)
                for half in range(2):
                    last = turn(pe, bank[kv][:, 256 + 64 * half:256 + 64 * half + 2 * N_CMP],
                                        hid_rows[0:2 * N_CMP, kv, half * P:(half + 1) * P],
                                        k("ident", slice(0, 2 * N_CMP), slice(0, 2 * N_CMP)))
                last.then_inc(S("hid_turned"), 1)
            pe.wait_ge(S("hid_copied"), 2)
            pe.wait_ge(S("w2_landed"), 16)
            for grp in range(2):
                for half in range(2):
                    pe.matmul(bank[3][64 * grp:64 * grp + 64, 0:N_CMP], w2s[:, 0, half, :],
                              hid[:, half, grp * N_CMP:(grp + 1) * N_CMP], start=(half == 0), stop=(half == 1))
            for grp in range(2):
                for half in range(2):
                    last = pe.matmul(bank[3][0:N_CMP, 64 + 64 * grp:128 + 64 * grp],
                                     hid[:, 2 + half, grp * N_CMP:(grp + 1) * N_CMP], w2s[:, 1, half, :],
                                     start=(half == 0), stop=(half == 1))
            last.then_inc(S("kc_made"), 1)
            pe.wait_ge(S("latents"), 2)
            row_unit(2, 6, low)
            row_unit(3, 6, high)
            pe.wait_ge(S("latents"), 3)
            row_unit(4, 2, low)
            row_unit(5, 2, high)
            for c in range(2, 4):
                rotate(c, all_, k("rot64"), qh[:, c, :])
            pe.wait_ge(S("kc_copied"), 3)
            pe.matmul(bank[7][0:N_CMP, 96:98], kc_sq[:, :], halves, start=True, stop=True).then_inc(ssq_made, 1)
            pe.wait_ge(S("kw_normed"), 2)
            rotate(4, all_, k("rot64"), ksw[:, 0, :])
            rotate(5, all_, k("rot64"), ksw[:, 1, :])
            pe.wait_ge(diag_made, 26)
            for grp in range(2):
                last = pe.matmul(bank[3][64 * grp:64 * grp + 64, 256:256 + N_CMP], ones[0:N_CMP, 0:64],
                                 diag[0:N_CMP, grp, 0:N_CMP], start=True, stop=True)
            last.then_inc(row_made, 1)
            pe.wait_ge(S("kc_normed"), 1)
            pe.matmul(bank[3][:, 320:320 + N_CMP], k("rot64"), kcr[:, :], start=True, stop=True).then_inc(S("kc_rot"), 1)

            pe.wait_ge(S("wuq_landed"), 16)
            pe.wait_ge(S("wukv_landed"), 16)

            def product(p):
                b = bank[p % 2]
                if p >= 2:
                    pe.wait_ge(S("prod_taken"), p - 1)
                if p < 8:
                    for c in range(2):
                        last = pe.matmul(b[0:96, :], wuq[:, c, 96 * p:96 * p + 96], cqr[:, c, :],
                                         start=(c == 0), stop=(c == 1))
                elif p < 16:
                    last = pe.matmul(b[0:64, :], wukv[:, 0, p - 8, :], ckvr[:, :], start=True, stop=True)
                else:
                    tt = p - 16
                    last = pe.matmul(b[:, :], ckvr[:, tt * P:(tt + 1) * P],
                                     wukv[:, 1, :, :].rearrange("p h d -> p (h d)"), start=True, stop=True)
                last.then_inc(S("prod_made"), 1)

            def product_sums(p):
                pe.wait_ge(S("prod_taken"), p + 1)
                for tt in range(TT):
                    last = pe.matmul(bank[6 + p // 8][:, 128 + tt * 16 + p:129 + tt * 16 + p],
                                     sqb[0:96, p % 2, tt * P:(tt + 1) * P], ones[0:96, 0:1], start=True, stop=True)
                last.then_inc(S("mla_sums_made"), 1)

            rot_rows = slice(64, 96)
            for p in range(20):
                product(p)
                if 1 <= p <= 16:
                    product_sums(p - 1)
                if 2 <= p < 10:
                    rotate(6 + p - 2, rot_rows, k("rot32", rot_rows), mq[rot_rows, p - 2, :])
                if p == 12:
                    pe.wait_ge(S("kr_scaled"), 1)
                    rotate(14, rot_rows, k("rot32", rot_rows), krg[rot_rows, :])
            pe.wait_ge(S("roped"), 6)
            pe.wait_ge(S("kc_roped"), 1)
            pe.wait_ge(S("prod_taken"), 20)
            pass_scores(pe, 0)
            pe.wait_ge(S("rot_used"), 15)
            for h in range(8):
                if h >= 2:
                    pe.wait_ge(S("mk_normed"), h - 1)
                row_unit(6 + h, 4 + h % 2, slice(0, 96))

            pe.wait_ge(S("roped"), 15)
            pe.wait_ge(S("mk_normed"), 8)
            pass_scores(pe, 1)
            for p in range(len(PASSES)):
                if p + 2 < len(PASSES):
                    pass_scores(pe, p + 2)
                pass_turn(pe, p)
                if p:
                    pass_mix(pe, p - 1)
                if p == 18:
                    pe.wait_ge(S("o_squared"), 4)
                    for c in range(4):
                        last = add_squares(7, sqo[:, c, :], c == 0, c == 3)
                    last.then_inc(sums_made, 1)
            pe.wait_ge(S("means_made"), 4)
            for c in range(3):
                pe.wait_ge(S("o_squared"), 5 + c)
                add_squares(7, sqo[:, c, :], c == 0)
            pe.wait_ge(S("p_masked"), 4 * len(PASSES))
            for m in range(4):
                multiply(pe, Job(J_E + m), act_hi, act_lo, chunk_normed(2 * KC), range(4))
                if m == 0:
                    pass_mix(pe, len(PASSES) - 1)
                    pe.wait_ge(S("o_squared"), 8)
                    add_squares(7, sqo[:, 3, :], last=True).then_inc(sums_made, 1)
            for m in range(4):
                multiply(pe, Job(J_E + m), act_hi, act_lo, chunk_normed(2 * KC), range(4, KC))
            for m in range(4, KC):
                multiply(pe, Job(J_E + m), act_hi, act_lo)
            for m, chunk in enumerate((0, 6, 7)):
                pe.wait_ge(*((S("sq_added"), 15) if m == 0 else (sq_made, 3 * KC + chunk + 1)))
                last = add_squares(4, sq[:, chunk, :], m == 0, m == 2)
            last.then_inc(sums_made, 1)
            for m in range(16):
                multiply(pe, Job(J_F + m), act_hi, act_lo, chunk_normed(3 * KC) if m == 0 else None)
            def u_job(n):
                multiply(pe, Job(J_U + n), act_hi, act_lo)

            u_job(0)
            pe.wait_ge(S("halves_added"), 8)
            for h in range(8):
                for tt in range(TT):
                    last = pe.matmul(bank[7][:, tt * 8 + h:tt * 8 + h + 1],
                                     sqf[:, 2 * h, tt * P:(tt + 1) * P], ones[:, 0:1], start=True, stop=True)
            last.then_inc(ssq_made, 1)
            u_job(1)

            def routes(tt):
                for hc in range(16):
                    last = pe.matmul(bank[4 + hc // 4][:, (hc % 4) * P:(hc % 4 + 1) * P],
                                     pq[:, hc, tt * P:(tt + 1) * P], subk[:, hc, :], start=True, stop=True)
                last.then_inc(S("routes_made"), 1)

            pe.wait_ge(S("subk_landed"), 16)
            pe.wait_ge(ms_made, 7)
            routes(0)
            u_job(2)
            u_job(3)
            for tt in range(TT):
                for m in range(U_TILE):
                    u_job(U_FIRST + U_TILE * tt + m)
                    if m == 2:
                        pe.wait_ge(S("routes_scaled"), 8 * tt + 8)
                        if tt:
                            turn_selection(pe, tt - 1)
                    if m == 4 and tt + 1 < TT:
                        if tt:
                            pe.wait_ge(S("sel_copied"), tt)
                        routes(tt + 1)
            turn_selection(pe, TT - 1)
            pe.wait_ge(S("sel_copied"), TT)
            pe.sem_inc(S("gates_made4"), 4)
            with pe.Fori(0, TT) as tile:
                for q in range(8):
                    multiply(pe, Job(J_U + U_GATES + q, tile, 8), act_hi, act_lo)
                    for grp in range(4):
                        gi = tile * 32 + (q * 4 + grp)
                        pe.wait_ge(S("hot_made"), gi + 1)
                        pe.wait_ge(S("gates_copied"), gi + 1)
                        for x in range(4):
                            slot = grp * 4 + x
                            last = pe.matmul(bank[4 + grp][:, x * P:(x + 1) * P], hot[:, slot, 0, :],
                                             hot[:, slot, 1, :], start=True, stop=True)
                        last.then_inc(S("gates_made4"), 1)
            with pe.Fori(0, (P - U_REST) // RING) as i:
                for m in range(RING):
                    multiply(pe, Job(J_U + U_REST + m, i), act_hi, act_lo)
            with pe.Fori(0, GROUPS // 2) as g2:
                for slot in range(2):
                    for dc in range(KC):
                        def part_split(kc):
                            if dc == 0:
                                pe.wait_ge(S("h_split"), g2 * 16 + (8 * slot + kc + 1))
                        multiply(pe, Job(J_V + GJ * slot + dc, g2, 2 * GJ), h_hi[:, slot, :, :],
                                 h_lo[:, slot, :, :], part_split)

        @block.scalar
        def _(act):
            for i in range(4):
                act.dma_start(res[:, 2 * i:2 * i + 2, :], x_t[:, 2 * i:2 * i + 2, :]).then_inc(x_landed[i], 16)
            for b in range(RING):
                act.sem_inc(taken[b], 1)
            act.sem_inc(turned_copied, 1)
            for kc in range(KC):
                act.wait_ge(x_landed[kc // 2], 16)
                act.activation(sq[:, kc, :], res[:, kc, :], ACT.Square).then_inc(sq_made, 1)
            for m in range(AHEAD):
                make_hi(act, Job(m))

            def root(n, slot, b, width):
                act.wait_ge(sums_made, n)
                act.activation(rrow[:, slot, :], bank[b][:, :], ACT.Sqrt, scale=1.0 / width, bias=k("eps"))\
                    .then_inc(roots_made, 1)
                if n > 1:
                    act.wait_ge(rrow_made, n - 1)
                act.activation(mean[:, :], bank[b][:, :], ACT.Identity, scale=-0.5 / width, bias=k("half_eps"))\
                    .then_inc(S("means_made"), 1)

            act.wait_ge(const_landed, 32)
            root(1, 0, 4, D)
            for kc in range(KC):
                act.wait_ge(normed, kc + 1)
                act.activation(act_hi[:, kc, :], hg[:, kc, :], ACT.Copy).then_inc(hi_act, 1)

            def exps(c, e):
                act.wait_ge(negmax_made, c * 2 + e + 1)
                for qt in range(TT):
                    s = slice(QOFF[qt], QOFF[qt] + QW[qt])
                    act.activation(prob[:, e, s], prob[:, e, s], ACT.Exp, bias=negmax[:, 4 * e + qt:4 * e + qt + 1],
                                   accum_out=den[:, 4 * e + qt:4 * e + qt + 1]).then_inc(probs_exp, 1)

            def copy_turned(c, e):
                act.wait_ge(probs_turned, c * 8 + 4 * e + 2)
                act.activation(probT[:, 0, 0:256], bank[4][:, 0:256], ACT.Copy).then_inc(turned_copied, 1)
                act.activation(probT[:, 1, P:2 * P], bank[4][:, 256:384], ACT.Copy).then_inc(turned_copied, 1)
                for qt in (2, 3):
                    act.wait_ge(probs_turned, c * 8 + 4 * e + qt + 1)
                    act.activation(probT[:, 0:qt + 1, qt * P:(qt + 1) * P],
                                   bank[3 + qt][:, 0:QW[qt]].rearrange("p (k q) -> p k q", q=P),
                                   ACT.Copy).then_inc(turned_copied, 1)

            with act.Fori(0, KC) as c:
                def J(m):
                    return Job(m, c, 8)
                make_hi(act, J(0).ahead())
                make_hi(act, J(1).ahead())
                result_of(act, J(0))
                act.activation(qT[:, :], bank[0][:, :], ACT.Copy).then_inc(taken[0], 1)
                make_hi(act, J(2).ahead())
                result_of(act, J(1))
                act.activation(kT[:, :], bank[1][:, :], ACT.Copy).then_inc(taken[1], 1)
                make_hi(act, J(3).ahead())
                result_of(act, J(2))
                act.activation(vT[:, :], bank[2][:, :], ACT.Copy).then_inc(taken[2], 1)
                exps(c, 0)
                make_hi(act, J(4).ahead())
                result_of(act, J(3))
                act.activation(xc[:, :], bank[3][:, :], ACT.Copy).then_inc(taken[3], 1)
                act.wait_ge(v_turned, c + 1)
                act.activation(vtok[:, :, :], bank[7][:, :].rearrange("p (t v) -> p t v", t=TT),
                               ACT.Copy).then_inc(vtok_copied, 1)
                exps(c, 1)
                make_hi(act, J(5).ahead())
                copy_turned(c, 0)
                make_hi(act, J(6).ahead())
                act.wait_ge(heads_mixed, c * 2 + 1)
                copy_turned(c, 1)
                make_hi(act, J(7).ahead())
                result_of(act, J(6))
                act.activation(sgate[:, :], bank[2][:, :], ACT.Tanh, scale=0.5).then_inc(zc_tanh, 1)
                act.wait_ge(yc_made, c + 1)
                act.activation(yc_hi[:, bass.ds(c, 1), :], conv[:, :], ACT.Copy).then_inc(ychi_made, 1)
                result_of(act, J(7))
                act.activation(sgate[:, :], bank[3][:, :], ACT.Tanh, scale=0.5).then_inc(za_tanh, 1)
                act.wait_ge(ya_made, c + 2)
                act.activation(ya_hi[:, bass.ds(c, 1), :], sgate[:, :], ACT.Copy).then_inc(yahi_made, 1)

            act.wait_ge(halfb_made, 1)
            with act.Fori(0, 4) as i:
                def J(m):
                    return Job(J_B + m, i, 8)
                for h in range(2):
                    make_hi(act, J(4 * h).ahead())
                    make_hi(act, J(4 * h + 1).ahead())
                    result_of(act, J(4 * h))
                    act.activation(tg[:, 0, :], bank[0][:, :], ACT.Tanh, scale=0.5,
                                   bias=half_b[:, bass.ds(i * 2 + h, 1)]).then_inc(taken[0], 1)
                    make_hi(act, J(4 * h + 2).ahead())
                    make_hi(act, J(4 * h + 3).ahead())
                    result_of(act, J(4 * h + 2))
                    act.activation(tg[:, 1, :], bank[2][:, :], ACT.Tanh, scale=0.5,
                                   bias=half_b[:, bass.ds(i * 2 + h + 8, 1)]).then_inc(taken[2], 1)
                    act.wait_ge(merged, i * 2 + h + 1)
                    act.activation(mg_hi[:, bass.ds(i * 2 + h, 1), :], m1[:, :], ACT.Copy,
                                   scale=0.5).then_inc(mghi_made, 1)

            for m in range(8):
                make_hi(act, Job(J_C + m).ahead())
                was_taken(act, Job(J_C + m))
                act.activation(sq[:, m, :], res[:, m, :], ACT.Square).then_inc(sq_made, 1)
                act.wait_ge(normed, KC + m + 1)
                act.activation(act_hi[:, m, :], xn[:, m % 2, :], ACT.Copy).then_inc(hi_act, 1)
                act.activation(sq2[:, m, :], hg[:, m, :], ACT.Square).then_inc(sq_made, 1)
            make_hi(act, Job(J_D).ahead())
            make_hi(act, Job(J_D + 1).ahead())
            act.wait_ge(S("means_made"), 2)
            act.activation(rrow[:, 1, :], mean[:, :], ACT.Sqrt, scale=-2.0).then_inc(roots_made, 1)
            root(3, 0, 4, D)

            def copy(dst, src, sm, scale=1.0):
                act.activation(dst, src, ACT.Copy, scale=scale).then_inc(sm, 1)

            def square(dst, src, sm):
                act.activation(dst, src, ACT.Square).then_inc(sm, 1)

            def rotary_tables():
                for j in range(2):
                    act.wait_ge(S("angles"), j + 1)
                    act.activation(rope[:, 2 * j + 1, :], angle[:, j, :], ACT.Sin).then_inc(S("rope_made"), 1)
                    act.activation(angle_abs[:, j, :], angle[:, j, :], ACT.Abs).then_inc(S("rope_made"), 1)
                for j in range(2):
                    act.wait_ge(S("rope_made"), 2 * j + 2)
                    act.activation(rope[:, 2 * j, :], angle_abs[:, j, :], ACT.Sin, scale=-1.0,
                                   bias=k("half_pi")).then_inc(S("rope_made"), 1)

            for m in range(14):
                j = Job(J_D + m)
                if m < 12:
                    make_hi(act, j.ahead(RING))
                if m == 5:
                    rotary_tables()
                if m == 8:
                    act.wait_ge(S("rope_made"), 6)
                was_taken(act, j)
                done = S("d_finished")
                if m < 2:
                    square(sqc[:, m, :], cqr[:, m, :], done)
                elif m == 2:
                    square(sqc[:, 2, :], ckvr[:, :], done)
                elif m == 3:
                    act.activation(krg[0:32, :], krg[0:32, :], ACT.Tanh, scale=0.5).then_inc(done, 1)
                elif m in (6, 7):
                    square(sqk[:, m - 6, :], ksw[:, m - 6, :], done)
                elif m >= 10:
                    square(sqq[:, m - 10, :], qh[:, m - 10, :], done)
                    act.wait_ge(done, 2 * m - 13)
                    copy(qh[:, m - 10, :], qh[:, m - 10, :], done, g("q"))
            for b in range(2):
                act.wait_ge(S("vb_turned"), b + 1)
                copy(vtb[:, b, :, :], bank[4 + b][:, :].rearrange("p (t v) -> p t v", t=TT), S("vtb_copied"))
            for m in (12, 13):
                make_hi(act, Job(J_D + m).ahead(RING))
            for kv in range(2):
                act.wait_ge(S("hidden_made"), kv + 1)
                act.activation(hid_rows[0:2 * N_CMP, kv, :], bank[kv][0:2 * N_CMP, 0:256],
                               ACT.Gelu_apprx_tanh).then_inc(S("hid_made"), 1)
            for kv in range(2):
                act.wait_ge(S("hid_turned"), kv + 1)
                copy(hid[:, 2 * kv:2 * kv + 2, :],
                     bank[kv][:, 256:384].rearrange("p (h n) -> p h n", h=2)[:, :, 0:2 * N_CMP], S("hid_copied"))
            act.wait_ge(S("kc_made"), 1)
            copy(kcr[:, :], bank[3][:, 0:N_CMP], S("kc_copied"))
            square(kc_sq[:, :], bank[3][:, 0:N_CMP], S("kc_copied"))
            copy(vcs[0:N_CMP, :], bank[3][0:N_CMP, 64:192], S("kc_copied"))
            for p in range(20):
                act.wait_ge(S("prod_made"), p + 1)
                b = bank[p % 2]
                if 2 <= p < 16:
                    act.wait_ge(S("mla_sums_made"), p - 1)
                if p < 8:
                    copy(mq[0:96, p, :], b[0:96, :], S("prod_copied"), g("mq", 0, slice(0, 96)))
                    square(sqb[0:96, p % 2, :], b[0:96, :], S("prod_taken"))
                elif p < 16:
                    copy(mk[0:64, p - 8, :], b[0:64, :], S("prod_copied"), g("mk", 0, slice(0, 64)))
                    if p < 10:
                        square(sqb[64:96, p % 2, :], krg[64:96, :], S("kr_squared"))
                    square(sqb[0:64, p % 2, :], b[0:64, :], S("prod_taken"))
                else:
                    copy(mv[:, p - 16, :], b[:, :], S("prod_taken"))
            act.wait_ge(S("roped"), 15)
            copy(mk[64:96, :, :], krg[64:96, :].unsqueeze(1).broadcast_to((32, 8, T)), S("kr_spread"))

            def pass_exp(p):
                x, s3 = PASSES[p], 4 * (p % 3)
                act.wait_ge(S("p_negmax"), p + 1)
                for qt in range(TT):
                    s = slice(QOFF[qt], QOFF[qt] + QW[qt])
                    act.activation(prob3[:, p % 3, s], prob3[:, p % 3, s], ACT.Exp,
                                   bias=negmax[:, s3 + qt:s3 + qt + 1],
                                   accum_out=den[:, s3 + qt:s3 + qt + 1]).then_inc(S("p_exp"), 1)
                if x["head"] is not None:
                    h = x["head"]
                    act.wait_ge(S("c_negmax"), h + 1)
                    c0 = 16 + 4 * (h % 2)
                    for qt in range(TT):
                        s = slice(P * (h % 2) + 32 * qt, P * (h % 2) + 32 * qt + N_CMP)
                        act.activation(cprob[:, s], cprob[:, s], ACT.Exp, bias=negmax[:, c0 + qt:c0 + qt + 1],
                                       accum_out=den[:, c0 + qt:c0 + qt + 1]).then_inc(S("c_exp"), 1)

            def pass_copy(p):
                x = PASSES[p]
                act.wait_ge(S("p_turned"), 4 * p + 2)
                copy(probT2[:, p % 2, 0, 0:256], bank[3][:, 0:256], S("p_copied"))
                copy(probT2[:, p % 2, 1, P:2 * P], bank[3][:, 256:384], S("p_copied"))
                for qt in (2, 3):
                    act.wait_ge(S("p_turned"), 4 * p + qt + 1)
                    copy(probT2[:, p % 2, 0:qt + 1, qt * P:(qt + 1) * P],
                         bank[2 + qt][:, 0:QW[qt]].rearrange("p (k q) -> p k q", q=P), S("p_copied"))
                if x["head"] is not None:
                    act.wait_ge(S("c_turned"), x["head"] + 1)
                    if x["head"]:
                        act.wait_ge(S("p_mixed"), p - 1)
                    copy(cprobT[0:N_CMP, :], bank[7][0:N_CMP, :], S("c_copied"))

            def pass_out(p):
                x = PASSES[p]
                if x["closes"]:
                    act.wait_ge(S("p_mixed"), p + 1)
                    c = x["chunk"]
                    if c == 4:
                        act.wait_ge(sums_made, 4)
                    square(sqo[:, c % 4, :], bank[6][:, :], S("o_squared"))
                    copy(o_a[:, c, :] if c < 4 else o_b[:, c - 4, :], bank[6][:, :], S("o_taken"))

            pass_exp(0)
            for p in range(len(PASSES)):
                if p + 1 < len(PASSES):
                    pass_exp(p + 1)
                if p >= 2:
                    pass_out(p - 2)
                pass_copy(p)
                if p == 19:
                    root(4, 0, 7, 512)
            for c in range(4):
                act.wait_ge(normed, 2 * KC + c + 1)
                copy(act_hi[:, c, :], o_a[:, c, :], hi_act)
            pass_out(len(PASSES) - 1)
            root(5, 1, 7, 512)
            for c in range(4, 8):
                act.wait_ge(normed, 2 * KC + c + 1)
                copy(act_hi[:, c, :], o_a[:, c, :] if c < 4 else o_b[:, c - 4, :], hi_act)
            for m in range(8):
                if m + RING < 8 + AHEAD:
                    make_hi(act, Job(J_E + m).ahead(RING))
                was_taken(act, Job(J_E + m))
                square(sq[:, m, :], res[:, m, :], sq_made)
            root(6, 0, 4, D)
            for c in range(8):
                act.wait_ge(normed, 3 * KC + c + 1)
                copy(act_hi[:, c, :], hg[:, c, :], hi_act)
            for m in range(16):
                j = Job(J_F + m)
                make_hi(act, j.ahead())
                result_of(act, j)
                copy(pq[:, m, :], bank[j.slot][:, :], S("pq_copied"))
                square(sqf[:, m, :], bank[j.slot][:, :], taken[j.slot])

            def activation_of(j, turn):
                act.wait_ge(acts_stored[(j.slot - J_U) % RING], turn * 16 + 16)
                result_of(act, j)
                act.activation(gelu[:, (j.slot - J_U) % RING, :], bank[j.slot][:, :],
                               ACT.Gelu_apprx_tanh).then_inc(taken[j.slot], 1)

            def u_job(n):
                j = Job(J_U + n)
                make_hi(act, j.ahead())
                activation_of(j, n // RING)

            def scale_routes(tt):
                act.wait_ge(S("routes_made"), tt + 1)
                if tt:
                    act.wait_ge(S("ssb_used"), tt)
                for h in range(8):
                    act.activation(ssb[:, 2 * h:2 * h + 2, :],
                                   bank[4 + h // 2][:, (h % 2) * 256:(h % 2) * 256 + 256].rearrange("p (a n) -> p a n", a=2),
                                   ACT.Copy, scale=rstd[:, tt * 8 + h:tt * 8 + h + 1]).then_inc(S("routes_scaled"), 1)

            def copy_selection(tt):
                act.wait_ge(S("sel_turned"), tt + 1)
                copy(selT[:, :, tt * P:(tt + 1) * P], bank[4][:, 0:3 * P].rearrange("p (n t) -> p n t", n=3),
                     S("sel_copied"))

            for slot in range(RING):
                act.sem_inc(acts_stored[slot], 16)
            act.wait_ge(ssq_made, 3)
            u_job(0)
            u_job(1)
            act.wait_ge(rstd_made, 5)
            scale_routes(0)
            u_job(2)
            u_job(3)
            for tt in range(TT):
                for m in range(U_TILE):
                    u_job(U_FIRST + U_TILE * tt + m)
                    if m == 3 and tt:
                        copy_selection(tt - 1)
                    if m == 7 and tt + 1 < TT:
                        scale_routes(tt + 1)
                    if m == 8:
                        act.wait_ge(S("vals_shifted"), tt + 1)
                        act.activation(sel[:, 2, :, :], sel[:, 2, :, :], ACT.Exp).then_inc(S("vals_exp"), 1)
            copy_selection(TT - 1)
            act.sem_inc(S("gates_copied"), 4)
            act.sem_inc(S("gates_stored0"), 16)
            act.sem_inc(S("gates_stored1"), 16)
            with act.Fori(0, TT) as tile:
                for q in range(8):
                    j = Job(J_U + U_GATES + q, tile, 8)
                    make_hi(act, j.ahead())
                    activation_of(j, tile * 2 + (U_GATES + q) // RING)
                    buf = q // 4
                    if q % 4 == 0:
                        act.wait_ge(S(f"gates_stored{buf}"), tile * 16 + 16)
                    for grp in range(4):
                        gi = tile * 32 + (q * 4 + grp)
                        act.wait_ge(S("gates_made4"), gi + 5)
                        t = (q % 4) * 16 + grp * 4
                        act.activation(stage[:, buf, :, t:t + 4].rearrange("p j t -> p t j"),
                                       bank[4 + grp][:, :].rearrange("p (t j) -> p t j", t=4),
                                       ACT.Copy).then_inc(S("gates_copied"), 1)
                    if q % 4 == 3:
                        act.wait_ge(S("gates_copied"), tile * 32 + (4 * q + 8))
                        act.dma_start(gates_dram[bass.ds(tile * 2 + buf, 1), :, :, :],
                                      stage[:, buf, :, :]).then_inc(S(f"gates_stored{buf}"), 16)
            with act.Fori(0, (P - U_REST) // RING) as i:
                for m in range(RING):
                    j = Job(J_U + U_REST + m, i)
                    make_hi(act, j.ahead())
                    activation_of(j, i + (U_REST + m) // RING)

            def weigh_hi(grp, slot, m):
                act.wait_ge(S("gated"), grp * GJ + (m + 1))
                act.activation(h_hi[:, slot, m, :], hf[:, slot, m, :], ACT.Copy).then_inc(S("h_hi_made"), 1)

            for m in range(GJ):
                weigh_hi(0, 0, m)

            def group(g2, slot, last=False):
                for dc in range(KC):
                    j = Job(J_V + GJ * slot + dc, g2, 2 * GJ)
                    if not (last and dc + AHEAD >= KC):
                        make_hi(act, j.ahead())
                    if not last:
                        weigh_hi(g2 * 2 + (slot + 1), 1 - slot, dc)

            with act.Fori(0, GROUPS // 2 - 1) as g2:
                group(g2, 0)
                group(g2, 1)
            group(GROUPS // 2 - 1, 0)
            group(GROUPS // 2 - 1, 1, last=True)
            for slot in range(RING):
                was_taken(act, Job(JOBS - RING + slot))
            act.dma_start(out, res[:, :, :]).then_inc(stored, 16)
            act.wait_ge(stored, 16)

        @block.vector
        def _(dve):
            dve.sem_inc(lo_made, RING)
            dve.sem_inc(scores_masked, 1)
            dve.sem_inc(ya_made, 1)
            dve.sem_inc(mg_split, 1)
            dve.wait_ge(const_landed, 32)
            dve.tensor_scalar(half_b[:, :], gain[:, GAIN["b_merge"]:GAIN["b_merge"] + 16], 0.5, None,
                              ALU.mult).then_inc(halfb_made, 1)

            def invert(n, slot):
                reciprocal_of(n, slot)
                improve(n, slot)

            def reciprocal_of(n, slot):
                dve.wait_ge(roots_made, n)
                dve.reciprocal(rrow[:, slot, :], rrow[:, slot, :]).then_inc(S("newton"), 1)

            def improve(n, slot):
                y = rrow[:, slot, :]
                dve.wait_ge(S("newton"), 3 * n - 2)
                dve.tensor_tensor(mend[:, :], y, y, ALU.mult).then_inc(S("newton"), 1)
                dve.wait_ge(S("newton"), 3 * n - 1)
                dve.wait_ge(S("means_made"), n)
                dve.tensor_tensor(mend[:, :], mend[:, :], mean[:, :], ALU.mult).then_inc(S("newton"), 1)
                dve.wait_ge(S("newton"), 3 * n)
                dve.scalar_tensor_tensor(out=y, in0=mend[:, :], scalar=1.5, in1=y, op0=ALU.add, op1=ALU.mult)\
                    .then_inc(rrow_made, 1)
                dve.wait_ge(rrow_made, n)

            def split_activations(src, gains, slot, before, first=0, stages=8):
                for kc in range(first, first + stages + 1):
                    if kc < first + stages:
                        x, to = src(kc)
                        dve.scalar_tensor_tensor(out=to, in0=x, scalar=g(gains, kc), in1=rrow[:, slot, :],
                                                 op0=ALU.mult, op1=ALU.mult).then_inc(normed, 1)
                    if kc > first:
                        make_act_lo(src(kc - 1)[1], before, kc - 1)

            def make_act_lo(x, before, kc):
                dve.wait_ge(hi_act, before + kc + 1)
                dve.tensor_tensor(act_lo[:, kc, :], x, act_hi[:, kc, :].bitcast(F32), ALU.subtract)\
                    .then_inc(lo_act, 1)

            for m in range(AHEAD):
                make_lo(dve, Job(m))
            invert(1, 0)
            split_activations(lambda kc: (res[:, kc, :], hg[:, kc, :]), "norm_g", 0, 0)

            def mask_scores(c, e):
                dve.wait_ge(bias_landed[e], (c + 1) * 16)
                dve.wait_ge(scores_made, c * 8 + 4 * e + 4)
                dve.memset(waited[:, e:e + 1], 0.0)
                for qt in range(TT):
                    b, col = QBANK[qt]
                    dve.tensor_tensor_reduce(out=prob[:, e, QOFF[qt]:QOFF[qt] + QW[qt]],
                                             in0=bank[4 + b][:, col:col + QW[qt]],
                                             in1=bias[:, e, T - QW[qt]:T], scale=SCALE_A, scalar=LOWEST,
                                             op0=ALU.add, op1=ALU.max,
                                             accum_out=mx[:, 4 * e + qt:4 * e + qt + 1]).then_inc(scores_masked, 1)
                dve.wait_ge(scores_masked, c * 8 + 4 * e + 5)
                dve.tensor_scalar(negmax[:, 4 * e:4 * e + 4], mx[:, 4 * e:4 * e + 4], -1.0, None,
                                  ALU.mult).then_inc(negmax_made, 1)

            def scale_probs(c, e):
                dve.wait_ge(probs_exp, c * 8 + 4 * e + 4)
                dve.reciprocal(inv[:, 4 * e:4 * e + 4], den[:, 4 * e:4 * e + 4]).then_inc(inv_made, 1)
                dve.wait_ge(inv_made, c * 2 + e + 1)
                for qt in range(TT):
                    s = slice(QOFF[qt], QOFF[qt] + QW[qt])
                    dve.tensor_scalar(prob[:, e, s], prob[:, e, s], inv[:, 4 * e + qt:4 * e + qt + 1], None,
                                      ALU.mult).then_inc(probs_scaled, 1)

            conv0 = GAIN["conv_w"]
            with dve.Fori(0, KC) as c:
                def J(m):
                    return Job(m, c, 8)

                def tap(j):
                    return gain[:, bass.ds(c * 3 + (conv0 + j), 1)]

                for m in range(4):
                    make_lo(dve, J(m).ahead())
                mask_scores(c, 0)
                make_lo(dve, J(4).ahead())
                mask_scores(c, 1)
                scale_probs(c, 0)
                make_lo(dve, J(5).ahead())
                was_taken(dve, J(3))
                result_of(dve, J(4))
                dve.tensor_tensor(prod[:, 2:T + 2], bank[0][:, :], xc[:, :], ALU.mult).then_inc(taken[0], 1)
                scale_probs(c, 1)
                was_taken(dve, J(4))
                dve.tensor_scalar(conv[:, :], prod[:, 2:T + 2], tap(2), None, ALU.mult).then_inc(conv_step, 1)
                dve.wait_ge(conv_step, c * 3 + 1)
                dve.scalar_tensor_tensor(out=conv[:, :], in0=prod[:, 1:T + 1], scalar=tap(1), in1=conv[:, :],
                                         op0=ALU.mult, op1=ALU.add).then_inc(conv_step, 1)
                dve.wait_ge(conv_step, c * 3 + 2)
                dve.scalar_tensor_tensor(out=conv[:, :], in0=prod[:, 0:T], scalar=tap(0), in1=conv[:, :],
                                         op0=ALU.mult, op1=ALU.add).then_inc(conv_step, 1)
                make_lo(dve, J(6).ahead())
                dve.wait_ge(conv_step, c * 3 + 3)
                result_of(dve, J(5))
                dve.tensor_tensor(conv[:, :], conv[:, :], bank[1][:, :], ALU.mult).then_inc(taken[1], 1)
                make_lo(dve, J(7).ahead())
                dve.wait_ge(zc_tanh, c + 1)
                dve.scalar_tensor_tensor(out=sgate[:, :], in0=sgate[:, :], scalar=1.0, in1=bank[2][:, :],
                                         op0=ALU.add, op1=ALU.mult).then_inc(taken[2], 1)
                was_taken(dve, J(5))
                was_taken(dve, J(6))
                dve.scalar_tensor_tensor(out=conv[:, :], in0=sgate[:, :], scalar=0.5, in1=conv[:, :],
                                         op0=ALU.mult, op1=ALU.mult).then_inc(yc_made, 1)
                dve.wait_ge(ychi_made, c + 1)
                dve.tensor_tensor(yc_lo[:, bass.ds(c, 1), :], conv[:, :],
                                  yc_hi[:, bass.ds(c, 1), :].bitcast(F32), ALU.subtract).then_inc(y_split, 1)
                dve.wait_ge(za_tanh, c + 1)
                dve.scalar_tensor_tensor(out=sgate[:, :], in0=sgate[:, :], scalar=1.0, in1=bank[3][:, :],
                                         op0=ALU.add, op1=ALU.mult).then_inc(taken[3], 1)
                was_taken(dve, J(7))
                dve.wait_ge(heads_mixed, c * 2 + 2)
                dve.scalar_tensor_tensor(out=sgate[:, :], in0=sgate[:, :], scalar=0.5, in1=bank[7][:, :],
                                         op0=ALU.mult, op1=ALU.mult).then_inc(ya_made, 1)
                dve.wait_ge(yahi_made, c + 1)
                dve.tensor_tensor(ya_lo[:, bass.ds(c, 1), :], sgate[:, :],
                                  ya_hi[:, bass.ds(c, 1), :].bitcast(F32), ALU.subtract).then_inc(y_split, 1)

            with dve.Fori(0, 4) as i:
                def J(m):
                    return Job(J_B + m, i, 8)
                for h in range(2):
                    chunk = bass.ds(i * 2 + h, 1)
                    make_lo(dve, J(4 * h).ahead())
                    make_lo(dve, J(4 * h + 1).ahead())
                    was_taken(dve, J(4 * h))
                    result_of(dve, J(4 * h + 1))
                    dve.wait_ge(mg_split, i * 2 + h + 1)
                    dve.scalar_tensor_tensor(out=m1[:, :], in0=tg[:, 0, :], scalar=1.0, in1=bank[1][:, :],
                                             op0=ALU.add, op1=ALU.mult).then_inc(taken[1], 1)
                    make_lo(dve, J(4 * h + 2).ahead())
                    make_lo(dve, J(4 * h + 3).ahead())
                    was_taken(dve, J(4 * h + 2))
                    result_of(dve, J(4 * h + 3))
                    dve.scalar_tensor_tensor(out=tg[:, 1, :], in0=tg[:, 1, :], scalar=1.0, in1=bank[3][:, :],
                                             op0=ALU.add, op1=ALU.mult).then_inc(taken[3], 1)
                    was_taken(dve, J(4 * h + 3))
                    dve.tensor_tensor(m1[:, :], m1[:, :], tg[:, 1, :], ALU.add).then_inc(merged, 1)
                    dve.wait_ge(mghi_made, i * 2 + h + 1)
                    dve.scalar_tensor_tensor(out=mg_lo[:, chunk, :], in0=m1[:, :], scalar=0.5,
                                             in1=mg_hi[:, chunk, :].bitcast(F32), op0=ALU.mult,
                                             op1=ALU.subtract).then_inc(mg_split, 1)

            for m in range(8):
                make_lo(dve, Job(J_C + m).ahead())
                j = Job(J_C + m)
                result_of(dve, j)
                dve.tensor_tensor(res[:, m, :], res[:, m, :], bank[j.slot][:, :], ALU.add).then_inc(taken[j.slot], 1)
                was_taken(dve, j)
                dve.tensor_scalar(hg[:, m, :], res[:, m, :], g("final_g", m), None, ALU.mult).then_inc(hg_made, 1)
                dve.wait_ge(hg_made, m + 1)
                dve.tensor_scalar(xn[:, m % 2, :], hg[:, m, :], g("norm1", m), None, ALU.mult).then_inc(normed, 1)
                if m:
                    make_act_lo(xn[:, (m - 1) % 2, :], KC, m - 1)
            make_act_lo(xn[:, 1, :], KC, 7)
            make_lo(dve, Job(J_D).ahead())
            dve.wait_ge(sums_made, 3)
            dve.tensor_scalar(rrow[:, 1, :], bank[4][:, :], -0.5 * EPS / D, -0.5 * EPS * EPS, ALU.mult, ALU.add)\
                .then_inc(S("h1_mean"), 1)
            dve.wait_ge(S("h1_mean"), 1)
            dve.scalar_tensor_tensor(out=mean[:, :], in0=bank[5][:, :], scalar=-0.5 / D, in1=rrow[:, 1, :],
                                     op0=ALU.mult, op1=ALU.add).then_inc(S("means_made"), 1)
            invert(2, 1)
            make_lo(dve, Job(J_D + 1).ahead())
            invert(3, 0)
            make_lo(dve, Job(J_D).ahead(RING))
            for kc in range(KC):
                dve.tensor_tensor(res[:, kc, :], hg[:, kc, :], rrow[:, 0, :], ALU.mult).then_inc(S("h1_made"), 1)

            MAGIC = 1.5 * 2.0 ** 23
            TWO_PI = (6.28125, 0.0019350051879882812, 3.0198386e-07)
            v = S("angle_step")

            def angles(j):
                fr = k("freq")
                n = 1 + 6 * j
                if j == 0:
                    dve.wait_ge(S("pos_landed"), 16)
                    dve.tensor_copy(pos_f[:, :], pos_i[:, :]).then_inc(v, 1)
                dve.wait_ge(v, n)
                dve.tensor_scalar(angle[:, j, :], pos_f[:, :], fr[:, j:j + 1], None, ALU.mult).then_inc(v, 1)
                n += 1
                dve.wait_ge(v, n)
                dve.tensor_scalar(turns[:, :], angle[:, j, :], 1 / (2 * np.pi), MAGIC, ALU.mult, ALU.add).then_inc(v, 1)
                n += 1
                dve.wait_ge(v, n)
                dve.tensor_scalar(turns[:, :], turns[:, :], -MAGIC, None, ALU.add).then_inc(v, 1)
                n += 1
                for part in TWO_PI:
                    dve.wait_ge(v, n)
                    dve.scalar_tensor_tensor(out=angle[:, j, :], in0=turns[:, :], scalar=-part,
                                             in1=angle[:, j, :], op0=ALU.mult, op1=ALU.add).then_inc(v, 1)
                    n += 1
                dve.wait_ge(v, n)
                dve.tensor_scalar(angle[:, j, :], angle[:, j, :], 3.1415925, -3.1415925,
                                  ALU.min, ALU.max).then_inc(S("angles"), 1)

            d_places = [cqr[:, 0, :], cqr[:, 1, :], ckvr[:, :], krg[:, :], None, None, ksw[:, 0, :], ksw[:, 1, :],
                        vsw[:, 0, :], vsw[:, 1, :]] + [qh[:, c, :] for c in range(4)]

            def divide(m):
                j = Job(J_D + m)
                result_of(dve, j)
                if d_places[m] is None:
                    dve.tensor_tensor(kvc[0:64, 0, m - 4, :], bank[j.slot][0:64, :], rrow[0:64, 1, :], ALU.mult)\
                        .then_inc(S("d_part"), 1)
                    dve.tensor_tensor(kvc[64:P, 1, m - 4, :], bank[j.slot][64:P, :], rrow[64:P, 1, :], ALU.mult)\
                        .then_inc(taken[j.slot], 1)
                else:
                    dve.tensor_tensor(d_places[m], bank[j.slot][:, :], rrow[:, 1, :], ALU.mult).then_inc(taken[j.slot], 1)

            dve.wait_ge(S("h1_made"), KC)
            divide(0)
            for m in range(1, 14):
                if m < 12:
                    make_lo(dve, Job(J_D + m).ahead(RING))
                if m in (2, 4):
                    angles(m // 2 - 1)
                if m in (8, 9):
                    dve.wait_ge(S("rope_made"), 6)
                divide(m)
                if m == 7:
                    dve.wait_ge(S("rope_made"), 6)
                    dve.wait_ge(S("shifted"), 32)
                    for kv in range(2):
                        for grp in range(2):
                            src = kvc[:, kv, grp, :]
                            src = bass.AP(tensor=src.tensor, offset=src.offset,
                                          ap=[list(src.ap[0]), [2, CMP_LEN // 2], [CMP_STRIDE, N_CMP]])
                            at0 = GAIN["pos"] + kv * CMP_LEN // 2
                            pos = gain[:, at0:at0 + CMP_LEN // 2].unsqueeze(2).broadcast_to((P, CMP_LEN // 2, N_CMP))
                            dve.tensor_tensor(kp[:, kv, :, grp * N_CMP:(grp + 1) * N_CMP], src, pos, ALU.add)\
                                .then_inc(S("kp_made"), 1)
            dve.wait_ge(S("gates_turned"), 1)
            dve.tensor_scalar(gate[:, :], bank[6][:, 0:TT * 24], 0.5, 0.5, ALU.mult, ALU.add).then_inc(S("gates_made"), 1)
            for m in (12, 13):
                make_lo(dve, Job(J_D + m).ahead(RING))
            dve.wait_ge(ssq_made, 1)

            def by_tile(t, a, b):
                return t.rearrange("p (t n) -> p t n", t=TT)[:, :, a:b]

            for a, b, width in ((0, 12, 64), (12, 13, 256), (13, 14, 128)):
                dve.tensor_scalar(by_tile(ms[:, 0:64], a, b), by_tile(bank[7][:, 0:64], a, b), 1.0 / width, EPS,
                                  ALU.mult, ALU.add).then_inc(ms_made, 1)
            dve.wait_ge(rstd_made, 1)
            dve.tensor_scalar(by_tile(rq_a[:, :], 0, 8), by_tile(rstd[:, 0:64], 0, 8), SCALE_A, None,
                              ALU.mult).then_inc(S("rq_made"), 1)

            def diag_unit(u, col, per=16):
                if u >= 2:
                    dve.wait_ge(row_made, u - 1 + (u > 6))
                for tt in range(TT):
                    dve.tensor_scalar(diag[:, 4 * (u % 2) + tt, :], ident, rstd[:, tt * per + col:tt * per + col + 1],
                                      None, ALU.mult).then_inc(diag_made, 1)

            diag_unit(0, 12)
            diag_unit(1, 13)
            dve.wait_ge(row_made, 1)
            for c in range(2):
                dve.scalar_tensor_tensor(out=cqr[:, c, :], in0=cqr[:, c, :], scalar=g("cq", c), in1=bank[6][:, :],
                                         op0=ALU.mult, op1=ALU.mult).then_inc(S("latents"), 1)
            diag_unit(2, 8)
            dve.wait_ge(row_made, 2)
            dve.scalar_tensor_tensor(out=ckvr[:, :], in0=ckvr[:, :], scalar=g("ckv"), in1=bank[2][:, :],
                                     op0=ALU.mult, op1=ALU.mult).then_inc(S("latents"), 1)
            diag_unit(3, 9)

            def apply_rope(r_, x, rows=slice(0, P), table=0):
                dve.wait_ge(S("rot_made"), r_ + 1)
                if r_ >= 2:
                    dve.wait_ge(S("roped"), r_ - 1)
                tmp = rtmp[rows, r_ % 2, :]
                dve.tensor_tensor(tmp, bank[4 + r_ % 2][rows, :], rope[rows, 2 * table + 1, :], ALU.mult)\
                    .then_inc(S("rot_used"), 1)
                dve.tensor_tensor(x, x, rope[rows, 2 * table, :], ALU.mult).then_inc(S("rope_half"), 1)
                dve.wait_ge(S("rope_half"), r_ + 1)
                dve.tensor_tensor(x, x, tmp, ALU.add).then_inc(S("roped"), 1)

            diag_unit(4, 10)
            diag_unit(5, 11)
            for c in range(2):
                apply_rope(c, qh[:, c, :])
            dve.wait_ge(row_made, 4)
            dve.scalar_tensor_tensor(out=ksw[:, 0, :], in0=ksw[:, 0, :], scalar=g("ks"), in1=bank[6][:, :],
                                     op0=ALU.mult, op1=ALU.mult).then_inc(S("kw_normed"), 1)
            dve.wait_ge(row_made, 6)
            dve.scalar_tensor_tensor(out=ksw[:, 1, :], in0=ksw[:, 1, :], scalar=g("kw"), in1=bank[2][:, :],
                                     op0=ALU.mult, op1=ALU.mult).then_inc(S("kw_normed"), 1)
            for c in range(2, 4):
                apply_rope(c, qh[:, c, :])
            dve.wait_ge(ssq_made, 2)
            dve.tensor_scalar(ms[0:N_CMP, 0:2], bank[7][0:N_CMP, 96:98], 1.0 / 64, EPS, ALU.mult, ALU.add)\
                .then_inc(ms_made, 1)
            dve.wait_ge(rstd_made, 2)
            for grp in range(2):
                dve.tensor_scalar(diag[0:N_CMP, grp, 0:N_CMP], k("ident", slice(0, N_CMP), slice(0, N_CMP)),
                                  rstd[0:N_CMP, grp:grp + 1], None, ALU.mult).then_inc(diag_made, 1)
            dve.wait_ge(row_made, 7)
            dve.scalar_tensor_tensor(out=kcr[:, :], in0=kcr[:, :], scalar=g("kc"), in1=bank[3][:, 256:256 + N_CMP],
                                     op0=ALU.mult, op1=ALU.mult).then_inc(S("kc_normed"), 1)
            apply_rope(4, ksw[:, 0, :])
            apply_rope(5, ksw[:, 1, :])

            def at_ends(j):
                t = rope[:, j, :]
                return bass.AP(tensor=t.tensor, offset=t.offset + CMP_LEN - 1,
                               ap=[list(t.ap[0]), [CMP_STRIDE, N_CMP]])
            dve.wait_ge(S("kc_rot"), 1)
            dve.tensor_tensor(kc_tmp[:, :], bank[3][:, 320:320 + N_CMP], at_ends(1), ALU.mult).then_inc(S("kc_step"), 1)
            dve.tensor_tensor(kcr[:, :], kcr[:, :], at_ends(0), ALU.mult).then_inc(S("kc_step"), 1)
            dve.wait_ge(S("kc_step"), 2)
            dve.tensor_tensor(kcr[:, :], kcr[:, :], kc_tmp[:, :], ALU.add).then_inc(S("kc_roped"), 1)

            r96 = slice(64, 96)
            for h in range(8):
                if h == 7:
                    dve.wait_ge(S("mla_sums_made"), 8)
                    dve.tensor_scalar(by_tile(ms[:, 0:64], 0, 8), by_tile(bank[6][:, 128:192], 0, 8), 1.0 / 96, EPS,
                                      ALU.mult, ALU.add).then_inc(ms_made, 1)
                dve.wait_ge(S("prod_taken"), h + 1)
                apply_rope(6 + h, mq[r96, h, :], r96, 1)
            dve.wait_ge(S("kr_squared"), 2)
            dve.tensor_scalar(krg[r96, :], krg[r96, :], g("mk", 0, r96), None, ALU.mult).then_inc(S("kr_scaled"), 1)
            dve.wait_ge(S("kr_scaled"), 1)
            apply_rope(14, krg[r96, :], r96, 1)
            dve.wait_ge(S("mla_sums_made"), 16)
            dve.tensor_scalar(by_tile(ms[:, 0:64], 8, 16), by_tile(bank[7][:, 128:192], 8, 16), 1.0 / 96, EPS,
                              ALU.mult, ALU.add).then_inc(ms_made, 1)
            causal, cmask = k("causal"), k("cmp_mask")

            def pass_mask(p):
                x, s3 = PASSES[p], 4 * (p % 3)
                for qt in range(TT):
                    b, col = QBANK[qt]
                    dve.wait_ge(S("p_scores"), 4 * p + max(qt + 1, 2))
                    if qt == 0 and x["head"] is not None:
                        dve.wait_ge(S("c_scores"), x["head"] + 1)
                    dve.tensor_tensor_reduce(out=prob3[:, p % 3, QOFF[qt]:QOFF[qt] + QW[qt]],
                                             in0=bank[b][:, col:col + QW[qt]], in1=causal[:, T - QW[qt]:T],
                                             scale=rq_col(x, qt), scalar=LOWEST, op0=ALU.add, op1=ALU.max,
                                             accum_out=mx[:, s3 + qt:s3 + qt + 1]).then_inc(S("p_masked"), 1)
                if x["head"] is not None:
                    h = x["head"]
                    c0 = 16 + 4 * (h % 2)
                    for qt in range(TT):
                        dve.tensor_tensor_reduce(out=cprob[:, P * (h % 2) + 32 * qt:P * (h % 2) + 32 * qt + N_CMP],
                                                 in0=bank[0][:, 384 + 32 * qt:384 + 32 * qt + N_CMP],
                                                 in1=cmask[:, N_CMP * qt:N_CMP * (qt + 1)], scale=rq_col(x, qt),
                                                 scalar=LOWEST, op0=ALU.add, op1=ALU.max,
                                                 accum_out=mx[:, c0 + qt:c0 + qt + 1]).then_inc(S("c_masked"), 1)
                dve.wait_ge(S("p_masked"), 4 * p + 4)
                dve.tensor_scalar(negmax[:, s3:s3 + 4], mx[:, s3:s3 + 4], -1.0, None, ALU.mult).then_inc(S("p_negmax"), 1)
                if x["head"] is not None:
                    dve.wait_ge(S("c_masked"), 4 * h + 4)
                    dve.tensor_scalar(negmax[:, c0:c0 + 4], mx[:, c0:c0 + 4], -1.0, None, ALU.mult)\
                        .then_inc(S("c_negmax"), 1)

            dve.wait_ge(S("rq_made"), 1)
            pass_mask(0)
            dve.wait_ge(rstd_made, 4)
            dve.tensor_scalar(by_tile(rq_b[:, :], 0, 8), by_tile(rstd[:, 0:64], 0, 8), SCALE_B, None,
                              ALU.mult).then_inc(S("rq_made"), 1)
            dve.wait_ge(S("kr_spread"), 1)
            for h in range(9):
                if h < 8:
                    diag_unit(6 + h, 8 + h)
                if h:
                    dve.wait_ge(row_made, 7 + h)
                    dve.tensor_tensor(mk[0:96, h - 1, :], mk[0:96, h - 1, :], bank[4 + (h - 1) % 2][0:96, :], ALU.mult)\
                        .then_inc(S("mk_normed"), 1)
            dve.wait_ge(S("rq_made"), 2)

            def gates_of(h, branch):
                return gate[:, :].rearrange("p (t n) -> p t n", t=TT)[:, :, 3 * h + branch:3 * h + branch + 1]\
                    .rearrange("p t n -> p (t n)")

            def pass_scale(p):
                x, s3 = PASSES[p], 4 * (p % 3)
                dve.wait_ge(S("p_exp"), 4 * p + 4)
                dve.reciprocal(inv[:, s3:s3 + 4], den[:, s3:s3 + 4]).then_inc(S("p_inv"), 1)
                by = inv
                if x["gate"]:
                    dve.wait_ge(S("p_inv"), p + 1)
                    dve.tensor_tensor(factor[:, s3:s3 + 4], inv[:, s3:s3 + 4], gates_of(*x["gate"]), ALU.mult)\
                        .then_inc(S("p_factor"), 1)
                    dve.wait_ge(S("p_factor"), p + 1)
                    by = factor
                else:
                    dve.wait_ge(S("p_inv"), p + 1)
                for qt in range(TT):
                    s = slice(QOFF[qt], QOFF[qt] + QW[qt])
                    dve.tensor_scalar(prob3[:, p % 3, s], prob3[:, p % 3, s], by[:, s3 + qt:s3 + qt + 1], None,
                                      ALU.mult).then_inc(S("p_scaled"), 1)
                if x["head"] is not None:
                    h = x["head"]
                    c0 = 16 + 4 * (h % 2)
                    dve.wait_ge(S("c_exp"), 4 * h + 4)
                    dve.reciprocal(inv[:, c0:c0 + 4], den[:, c0:c0 + 4]).then_inc(S("c_step"), 1)
                    dve.wait_ge(S("c_step"), 3 * h + 1)
                    dve.tensor_tensor(factor[:, c0:c0 + 4], inv[:, c0:c0 + 4], gates_of(x["gate"][0], 0), ALU.mult)\
                        .then_inc(S("c_step"), 1)
                    dve.wait_ge(S("c_step"), 3 * h + 2)
                    dve.tensor_tensor(factor[:, c0:c0 + 1], factor[:, c0:c0 + 1], k("valid"), ALU.mult)\
                        .then_inc(S("c_step"), 1)
                    dve.wait_ge(S("c_step"), 3 * h + 3)
                    for qt in range(TT):
                        s = slice(P * (h % 2) + 32 * qt, P * (h % 2) + 32 * qt + N_CMP)
                        dve.tensor_scalar(cprob[:, s], cprob[:, s], factor[:, c0 + qt:c0 + qt + 1], None, ALU.mult)\
                            .then_inc(S("c_scaled"), 1)

            pass_mask(1)
            for p in range(len(PASSES)):
                pass_scale(p)
                if p + 2 < len(PASSES):
                    pass_mask(p + 2)
                if p == 20:
                    reciprocal_of(4, 0)
                if p == 21:
                    improve(4, 0)
                if p >= 22:
                    for c in (2 * p - 44, 2 * p - 43):
                        dve.scalar_tensor_tensor(out=o_a[:, c, :], in0=o_a[:, c, :], scalar=g("out", c),
                                                 in1=rrow[:, 0, :], op0=ALU.mult, op1=ALU.mult).then_inc(normed, 1)
            for c in range(4):
                make_act_lo(o_a[:, c, :], 2 * KC, c)
            invert(5, 1)
            split_activations(lambda kc: (o_b[:, kc - 4, :], o_b[:, kc - 4, :]), "out", 1, 2 * KC, 4, 4)
            for m in range(8):
                j = Job(J_E + m)
                result_of(dve, j)
                dve.tensor_tensor(res[:, m, :], res[:, m, :], bank[j.slot][:, :], ALU.add).then_inc(taken[j.slot], 1)
                if m + RING < 8 + AHEAD:
                    make_lo(dve, j.ahead(RING))
            def add_halves(h):
                was_taken(dve, Job(J_F + 2 * h + 1))
                was_taken(dve, Job(J_F + 2 * h))
                dve.tensor_tensor(sqf[:, 2 * h, :], sqf[:, 2 * h, :], sqf[:, 2 * h + 1, :], ALU.add)\
                    .then_inc(S("halves_added"), 1)

            invert(6, 0)
            split_activations(lambda kc: (res[:, kc, :], hg[:, kc, :]), "norm2", 0, 3 * KC)
            for m in range(16):
                make_lo(dve, Job(J_F + m).ahead())
                if m % 2 and m > 2:
                    add_halves((m - 3) // 2)

            def u_job(n):
                make_lo(dve, Job(J_U + n).ahead())

            add_halves(7)
            u_job(0)
            dve.wait_ge(ssq_made, 3)
            dve.tensor_scalar(ms[:, 0:32], bank[7][:, 0:32], 1.0 / 256, EPS, ALU.mult, ALU.add).then_inc(ms_made, 1)

            q = [0]
            step = S("route_step")

            def then(ins):
                q[0] += 1
                ins.then_inc(step, 1)
                dve.wait_ge(step, q[0])

            def mark(ins):
                q[0] += 1
                ins.then_inc(step, 1)

            iota = k("iota")
            for n in range(1, U_FIRST):
                u_job(n)
            for tt in range(TT):
                def beside(m):
                    u_job(U_FIRST + U_TILE * tt + m)

                for hc in range(16):
                    if hc % 2 == 0:
                        dve.wait_ge(S("routes_scaled"), 8 * tt + hc // 2 + 1)
                    mark(dve.max(v16[:, hc, 0:8], ssb[:, hc, :]))
                beside(0)
                dve.wait_ge(step, q[0])
                for hc in range(16):
                    mark(dve.match_replace(srep[:, hc, :], v16[:, hc, 0:8], ssb[:, hc, :], LOWEST))
                    mark(dve.max_index(i16[:, hc, 0:8], v16[:, hc, 0:8], ssb[:, hc, :]))
                    if hc == 7:
                        beside(1)
                beside(2)
                dve.wait_ge(step, q[0])
                for hc in range(16):
                    mark(dve.max(v16[:, hc, 8:16], srep[:, hc, :]))
                beside(3)
                dve.wait_ge(step, q[0])
                for hc in range(16):
                    ins = dve.max_index(i16[:, hc, 8:16], v16[:, hc, 8:16], srep[:, hc, :])
                    if hc < 15:
                        mark(ins)
                ins.then_inc(S("ssb_used"), 1)
                beside(4)
                dve.wait_ge(S("ssb_used"), tt + 1)
                mark(dve.tensor_copy(i16f[:, :, :], i16[:, :, :]))
                vv = v16[:, :, :].rearrange("p (h a) k -> p h a k", a=2)
                then(dve.tensor_tensor(cand[:, :, :, :], vv[:, :, 0, :].unsqueeze(3).broadcast_to((P, 8, 16, 16)),
                                       vv[:, :, 1, :].unsqueeze(2).broadcast_to((P, 8, 16, 16)), ALU.add))

                def flat(t, h):
                    return t[:, h, :, :].rearrange("p a b -> p (a b)")
                for h in range(8):
                    mark(dve.max(vals[:, h, 0:8], flat(cand, h)))
                dve.wait_ge(step, q[0])
                beside(5)
                for h in range(8):
                    mark(dve.match_replace(flat(crep, h), vals[:, h, 0:8], flat(cand, h), LOWEST))
                    mark(dve.max_index(vci[:, h, 0:8], vals[:, h, 0:8], flat(cand, h)))
                dve.wait_ge(step, q[0])
                for h in range(8):
                    mark(dve.max(vals[:, h, 8:16], flat(crep, h)))
                beside(6)
                dve.wait_ge(step, q[0])
                if tt:
                    dve.wait_ge(S("sel_turned"), tt)
                dve.tensor_tensor(sel[:, 2, :, :], vals[:, :, :], vals[:, :, 0:1].broadcast_to((P, 8, 16)), ALU.subtract)\
                    .then_inc(S("vals_shifted"), 1)
                for h in range(8):
                    mark(dve.max_index(vci[:, h, 8:16], vals[:, h, 8:16], flat(crep, h)))
                dve.wait_ge(step, q[0])
                mark(dve.tensor_scalar(ca[:, 0, :, :], vci[:, :, :], 4, None, ALU.logical_shift_right))
                then(dve.tensor_scalar(ca[:, 1, :, :], vci[:, :, :], 15, None, ALU.bitwise_and))
                then(dve.tensor_copy(caf[:, :, :, :], ca[:, :, :, :]))
                beside(7)
                for half in range(2):
                    then(dve.tensor_tensor(eq[:, :, :, :].rearrange("p h k a -> p (h k) a"),
                                           iota[:, 0:16].unsqueeze(1).broadcast_to((P, P, 16)),
                                           caf[:, half, :, :].rearrange("p h k -> p (h k)").unsqueeze(2).broadcast_to((P, P, 16)),
                                           ALU.is_equal))
                    ii = i16f[:, :, :].rearrange("p (h a) k -> p h a k", a=2)[:, :, half, :]
                    then(dve.tensor_tensor(eq[:, :, :, :], eq[:, :, :, :],
                                           ii.unsqueeze(2).broadcast_to((P, 8, 16, 16)), ALU.mult))
                    then(dve.tensor_reduce(sel[:, half, :, :].rearrange("p h k -> p (h k)"),
                                           eq[:, :, :, :].rearrange("p h k a -> p (h k) a"), AX, ALU.add))
                    beside(8 + half)
                dve.wait_ge(S("vals_exp"), tt + 1)
                then(dve.tensor_reduce(vsum[:, 0, :], sel[:, 2, :, :], AX, ALU.add))
                then(dve.reciprocal(vsum[:, 1, :], vsum[:, 0, :]))
                dve.tensor_tensor(sel[:, 2, :, :], sel[:, 2, :, :], vsum[:, 1, :].unsqueeze(2).broadcast_to((P, 8, 16)),
                                  ALU.mult).then_inc(S("selected"), 1)
                beside(10)

            dve.wait_ge(S("sel_copied"), TT)
            with dve.Fori(0, TT) as tile:
                for q in range(8):
                    for grp in range(4):
                        if grp == 2:
                            make_lo(dve, Job(J_U + U_GATES + q, tile, 8).ahead())
                        dve.wait_ge(S("gates_made4"), tile * 32 + (q * 4 + grp + 1))
                        for x in range(4):
                            t = tile * P + (q * 16 + grp * 4 + x)
                            slot = grp * 4 + x
                            dve.tensor_scalar(hot[:, slot, 0, :], iota, selT[:, 0, bass.ds(t, 1)], None, ALU.is_equal)
                            ins = dve.tensor_scalar(hot[:, slot, 1, :], iota, selT[:, 1, bass.ds(t, 1)],
                                                    selT[:, 2, bass.ds(t, 1)], ALU.is_equal, ALU.mult)
                        ins.then_inc(S("hot_made"), 1)
            with dve.Fori(0, (P - U_REST) // RING) as i:
                for m in range(RING):
                    make_lo(dve, Job(J_U + U_REST + m, i).ahead())

            def weigh(grp, slot, m):
                dve.tensor_tensor(hf[:, slot, m, :].rearrange("p (b t) -> p b t", t=64),
                                  hf[:, slot, m, :].rearrange("p (b t) -> p b t", t=64),
                                  wg[:, slot, :, m, :], ALU.mult).then_inc(S("gated"), 1)

            def weigh_lo(grp, slot, m):
                dve.wait_ge(S("h_hi_made"), grp * GJ + (m + 1))
                dve.tensor_tensor(h_lo[:, slot, m, :], hf[:, slot, m, :], h_hi[:, slot, m, :].bitcast(F32),
                                  ALU.subtract).then_inc(S("h_split"), 1)

            def group_landed(lap, slot):
                dve.wait_ge(S(f"wg_landed{slot}"), lap * 16 + 16)
                dve.wait_ge(S(f"hf_landed{slot}"), lap * 16 + 16)

            group_landed(0, 0)
            for m in range(GJ):
                weigh(0, 0, m)
            for m in range(GJ):
                weigh_lo(0, 0, m)

            def group(g2, slot, last=False):
                if not last:
                    group_landed(g2 + slot, 1 - slot)
                for dc in range(KC):
                    j = Job(J_V + GJ * slot + dc, g2, 2 * GJ)
                    if not (last and dc + AHEAD >= KC):
                        make_lo(dve, j.ahead())
                    if not last:
                        weigh(g2 * 2 + (slot + 1), 1 - slot, dc)
                        if dc:
                            weigh_lo(g2 * 2 + (slot + 1), 1 - slot, dc - 1)
                    result_of(dve, j)
                    dve.tensor_tensor(res[:, dc, :], res[:, dc, :], bank[j.slot][:, :], ALU.add)\
                        .then_inc(taken[j.slot], 1)
                if not last:
                    weigh_lo(g2 * 2 + (slot + 1), 1 - slot, KC - 1)

            with dve.Fori(0, GROUPS // 2 - 1) as g2:
                group(g2, 0)
                group(g2, 1)
            group(GROUPS // 2 - 1, 0)
            group(GROUPS // 2 - 1, 1, last=True)


def _weights(a):
    n = a.shape[1] // P
    return a.reshape(KC, P, n, P).transpose(2, 1, 0, 3).reshape(n, P, KC * P)


def lay_out(i):
    f = {k: np.asarray(v) for k, v in i.items()}
    w_in = _weights(f["w_in"][0])
    part = {n: w_in[8 * j:8 * j + 8] for j, n in enumerate("xc bg cg zc q k v za gc ga".split())}
    woc, woa, wo = (_weights(f[n][0]) for n in ("w_out_conv", "w_out_attn", "w_o"))
    a = np.stack([part[n] for n in "q k v xc cg bg zc za".split()], 1).reshape(64, P, D)
    b = np.stack([part["gc"], woc, part["ga"], woa], 1).reshape(32, P, D)

    w2 = f["w_in_2"][0]
    cut = np.cumsum([0, 512, 128, 128, 128, 128, 128, 128, 24, 256, 128, 32])
    q, kc, vc, ks, vs, kw, vw, gt, cq, ckv, kr = (w2[:, cut[j]:cut[j + 1]] for j in range(11))
    order = [h for c in range(4) for h in (c, c + 4)]
    qh = q.reshape(D, 8, 64)[:, order].reshape(D, 512)
    krg = np.zeros((D, P), w2.dtype)
    krg[:, 0:24] = gt
    krg[:, 64:96] = kr
    d = np.concatenate([cq, ckv, krg, kc[:, :64], vc[:, :64], kc[:, 64:], vc[:, 64:], ks, kw, vs, vw, qh], 1)
    wo2 = f["w_out_2"][0]
    wo2 = np.concatenate([wo2[:512].reshape(8, 64, D)[order].reshape(512, D), wo2[512:]], 0)
    u = f["peer_u_2"][0].reshape(P, GROUPS, GJ, KC, P).transpose(1, 2, 4, 3, 0).reshape(GROUPS, GJ, P, D)
    v = f["peer_v_2"][0].reshape(P, GROUPS, GJ, KC, P).transpose(1, 3, 0, 2, 4).reshape(GROUPS, KC, P, D)
    u, v = u.reshape(P, P, D), v.reshape(GROUPS * KC, P, D)
    tiles = np.concatenate([a, b, wo, _weights(d), _weights(wo2), _weights(f["peer_w_q_2"][0]), u, v], 0)

    def chunks(v):
        return v.reshape(-1, P).T

    gains = np.zeros((P, N_GAIN), np.float32)

    def put(name, v):
        gains[:v.shape[0], GAIN[name]:GAIN[name] + v.shape[1]] = v

    put("norm_g", chunks(f["norm_g"][0]))
    put("final_g", chunks(f["final_g"]))
    put("b_merge", chunks(f["b_merge"][0]))
    put("conv_w", f["conv_w"][0].reshape(3, 8, P).transpose(2, 1, 0).reshape(P, 24))
    put("norm1", chunks(f["norm1_gain_2"][0]))
    for n, s in (("q", "nsa_q_gain_2"), ("kc", "nsa_kc_gain_2"), ("ks", "nsa_ks_gain_2"), ("kw", "nsa_kw_gain_2")):
        put(n, np.concatenate([f[s][0], f[s][0]])[:, None])
    put("cq", chunks(f["mla_q_lora_gain_2"][0]))
    put("ckv", chunks(f["mla_kv_lora_gain_2"][0]))
    put("mq", f["mla_q_gain_2"][0][:, None])
    put("mk", f["mla_k_gain_2"][0][:, None])
    ga = f["out_gain_a_2"][0].reshape(8, 64)[order].reshape(512)
    put("out", chunks(np.concatenate([ga, f["out_gain_b_2"][0]])))
    put("norm2", chunks(f["norm2_gain_2"][0]))
    pos = f["cmp_pos_2"][0].T
    even, odd = pos[:, 0::2], pos[:, 1::2]
    put("pos", np.concatenate([np.concatenate([even, odd], 1), np.concatenate([odd, even], 1)], 0))

    def w1(a, first):
        a = a.reshape(CMP_LEN // 2, 2, 64, 256)[:, [first, 1 - first]]
        return a.transpose(1, 2, 0, 3).reshape(P, CMP_LEN // 2, 256)

    cmp_w1 = np.stack([w1(f["cmp_k_w1_2"][0], 0), w1(f["cmp_v_w1_2"][0], 1)], 1)
    cmp_w2 = np.stack([f["cmp_k_w2_2"][0].reshape(2, P, 64), f["cmp_v_w2_2"][0].reshape(2, P, 64)], 0)
    ukv = f["mla_w_ukv_2"][0].reshape(P, 8, 2, 64).transpose(0, 2, 1, 3)
    return dict(
        tiles=tiles, x_t=f["x"][0].T.reshape(KC, P, T).transpose(1, 0, 2), consts=CONSTS, gains=gains,
        alibi=_alibi(), positions=f["positions_2"],
        cmp_w1=cmp_w1, cmp_w2=cmp_w2.transpose(2, 0, 1, 3),
        w_uq=f["mla_w_uq_2"][0].reshape(2, P, 768).transpose(1, 0, 2), w_ukv=ukv,
        sub_keys=f["peer_sub_keys_2"][0].transpose(3, 0, 1, 2).reshape(P, 16, P),
    )


def kernel(**inputs):
    import concourse.bacc as bacc
    from concourse.bass_utils import run_bass_kernel_spmd

    nc = bacc.Bacc("TRN2", target_bir_lowering=False, num_devices=1)
    arrays = {n: np.ascontiguousarray(a) for n, a in lay_out(inputs).items()}
    args = [nc.dram_tensor(n, a.shape, mybir.dt.from_np(a.dtype), kind="ExternalInput").ap()
            for n, a in arrays.items()]
    gates = nc.dram_tensor("gates_dram", (TT * 2, P, P, 64), F32, kind="Internal").ap()
    acts = nc.dram_tensor("acts_dram", (P, P, T), F32, kind="Internal").ap()
    out = nc.dram_tensor("out_t", (P, KC, T), F32, kind="ExternalOutput").ap()
    two_layer_kernel(nc, *args, gates, acts, out)
    r = run_bass_kernel_spmd(nc, [arrays], core_ids=[0])
    out = r.results[0]["out_t"]
    return np.ascontiguousarray(out.transpose(2, 1, 0).reshape(1, T, D))
```
